# Optimizing a Trainium2 kernel written in Bass

```python
import jax
import jax.numpy as jnp
from jax import lax
import numpy as np

D_MODEL = 1024
BATCH = 1
SEQ = 512
DEPTH = 2

CTX_LEN = 256
GRID_W = 64
D_MIX = D_MODEL
D_CONV = D_MIX // 2
CONV_WIDTH = 31
H_MLSTM = 4
D_MLSTM = D_MIX - D_CONV
HD_MLSTM = D_MLSTM // H_MLSTM
MLSTM_CHUNK = 64
N_GATES = 4
EVEN_IN = 2 * D_CONV + 4 * D_MLSTM + N_GATES * H_MLSTM
D_POOL = D_MIX // 4
POOL_WINDOWS = (2, 4, 8, 16)
POOL_GROUP = D_POOL // len(POOL_WINDOWS)
HEAD_DIM = 128
N_Q_HEADS = (D_MIX - D_POOL) // HEAD_DIM
N_KV_HEADS = 2
Q_PER_KV = N_Q_HEADS // N_KV_HEADS
D_Q = N_Q_HEADS * HEAD_DIM
D_KV = N_KV_HEADS * HEAD_DIM
ODD_IN = D_POOL + D_Q + 2 * D_KV
Q_BLOCK = 128
ROPE_THETA = 10000.0
D_FF = 256 * ((8 * D_MODEL // 3 + 255) // 256)
FFN_CONV_WIDTH = 3
N_EVEN = (DEPTH + 1) // 2
N_ODD = DEPTH // 2
EPS = 1e-6
ADA_STD = 0.5

kernel_name = 'hybrid_conv_mlstm_pool_gqa_dit_block'

def rms_norm(x, g):
    xf = x.astype(jnp.float32)
    y = xf * lax.rsqrt(jnp.mean(xf * xf, axis=-1, keepdims=True) + EPS)
    return (y * g.astype(jnp.float32)).astype(x.dtype)

def layer_norm(x, g, b):
    xf = x.astype(jnp.float32)
    mu = jnp.mean(xf, axis=-1, keepdims=True)
    var = jnp.mean(jnp.square(xf - mu), axis=-1, keepdims=True)
    y = (xf - mu) * lax.rsqrt(var + EPS) * g.astype(jnp.float32) + b.astype(jnp.float32)
    return y.astype(x.dtype)

def modulate(h, shift, scale):
    return h * (1 + scale) + shift

def dwconv(x, w):
    return lax.conv_general_dilated(x, w[:, None, :].astype(x.dtype), window_strides=(1,), padding='SAME',
                                    dimension_numbers=('NWC', 'WIO', 'NWC'), feature_group_count=x.shape[-1])

def axial_rope_angles(n_tokens):
    rows = n_tokens // GRID_W
    row = jnp.repeat(jnp.arange(rows), GRID_W).astype(jnp.float32)
    col = jnp.tile(jnp.arange(GRID_W), rows).astype(jnp.float32)
    n_freq = HEAD_DIM // 4
    inv = ROPE_THETA ** (-jnp.arange(n_freq, dtype=jnp.float32) / n_freq)
    ang = jnp.concatenate([row[:, None] * inv, col[:, None] * inv], axis=-1)
    return jnp.cos(ang), jnp.sin(ang)

def apply_rope(x, cos, sin):
    xf = x.astype(jnp.float32).reshape(*x.shape[:-1], HEAD_DIM // 2, 2)
    xe, xo = xf[..., 0], xf[..., 1]
    cs, sn = cos[:, None, :], sin[:, None, :]
    out = jnp.stack([xe * cs - xo * sn, xe * sn + xo * cs], axis=-1).reshape(x.shape)
    return out.astype(x.dtype)

def conv_module(glu_in, dw_w, ln_g, ln_b):
    a, b = jnp.split(glu_in, 2, axis=-1)
    u = a * jax.nn.sigmoid(b)
    u = dwconv(u, dw_w)
    u = layer_norm(u, ln_g, ln_b)
    return jax.nn.silu(u)

def mlstm_chunkwise(q, k, v, i_pre, log_f, state):
    B_, H_, T, d = q.shape
    nc = T // MLSTM_CHUNK

    def chunks(a):
        return jnp.moveaxis(a.reshape(B_, H_, nc, MLSTM_CHUNK, *a.shape[3:]), 2, 0)

    lower = jnp.tril(jnp.ones((MLSTM_CHUNK, MLSTM_CHUNK), dtype=bool))

    def step(carry, inp):
        C, n, m = carry
        qj, kj, vj, ij, fj = inp
        b = jnp.cumsum(fj, axis=-1)
        dmat = jnp.where(lower, b[..., :, None] - b[..., None, :] + ij[..., None, :], -jnp.inf)
        m_inter = b + m[..., None]
        m_t = jnp.maximum(m_inter, jnp.max(dmat, axis=-1))
        w_inter = jnp.exp(m_inter - m_t)
        s = jnp.einsum('bhld,bhsd->bhls', qj, kj) * jnp.exp(dmat - m_t[..., None])
        num = w_inter[..., None] * jnp.einsum('bhld,bhde->bhle', qj, C) + jnp.einsum('bhls,bhse->bhle', s, vj)
        den = w_inter * jnp.einsum('bhld,bhd->bhl', qj, n) + jnp.sum(s, axis=-1)
        h = num / jnp.maximum(jnp.abs(den), jnp.exp(-m_t))[..., None]
        b_last = b[..., -1]
        src = b_last[..., None] - b + ij
        m_new = jnp.maximum(b_last + m, jnp.max(src, axis=-1))
        a = jnp.exp(b_last + m - m_new)
        e = jnp.exp(src - m_new[..., None])
        C_new = a[..., None, None] * C + jnp.einsum('bhs,bhsd,bhse->bhde', e, kj, vj)
        n_new = a[..., None] * n + jnp.einsum('bhs,bhsd->bhd', e, kj)
        return (C_new, n_new, m_new), h

    state, hs = lax.scan(step, state, (chunks(q), chunks(k), chunks(v), chunks(i_pre), chunks(log_f)))
    return jnp.moveaxis(hs, 0, 2).reshape(B_, H_, T, d), state

def mlstm_inputs(p, gate_b):
    B_, T = p.shape[:2]
    off = 2 * D_CONV

    def heads(a):
        return a.reshape(B_, T, H_MLSTM, HD_MLSTM).transpose(0, 2, 1, 3).astype(jnp.float32)

    q = heads(p[..., off:off + D_MLSTM])
    k = heads(p[..., off + D_MLSTM:off + 2 * D_MLSTM]) * (HD_MLSTM ** -0.5)
    v = heads(p[..., off + 2 * D_MLSTM:off + 3 * D_MLSTM])
    o = p[..., off + 3 * D_MLSTM:off + 4 * D_MLSTM]
    g = p[..., off + 4 * D_MLSTM:].astype(jnp.float32).reshape(B_, T, N_GATES, H_MLSTM) + gate_b.astype(jnp.float32)
    g = g.transpose(2, 0, 3, 1)
    return q, k, v, o, g

def bidir_mlstm(qc, kc, vc, gc, q, k, v, g):
    B_ = q.shape[0]
    zero = (jnp.zeros((B_, H_MLSTM, HD_MLSTM, HD_MLSTM), jnp.float32),
            jnp.zeros((B_, H_MLSTM, HD_MLSTM), jnp.float32),
            jnp.zeros((B_, H_MLSTM), jnp.float32))
    rev = lambda a: jnp.flip(a, axis=2)
    lsig = jax.nn.log_sigmoid
    hc_f, st_f = mlstm_chunkwise(qc, kc, vc, gc[0], lsig(gc[1]), zero)
    hc_b, st_b = mlstm_chunkwise(rev(qc), rev(kc), rev(vc), rev(gc[2]), rev(lsig(gc[3])), zero)
    h_f, _ = mlstm_chunkwise(q, k, v, g[0], lsig(g[1]), st_f)
    h_b, _ = mlstm_chunkwise(rev(q), rev(k), rev(v), rev(g[2]), rev(lsig(g[3])), st_b)
    return h_f + rev(h_b), hc_f + rev(hc_b)

def mlstm_merge(h, o, norm_g):
    B_, _, T, _ = h.shape
    hn = rms_norm(h.transpose(0, 2, 1, 3), norm_g.reshape(H_MLSTM, HD_MLSTM))
    return hn.reshape(B_, T, D_MLSTM).astype(o.dtype) * jax.nn.sigmoid(o)

def even_mixer(h, hc, w_in, w_out, dw_w, ln_g, ln_b, gate_b, norm_g, need_ctx):
    p = h @ w_in
    pc = hc @ w_in
    q, k, v, o, g = mlstm_inputs(p, gate_b)
    qc, kc, vc, oc, gc = mlstm_inputs(pc, gate_b)
    h_m, hc_m = bidir_mlstm(qc, kc, vc, gc, q, k, v, g)
    y = jnp.concatenate([conv_module(p[..., :2 * D_CONV], dw_w, ln_g, ln_b),
                         mlstm_merge(h_m, o, norm_g).astype(h.dtype)], axis=-1) @ w_out
    yc = None
    if need_ctx:
        yc = jnp.concatenate([conv_module(pc[..., :2 * D_CONV], dw_w, ln_g, ln_b),
                              mlstm_merge(hc_m, oc, norm_g).astype(hc.dtype)], axis=-1) @ w_out
    return y, yc

def multiscale_pool(u, pool_w, pool_scale):
    B_, T, _ = u.shape
    uf = u.astype(jnp.float32)
    csum = jnp.concatenate([jnp.zeros_like(uf[:, :1]), jnp.cumsum(uf, axis=1)], axis=1)
    t = jnp.arange(T)
    outs = []
    for gi, w in enumerate(POOL_WINDOWS):
        lo = jnp.clip(t - w // 2, 0, T)
        hi = jnp.clip(t + w // 2, 0, T)
        sl = slice(gi * POOL_GROUP, (gi + 1) * POOL_GROUP)
        cs = csum[..., sl]
        mean = (cs[:, hi] - cs[:, lo]) / (hi - lo).astype(jnp.float32)[:, None]
        outs.append(mean - uf[..., sl])
    dpool = jnp.stack(outs, axis=2)
    y = jnp.einsum('btgc,gce->btge', dpool, pool_w.astype(jnp.float32)).reshape(B_, T, D_POOL)
    return (y * pool_scale.astype(jnp.float32)).astype(u.dtype)

def latent_attention(q, k, v, kc, vc):
    B_, Hk, G, T, d = q.shape
    k_all = jnp.concatenate([kc, k], axis=2)
    v_all = jnp.concatenate([vc, v], axis=2)
    nb = T // Q_BLOCK
    qb = jnp.moveaxis(q.reshape(B_, Hk, G, nb, Q_BLOCK, d), 3, 0)
    scale = HEAD_DIM ** -0.5

    def block(qblk):
        s = jnp.einsum('bhgqd,bhkd->bhgqk', qblk, k_all).astype(jnp.float32) * scale
        pr = jax.nn.softmax(s, axis=-1).astype(v_all.dtype)
        return jnp.einsum('bhgqk,bhkd->bhgqd', pr, v_all)

    o = lax.map(block, qb)
    return jnp.moveaxis(o, 0, 3).reshape(B_, Hk, G, T, d)

def context_attention(q, k, v):
    s = jnp.einsum('bhgqd,bhkd->bhgqk', q, k).astype(jnp.float32) * (HEAD_DIM ** -0.5)
    return jnp.einsum('bhgqk,bhkd->bhgqd', jax.nn.softmax(s, axis=-1).astype(v.dtype), v)

def attn_inputs(p, q_g, k_g):
    B_, T = p.shape[:2]
    q = p[..., D_POOL:D_POOL + D_Q].reshape(B_, T, N_Q_HEADS, HEAD_DIM)
    k = p[..., D_POOL + D_Q:D_POOL + D_Q + D_KV].reshape(B_, T, N_KV_HEADS, HEAD_DIM)
    v = p[..., D_POOL + D_Q + D_KV:].reshape(B_, T, N_KV_HEADS, HEAD_DIM)
    return rms_norm(q, q_g), rms_norm(k, k_g), v

def to_groups(q):
    B_, T = q.shape[:2]
    return q.reshape(B_, T, N_KV_HEADS, Q_PER_KV, HEAD_DIM).transpose(0, 2, 3, 1, 4)

def from_groups(o):
    B_, _, _, T, _ = o.shape
    return o.transpose(0, 3, 1, 2, 4).reshape(B_, T, D_Q)

def odd_mixer(h, hc, w_in, w_out, pool_w, pool_scale, q_g, k_g, cos, sin, need_ctx):
    p = h @ w_in
    pc = hc @ w_in
    q, k, v = attn_inputs(p, q_g, k_g)
    qc, kc, vc = attn_inputs(pc, q_g, k_g)
    q = apply_rope(q, cos, sin)
    k = apply_rope(k, cos, sin)
    kv = lambda a: a.transpose(0, 2, 1, 3)
    attn = from_groups(latent_attention(to_groups(q), kv(k), kv(v), kv(kc), kv(vc)))
    y = jnp.concatenate([multiscale_pool(p[..., :D_POOL], pool_w, pool_scale), attn], axis=-1) @ w_out
    yc = None
    if need_ctx:
        attn_c = from_groups(context_attention(to_groups(qc), kv(kc), kv(vc)))
        yc = jnp.concatenate([multiscale_pool(pc[..., :D_POOL], pool_w, pool_scale), attn_c], axis=-1) @ w_out
    return y, yc

def conv_ffn(h, w_in, conv_w, w_out):
    g, v = jnp.split(h @ w_in, 2, axis=-1)
    g = dwconv(g, conv_w)
    return (jax.nn.silu(g) * v) @ w_out

def setup_inputs(seed: int = 0) -> dict:
    key = jax.random.key(seed)
    ks = iter(jax.random.split(key, 40))
    f32 = jnp.float32

    def nrm(shape, std):
        return jax.random.normal(next(ks), shape, f32) * std

    def gain(shape):
        return 1.0 + 0.05 * jax.random.normal(next(ks), shape, f32)

    f_bias = jnp.linspace(3.0, 6.0, H_MLSTM, dtype=f32)
    gate_b = jnp.stack([nrm((N_EVEN, H_MLSTM), 0.1),
                        f_bias + nrm((N_EVEN, H_MLSTM), 0.1),
                        nrm((N_EVEN, H_MLSTM), 0.1),
                        f_bias + nrm((N_EVEN, H_MLSTM), 0.1)], axis=1)
    return {
        'x': nrm((BATCH, SEQ, D_MODEL), 1.0),
        'c': nrm((BATCH, D_MODEL), 1.0),
        'ctx': nrm((BATCH, CTX_LEN, D_MODEL), 1.0),
        'c_ctx': nrm((D_MODEL,), 1.0),
        'ada_w': nrm((DEPTH, D_MODEL, 6 * D_MODEL), ADA_STD * D_MODEL ** -0.5),
        'ada_b': nrm((DEPTH, 6 * D_MODEL), 0.02),
        'mix_pre_g': gain((DEPTH, D_MODEL)),
        'mix_post_g': gain((DEPTH, D_MODEL)),
        'ffn_pre_g': gain((DEPTH, D_MODEL)),
        'ffn_post_g': gain((DEPTH, D_MODEL)),
        'ffn_w_in': nrm((DEPTH, D_MODEL, 2 * D_FF), D_MODEL ** -0.5),
        'ffn_conv_w': nrm((DEPTH, FFN_CONV_WIDTH, D_FF), FFN_CONV_WIDTH ** -0.5),
        'ffn_w_out': nrm((DEPTH, D_FF, D_MODEL), D_FF ** -0.5),
        'even_w_in': nrm((N_EVEN, D_MODEL, EVEN_IN), D_MODEL ** -0.5),
        'even_w_out': nrm((N_EVEN, D_MIX, D_MODEL), D_MIX ** -0.5),
        'conv_dw_w': nrm((N_EVEN, CONV_WIDTH, D_CONV), CONV_WIDTH ** -0.5),
        'conv_ln_g': gain((N_EVEN, D_CONV)),
        'conv_ln_b': nrm((N_EVEN, D_CONV), 0.02),
        'mlstm_gate_b': gate_b,
        'mlstm_norm_g': gain((N_EVEN, D_MLSTM)),
        'odd_w_in': nrm((N_ODD, D_MODEL, ODD_IN), D_MODEL ** -0.5),
        'odd_w_out': nrm((N_ODD, D_MIX, D_MODEL), D_MIX ** -0.5),
        'pool_w': nrm((N_ODD, len(POOL_WINDOWS), POOL_GROUP, POOL_GROUP), POOL_GROUP ** -0.5),
        'pool_scale': gain((N_ODD, D_POOL)),
        'q_norm_g': gain((N_ODD, HEAD_DIM)),
        'k_norm_g': gain((N_ODD, HEAD_DIM)),
    }

def reference(x, c, ctx, c_ctx, ada_w, ada_b, mix_pre_g, mix_post_g, ffn_pre_g, ffn_post_g,
              ffn_w_in, ffn_conv_w, ffn_w_out, even_w_in, even_w_out, conv_dw_w, conv_ln_g, conv_ln_b,
              mlstm_gate_b, mlstm_norm_g, odd_w_in, odd_w_out, pool_w, pool_scale, q_norm_g, k_norm_g):
    cos, sin = axial_rope_angles(x.shape[1])
    silu_c = jax.nn.silu(c)
    silu_cc = jax.nn.silu(c_ctx)
    xc = ctx
    for l in range(DEPTH):
        need_ctx = l < DEPTH - 1
        mod = jnp.split((silu_c @ ada_w[l] + ada_b[l])[:, None, :], 6, axis=-1)
        mod_c = jnp.split(silu_cc @ ada_w[l] + ada_b[l], 6, axis=-1)
        h = modulate(rms_norm(x, mix_pre_g[l]), mod[0], mod[1])
        hc = modulate(rms_norm(xc, mix_pre_g[l]), mod_c[0], mod_c[1])
        if l % 2 == 0:
            e = l // 2
            y, yc = even_mixer(h, hc, even_w_in[e], even_w_out[e], conv_dw_w[e], conv_ln_g[e], conv_ln_b[e],
                               mlstm_gate_b[e], mlstm_norm_g[e], need_ctx)
        else:
            o = l // 2
            y, yc = odd_mixer(h, hc, odd_w_in[o], odd_w_out[o], pool_w[o], pool_scale[o],
                              q_norm_g[o], k_norm_g[o], cos, sin, need_ctx)
        x = x + mod[2] * rms_norm(y, mix_post_g[l])
        h = modulate(rms_norm(x, ffn_pre_g[l]), mod[3], mod[4])
        x = x + mod[5] * rms_norm(conv_ffn(h, ffn_w_in[l], ffn_conv_w[l], ffn_w_out[l]), ffn_post_g[l])
        if need_ctx:
            xc = xc + mod_c[2] * rms_norm(yc, mix_post_g[l])
            hc = modulate(rms_norm(xc, ffn_pre_g[l]), mod_c[3], mod_c[4])
            xc = xc + mod_c[5] * rms_norm(conv_ffn(hc, ffn_w_in[l], ffn_conv_w[l], ffn_w_out[l]), ffn_post_g[l])
    return x


_drawn_inputs = setup_inputs


def setup_inputs(seed=0):
    import zlib

    import numpy as np

    out = dict(_drawn_inputs(seed))
    spreads = {}
    factors = {'mix_post_g': 2.693,
     'ffn_post_g': 2.882,
     'conv_ln_g': 4.236,
     'conv_ln_b': 8.0,
     'mlstm_norm_g': 5.318,
     'pool_scale': 4.829,
     'q_norm_g': 8.0,
     'k_norm_g': 8.0}
    for name, (base, spread) in spreads.items():
        noise = np.random.default_rng([zlib.crc32(name.encode()), seed]).standard_normal(out[name].shape)
        drawn = base * np.exp(spread * noise) if base else spread * noise
        out[name] = jnp.asarray(drawn.astype(out[name].dtype))
    for name, factor in factors.items():
        out[name] = (out[name] * factor).astype(out[name].dtype)
    return out
```

```python
from contextlib import ExitStack

import numpy as np

import concourse.bass as bass
from concourse import mybir

F32 = mybir.dt.float32
F32R = mybir.dt.float32r
ALU = mybir.AluOpType
ACT = mybir.ActivationFunctionType
AX = mybir.AxisListType

P = 128
D = 1024
KD = D // P
LAT = 512
CTX = 256
T = LAT + CTX
NT = T // P
NL = LAT // P
EPS = 1e-6
D_FF = 2816
FT = D_FF // P
TAPS = 31
HEADS = 4
HD = 128
GATE_COL = 3072
VW = HD + 1
N_VECTORS = 21
N_Q, N_KV = 6, 2
D_POOL = 256
WINDOWS = (2, 4, 8, 16)
FFN_GROUPS = (8, 8, 6)
SEGS = {T: ((0, LAT), (LAT, T)), LAT: ((0, LAT),)}
HALF = TAPS // 2
U_LAT, U_CTX = HALF, 2 * HALF + LAT
U_LEN = 3 * HALF + T + 1
G_LAT, G_CTX = 1, LAT + 2
G_LEN = T + 4
CONV_LEN = {T: T + 1, LAT: LAT}


class Steps:

    def __init__(self, eng, sem):
        self.eng, self.sem, self.count, self.reg, self.per, self.first = eng, sem, 0, None, 0, 0

    def done(self, ins):
        self.count += 1
        ins.then_inc(self.sem, 1)
        return self.value()

    def value(self):
        return self.count if self.reg is None else self.reg * self.per + self.count

    def wait(self, value=None):
        self.eng.wait_ge(self.sem, self.value() if value is None else value)

    def loop(self, reg, per):
        self.reg, self.per, self.first = reg, per, self.count

    def end(self, trips):
        assert self.count - self.first == self.per, (self.count - self.first, self.per)
        self.count = self.first + self.per * trips
        self.reg = None


def plan():
    order = [("vec", 1, 0), ("xt", 4, 0), ("ada", 1, 0), ("n0", 2, 0), ("conv", 4, 2), ("gate", 1, 2), ("qkov", 8, 2),
             ("gcol", 1, 0), ("vt", 3, 0), ("ln", 4, 0), ("mlstm", 2, 0), ("out0", 4, 2)]
    for l in range(2):
        if l:
            order += [("n3", 2, 0), ("in1", 4, 2), ("kin", 1, 2), ("vin", 1, 2), ("qst", 1, 0), ("rot", 4, 0),
                      ("kb", 1, 0), ("pool", 1, 0), ("att", 2, 0), ("out1", 4, 2)]
        order += [(f"n{1 + 3 * l}", 2, 0), (f"m{1 + 3 * l}", 2, 0)]
        for g, size in enumerate(FFN_GROUPS):
            order += [(f"up{l}{g}", size, 2), (f"down{l}{g}", 4, 2)]
        order += [(f"n{2 + 3 * l}", 2, 0)]
    order += [("outT", 4, 0)]
    unit, granule, u, n = {}, {}, 0, 0
    for name, units, granules in order:
        unit[name], granule[name] = u, n
        u += units
        n += units * granules
    return unit, granule, n


ORDER = (4, 5, 0, 1, 2, 3)


def mlstm_steps():
    steps, e = [], 0
    for s in ORDER:
        if s < NL:
            of_tile = [(0, s * P, LAT), (1, 0, (s + 1) * P)]
        else:
            of_tile = [(0, 0, LAT), (0, s * P, T), (1, 0, LAT), (1, LAT, (s + 1) * P)]
        steps.append([(e + n, x) for n, x in enumerate(of_tile)])
        e += len(of_tile)
    return steps


STEPS = mlstm_steps()
TOUCHES = [[(q, d, t) for q in range(NT) for _, (d, t0, t1) in STEPS[q] for t in range(t0 // P, t1 // P)
            if (6 * d + t) // 3 == b] for b in range(4)]
FIRST_TOUCH = [x[0] for x in TOUCHES]
LAST_TOUCH = [x[-1] for x in TOUCHES]
ITEMS = [("X", h - 1, 0) if q == "X" else ("S", h, q) for h in range(HEADS) for q in (0, 1, 2, "X", 3, 4, 5)
         if q != "X" or h] + [("X", HEADS - 1, 0)]


def build(nc, a, out):
    U, G, N_GRANULES = plan()
    ctx = ExitStack()
    with ctx:
        used = {}

        def sem(name):
            if name not in used:
                used[name] = ctx.enter_context(nc.semaphore(name))
            return used[name]

        base = (nc.sbuf_base + 31) // 32 * 32
        top = nc.sbuf_usable_end
        at = [base]

        def place(name, shape, dt=F32, offset=None):
            size = int(np.prod(shape[1:])) * 4
            if offset is None:
                offset = at[0]
                at[0] += (size + 31) // 32 * 32
                assert at[0] <= top, (name, at[0] - top)
            assert offset + size <= top, name
            return nc.alloc_sbuf_tensor_at(name, shape, dt, offset=offset)

        xT = place("xT", [P, KD, T])
        H0 = at[0]
        h_hi = place("h_hi", [P, KD, T], F32R)
        h_lo = place("h_lo", [P, KD, T], F32R)
        raw = place("raw", [P, 2, 4, 256])
        w_hi = place("w_hi", [P, 4, 4, 256], F32R)
        w_lo = place("w_lo", [P, 4, 4, 256], F32R)
        ident = place("ident", [P, P])
        ones = place("ones", [P, P])
        vec0 = place("vec0", [P, 108])
        vec1 = place("vec1", [P, 84])
        ffn_cw = place("ffn_cw", [P, 2, 66])
        dw_w = place("dw_w", [P, TAPS, 4])
        mods = place("mods", [P, 2, 6, KD, 2])
        cond = place("cond", [P, KD, 2])
        st = place("st", [P, 2, NT])
        gate_b = place("gate_b", [P, 2])
        mark = place("mark", [P, 16])
        ADA = at[0]
        ada_w = place("ada_w", [P, 2, KD, P])
        A0 = at[0]
        ARENA = top // 32 * 32 - A0
        assert ARENA >= 86080, ARENA

        qkov = place("qkov", [P, 16, T], offset=A0)
        negM = place("negM", [P, 2, 2, T], offset=A0 + 8 * T * 4)
        sig_b = place("sig_b", [P, 4, T], offset=A0 + 8 * T * 4)
        v_tok = place("v_tok", [P, NT, HEADS, VW], offset=A0 + 49152)
        EP0 = A0 + 49152 + 12384
        probs = place("probs", [P, 4, LAT], offset=EP0)
        rows = place("rows", [P, 6, T], offset=A0 + 49152)
        ln_sq = place("ln_sq", [P, 2, T], offset=EP0)
        U0 = EP0 + 8192
        conv_u = place("conv_u", [P, 5, U_LEN], offset=U0)
        ln_diag = place("ln_diag", [P, T], offset=U0 + 4 * U_LEN * 4)
        h_tok = place("h_tok", [P, NT, P], offset=U0)
        merged = place("merged", [P, T], offset=U0 + 3072)
        sq_junk = place("sq_junk", [P, NT, P], offset=U0 + 6144)
        gcols = place("gcols", [P, 4, NT, 8], offset=ADA)
        den = place("den", [P, 2, 4, 3], offset=ADA + 1024)
        hss = place("hss", [P, 2, NT], offset=ADA + 1280)
        hid_hi = place("hid_hi", [P, 8, T], F32R, offset=A0)
        hid_lo = place("hid_lo", [P, 8, T], F32R, offset=A0 + 24576)
        tbuf = place("tbuf", [P, 2, T], offset=A0)
        y = place("y", [P, KD, T], offset=A0 + 49152)
        SCR = A0 + 73728
        gpad = place("gpad", [P, 2, G_LEN], offset=SCR)
        cbuf = place("cbuf", [P, 2, G_LEN], offset=SCR + 2 * G_LEN * 4)
        sq = place("sq", [P, 2, T], offset=SCR)
        sumsq = place("sumsq", [P, T], offset=SCR + 6144)
        diag = place("diag", [P, T], offset=SCR + 9216)
        x_tok = place("x_tok", [P, NT, D], offset=H0)
        ada_0 = place("ada_0", [P, 8, KD, 2 * P], offset=A0)
        vrows = place("vrows", [P, 5, P], offset=A0 + 65536)
        inb = place("inb", [P, 8, LAT], offset=A0)
        kT = place("kT", [P, N_KV, T], offset=A0 + 16384)
        v1 = place("v1", [P, NT, N_KV * HD], offset=A0 + 22528)
        rope = place("rope", [P, 2, LAT], offset=A0 + 28672)
        rotw = place("rotw", [P, 3, P], offset=A0 + 32768)
        icnt = place("icnt", [P, 2, LAT], offset=A0 + 34304)
        poolw = place("poolw", [P, 2, P], offset=A0 + 38400)
        PW = LAT + 16
        pu = place("pu", [P, 2, PW], offset=A0 + 39424)
        ps2 = place("ps2", [P, 2, PW], offset=A0 + 43648)
        ps4 = place("ps4", [P, 2, PW], offset=A0 + 47872)
        asq = place("asq", [P, 2, T], offset=A0 + 52096)
        adiag = place("adiag", [P, 2, T], offset=A0 + 58240)
        rt1 = place("rt1", [P, 2, LAT], offset=A0 + 64384)
        ptile = place("ptile", [P, 2, T], offset=A0 + 68480)
        pT = place("pT", [P, 2, T], offset=A0 + 74624)
        acol = place("acol", [P, 36], offset=ADA)
        arow = place("arow", [P, 24, 4], offset=ADA + 256)
        o_tok = place("o_tok", [P, NL, D], offset=A0)

        acc = ctx.enter_context(nc.psum_tensor("acc", [P, 2, 2, 2 * 512], F32))
        m_dram = nc.dram_tensor("m_rows", (2, HEADS, T), F32, kind="Internal").ap()

        raw_full = [sem("raw_full0"), sem("raw_full1")]
        high, low = sem("w_high"), sem("w_low")
        unit_done = sem("unit_done")
        set_free = [sem("set0_free"), sem("set1_free")]
        ada_full = [sem("ada_full0"), sem("ada_full1")]
        ada_out = sem("ada_out")
        h_ready, sq_ready, sq_used = sem("h_ready"), sem("sq_ready"), sem("sq_used")
        recip, root, diag_ready = sem("recip"), sem("root"), sem("diag_ready")
        x_new, t_ready, t_high = sem("x_new"), sem("t_ready"), sem("t_high")

        def psum_free(eng, u, i=0):
            eng.wait_ge(set_free[u % 2], u // 2 + 1 + i)

        def psum_full(eng, u, i=0):
            eng.wait_ge(unit_done, u + 1 + 2 * i)

        def psum_read(eng, u, i=0):
            eng.wait_ge(set_free[u % 2], u // 2 + 2 + i)

        def loaded(n, i=0):
            return 16 * (n // 2 + 1) + 32 * i

        w_even = a["even_w_in"][0].rearrange("(k p) n -> p k n", p=P)
        w_even_out = a["even_w_out"][0].rearrange("(k p) n -> p k n", p=P)
        w_odd = a["odd_w_in"][0].rearrange("(k p) n -> p k n", p=P)
        w_odd_out = a["odd_w_out"][0].rearrange("(k p) n -> p k n", p=P)
        w_ffn_in = [a["ffn_w_in"][l].rearrange("(k p) n -> p k n", p=P) for l in range(2)]
        w_ffn_out = [a["ffn_w_out"][l].rearrange("(k p) n -> p k n", p=P) for l in range(2)]
        w_ada = [a["ada_w"][l].rearrange("(k p) n -> p k n", p=P) for l in range(2)]
        SPLIT = {8: (4, 4), 6: (4, 2)}

        block = ctx.enter_context(nc.Block())

        def load(sp, n, src, i=0):
            sp.wait_ge(low, n + 3 + 4 * i)
            kt = src.shape[1]
            sp.dma_start(raw[:, n % 2, 0:kt, :], src).then_inc(raw_full[n % 2], 16)

        def load_unit(sp, n, w, col, k0=0, ktiles=KD, i=0):
            for part, kt in enumerate(SPLIT[ktiles]):
                k = k0 + 4 * part
                load(sp, n + part, w[:, k:k + kt, bass.ds(col, 256)], i)

        def load_ada(sp, u, r, l, tile, i=0):
            sp.wait_ge(unit_done, u + 2 * i)
            sp.dma_start(ada_w[:, r % 2], w_ada[l][:, :, bass.ds(tile * P, P)]).then_inc(ada_full[r % 2], 16)

        @block.sync
        def _(sp):
            sp.dma_start(ident[:, :], a["identity"]).then_inc(sem("ident_in"), 16)
            tile_rows = [0] * 5

            def vector_rows(block_, src):
                r = tile_rows[block_]
                n = src.shape[0]
                sp.dma_start(vrows[r:r + n, block_, :], src).then_inc(sem("vec_in"), 16)
                tile_rows[block_] = r + n

            gains = ("mix_pre_g", "mix_post_g", "ffn_pre_g", "ffn_post_g")
            for l in range(2):
                vector_rows(l, a["ada_b"][l].rearrange("(r p) -> r p", p=P))
                for g in gains:
                    vector_rows(l, a[g][l].rearrange("(r p) -> r p", p=P))
            vector_rows(0, a["c"][0].rearrange("(r p) -> r p", p=P))
            vector_rows(0, a["c_ctx"].rearrange("(r p) -> r p", p=P))
            for g in ("conv_ln_g", "conv_ln_b", "mlstm_norm_g"):
                vector_rows(0, a[g][0].rearrange("(r p) -> r p", p=P))
            for g in ("pool_scale", "q_norm_g", "k_norm_g"):
                vector_rows(1, a[g][0].rearrange("(r p) -> r p", p=P))
            for l in range(2):
                vector_rows(2 + l, a["ffn_conv_w"][l].rearrange("w (j p) -> (w j) p", p=P))
            vector_rows(4, a["conv_dw_w"][0].rearrange("w (j p) -> (w j) p", p=P))
            for q in range(4):
                sp.dma_start(gate_b[4 * (q // 2):4 * (q // 2) + 4, 1 - q % 2:2 - q % 2],
                             a["mlstm_gate_b"][0, q].rearrange("(h o) -> h o", o=1)).then_inc(sem("gate_b_in"), 16)
            for j in range(NT):
                src = a["x"][0, j * P:(j + 1) * P] if j < NL else a["ctx"][0, (j - NL) * P:(j - NL + 1) * P]
                sp.dma_start(x_tok[:, j, :], src).then_inc(sem("x_in"), 16)
            for q in range(8):
                sp.dma_start(ada_0[:, q], w_ada[0][:, :, q * 256:(q + 1) * 256]).then_inc(sem("ada0_in"), 16)
            with sp.Fori(0, 2) as i:
                n = G["conv"]
                load_unit(sp, n, w_even, i * 256 + 512, i=i)
                for r in (0, 1):
                    load_ada(sp, U["conv"], r, 0, 4 * i + 16 + r, i)
                load_unit(sp, n + 2, w_even, (i * 128) * 2, i=i)
                for r in (2, 3):
                    load_ada(sp, U["conv"] + 1, r, 0, 4 * i + 16 + r, i)
            for part in range(2):
                n = G["gate"] + part
                sp.wait_ge(low, n + 3)
                for q, (dst, src) in enumerate(((0, 4), (4, 12), (32, 0), (36, 8))):
                    if q == 3:
                        sp.wait_ge(sem("gate_parts"), 48 * (part + 1))
                    sp.dma_start(raw[:, n % 2, :, dst:dst + 4],
                                 w_even[:, 4 * part:4 * part + 4, GATE_COL + src:GATE_COL + src + 4]
                                 ).then_inc(raw_full[n % 2] if q == 3 else sem("gate_parts"), 16)
            with sp.Fori(0, 4) as i:
                for j in range(2):
                    load_unit(sp, G["qkov"] + 2 * j, w_even, i * 512 + (1024 + 256 * j), i=i)
                    for r in (8 + 2 * j, 9 + 2 * j):
                        load_ada(sp, U["qkov"] + j, r, 0, 4 * i + 16 + r, i)
            sp.wait_ge(sem("rows_ready"), 1)
            for d in range(2):
                sp.dma_start(m_dram[d], rows[4 * d:4 * d + 4, 1 + d, :]).then_inc(sem("m_out"), 16)
            n = G["out0"]
            load_unit(sp, n, w_even_out, 0)
            sp.wait_ge(sem("m_out"), 32)
            psum_read(sp, U["vt"] + 2)
            for h in range(HEADS):
                if h >= 2:
                    sp.wait_ge(sem("p_used"), 16 * (h - 1))
                sp.dma_start(negM[:, h % 2], m_dram[:, h, :].partition_broadcast(P)).then_inc(sem(f"m_in{h % 2}"), 16)
            sp.wait_ge(unit_done, U["out0"])
            for j in range(4):
                if j:
                    load_unit(sp, n + 2 * j, w_even_out, 256 * j)
                for r in (24 + 2 * j, 25 + 2 * j):
                    load_ada(sp, U["out0"] + j, r, 0, 16 + r)
            for l in range(2):
                if l:
                    w = w_odd
                    with sp.Fori(0, 2) as i:
                        for j in range(2):
                            load_unit(sp, G["in1"] + 2 * j, w, i * 512 + 256 * j, i=i)
                    sp.wait_ge(unit_done, U["n3"] + 2)
                    for dst, name in ((rope, "rope"), (icnt, "pool_count")):
                        sp.dma_start(dst[:, :, :], a[name].rearrange("a p t -> p a t")).then_inc(sem("tab_in"), 16)
                    sp.dma_start(rotw[:, 0, :], a["rotate"]).then_inc(sem("tab_in"), 16)
                    sp.wait_ge(sem("poolw_zero"), 1)
                    for g in range(4):
                        lo = 64 * (g % 2)
                        sp.dma_start(poolw[lo:lo + 64, g // 2, lo:lo + 64], a["pool_w"][0, g]).then_inc(sem("tab_in"), 16)
                    load_unit(sp, G["kin"], w, 1024)
                    load_unit(sp, G["vin"], w, 1280)
                    for j in range(4):
                        load_unit(sp, G["out1"] + 2 * j, w_odd_out, 256 * j)
                first = 0
                r0 = 32
                for g, size in enumerate(FFN_GROUPS):
                    n = G[f"up{l}{g}"]
                    with sp.Fori(0, size // 2) as i:
                        for j in range(2):
                            load_unit(sp, n + 2 * j, w_ffn_in[l], i * 256 + (first * P + j * D_FF), i=i)
                            if not l:
                                for r in (r0 + 2 * j, r0 + 2 * j + 1):
                                    load_ada(sp, U[f"up{l}{g}"] + j, r, 1, 4 * i + (r - 32), i)
                    if not l:
                        r0 += 2 * size
                    n = G[f"down{l}{g}"]
                    with sp.Fori(0, 2) as i:
                        for j in range(2):
                            load_unit(sp, n + 2 * j, w_ffn_out[l], i * 512 + 256 * j, first, size, i)
                            if not l and not g:
                                load_ada(sp, U[f"down{l}{g}"] + j, r0 + j, 1, 2 * i + (r0 + j - 32), i)
                    if not l and not g:
                        r0 += 4
                    first += size
            for j in range(NL):
                sp.wait_ge(sem("o_ready"), j + 1)
                sp.dma_start(out[0, j * P:(j + 1) * P], o_tok[:, j, :]).then_inc(sem("out_done"), 16)
            sp.wait_ge(sem("out_done"), 16 * NL)

        def product(pe, u, n, rhs, ready, ktiles=KD, segs=SEGS[T], i=0, ada=None, halves=(0, 1)):
            s = u % 2
            psum_free(pe, u, i)
            k = 0
            for part, kt in enumerate(SPLIT[ktiles]):
                slot = (n + part) % 4
                pe.wait_ge(low, n + part + 5 + 4 * i)
                for kk in range(kt):
                    ready(k)
                    for m in halves:
                        c = slice(m * P, (m + 1) * P)
                        for q, (w, x) in enumerate(((w_hi, rhs[0]), (w_hi, rhs[1]), (w_lo, rhs[0]))):
                            for t0, t1 in segs:
                                last = nc.tensor.matmul(acc[:, s, m, t0:t1], w[:, slot, kk, c], x[:, k, t0:t1],
                                                        start=(k == 0 and q == 0), stop=(k == ktiles - 1 and q == 2))
                    k += 1
            if ada:
                r0, count, per = ada
                for q in range(count):
                    r = r0 + q
                    pe.wait_ge(ada_full[r % 2], 16 * (r // 2 + 1) + 8 * per * i)
                    for k in range(KD):
                        last = nc.tensor.matmul(acc[:, s, 0, 1008 + 2 * q:1010 + 2 * q], ada_w[:, r % 2, k, :],
                                                cond[:, k, :], start=(k == 0), stop=(k == KD - 1))
            last.then_inc(unit_done, 1)

        @block.tensor
        def _(pe):
            def always(k):
                pass

            def h_tiles(stage):
                return lambda k: pe.wait_ge(h_ready, KD * stage + k + 1)

            def transpose(dst, src, rows_=P):
                return nc.tensor.transpose(dst, src, ident[0:rows_, 0:rows_])

            def column_sums(u, sources, tiles, wait, after):
                s = u % 2
                psum_free(pe, u)
                for m, src in enumerate(sources):
                    wait(m)
                    for j in range(tiles):
                        last = nc.tensor.matmul(acc[:, s, 0, j:j + 1], src(j), ones[:, 0:1],
                                                start=(m == 0 and j == 0),
                                                stop=(m == len(sources) - 1 and j == tiles - 1), skip_group_check=True)
                    if after is not None and m < len(sources) - 1:
                        last.then_inc(after, 1)
                last.then_inc(unit_done, 1)

            def spread(u, diagonal, tokens, count):
                psum_free(pe, u)
                pe.wait_ge(diag_ready, count)
                for t0, t1 in SEGS[tokens]:
                    last = nc.tensor.matmul(acc[:, u % 2, 0, t0:t1], ones[:, :], diagonal[:, t0:t1], start=True, stop=True)
                last.then_inc(unit_done, 1)

            def norm_x(u, first_sq, tokens, diag_count):
                column_sums(u, [(lambda j, m=m: sq[:, m % 2, j * P:(j + 1) * P]) for m in range(KD)], tokens // P,
                            lambda m: pe.wait_ge(sq_ready, first_sq + m + 1), sq_used)
                spread(u + 1, diag, tokens, diag_count)

            def norm_y(u, sums, tokens, diag_count):
                column_sums(u, [lambda j: sumsq[:, j * P:(j + 1) * P]], tokens // P,
                            lambda m: pe.wait_ge(sem("ysq_used"), KD * sums), None)
                spread(u + 1, diag, tokens, diag_count)

            pe.wait_ge(sem("ident_in"), 16)
            pe.wait_ge(sem("vec_in"), 16 * N_VECTORS)
            pe.wait_ge(sem("ones_set"), 1)
            psum_free(pe, U["vec"])
            for b, (n, m, col) in enumerate(((108, 0, 0), (84, 0, 128), (66, 0, 256), (66, 0, 384), (124, 1, 0))):
                last = transpose(acc[:, 0, m, col:col + n], vrows[0:n, b, :], n)
            last.then_inc(unit_done, 1)
            pe.wait_ge(sem("x_in"), 16 * NT)
            for v in range(4):
                u = U["xt"] + v
                psum_free(pe, u)
                for m in range(2):
                    for j in range(NT):
                        last = transpose(acc[:, u % 2, m, j * P:(j + 1) * P],
                                         x_tok[:, j, (2 * v + m) * P:(2 * v + m + 1) * P])
                last.then_inc(unit_done, 1)
            u = U["ada"]
            psum_free(pe, u)
            pe.wait_ge(sem("cond_ready"), 1)
            for m in range(16):
                if m % 2 == 0:
                    pe.wait_ge(sem("ada0_in"), 16 * 8)
                for k in range(KD):
                    last = nc.tensor.matmul(acc[:, u % 2, 0, 2 * m:2 * m + 2],
                                            ada_0[:, m // 2, k, (m % 2) * P:(m % 2 + 1) * P], cond[:, k, :],
                                            start=(k == 0), stop=(k == KD - 1))
            last.then_inc(unit_done, 1)
            norm_x(U["n0"], 0, T, 1)
            h = (h_hi, h_lo)
            with pe.Fori(0, 2) as i:
                for j in range(2):
                    product(pe, U["conv"] + j, G["conv"] + 2 * j, h, h_tiles(0), i=i, ada=(2 * j, 2, 4))
            product(pe, U["gate"], G["gate"], h, always, halves=(0,))
            with pe.Fori(0, 4) as i:
                for j in range(2):
                    product(pe, U["qkov"] + j, G["qkov"] + 2 * j, h, always, i=i, ada=(8 + 2 * j, 2, 4))
            u = U["gcol"]
            psum_free(pe, u)
            pe.wait_ge(sem("rows_ready"), 1)
            for x_, row in enumerate((5, 0, 3, 4)):
                for j in range(NT):
                    c = (x_ * NT + j) * 8
                    last = transpose(acc[:, u % 2, 0, c:c + 8], rows[0:8, row, j * P:(j + 1) * P], 8)
            last.then_inc(unit_done, 1)
            for v in range(3):
                u = U["vt"] + v
                psum_free(pe, u)
                for m in range(2):
                    j = 2 * v + m
                    for hd in range(HEADS):
                        last = transpose(acc[:, u % 2, m, hd * P:(hd + 1) * P], qkov[:, 8 + hd, j * P:(j + 1) * P])
                last.then_inc(unit_done, 1)
            def conv_cols(tile):
                return lambda j: conv_u[:, tile, (HALF + j * P if j < NL else U_CTX + (j - NL) * P):
                                        (HALF + j * P if j < NL else U_CTX + (j - NL) * P) + P]

            u = U["ln"]
            column_sums(u, [conv_cols(t) for t in range(4)], NT, lambda m: pe.wait_ge(sem("conv_done"), 1), None)
            spread(u + 1, ln_diag, T, 2)
            column_sums(u + 2, [(lambda j, m=m: ln_sq[:, m % 2, j * P:(j + 1) * P]) for m in range(4)], NT,
                        lambda m: pe.wait_ge(sem("ln_sq_ready"), m + 1), sem("ln_sq_used"))
            spread(u + 3, ln_diag, T, 3)
            u = U["mlstm"]
            psum_free(pe, u)
            psum_free(pe, u + 1)
            psum_read(pe, U["vt"] + 2)
            pe.wait_ge(sem("v_ones"), 1)

            def weigh(hd, q):
                for e, (d, t0, t1) in STEPS[q]:
                    pe.wait_ge(sem("p_ready"), 16 * hd + e + 1)
                    for t in range(t0 // P, t1 // P):
                        b, c = divmod(6 * d + t, 3)
                        dst = acc[:, 0, b // 2, (b % 2) * 512 + c * VW:(b % 2) * 512 + (c + 1) * VW]
                        last = nc.tensor.matmul(dst, probs[:, e % 4, t * P - t0:t * P - t0 + P], v_tok[:, ORDER[q], hd, :],
                                                start=(q, d, t) == FIRST_TOUCH[b], stop=(q, d, t) == LAST_TOUCH[b],
                                                skip_group_check=True)
                    last.then_inc(sem("p_used"), 1)

            pending = None
            pe.wait_ge(sem("qkov_ready"), 1)
            for z, (kind, hd, q) in enumerate(ITEMS):
                if kind == "X" and pending:
                    weigh(*pending)
                    pending = None
                if z >= 2:
                    was, of, q_ = ITEMS[z - 2]
                    if was == "S":
                        pe.wait_ge(sem("p_ready"), 16 * of + STEPS[q_][-1][0] + 1)
                    else:
                        pe.wait_ge(sem("merged_ready"), of + 1)
                if kind == "S":
                    for t0, t1 in (SEGS[T] if ORDER[q] >= NL else SEGS[LAT]):
                        last = nc.tensor.matmul(acc[:, 1, z % 2, t0:t1], qkov[:, 4 + hd, ORDER[q] * P:(ORDER[q] + 1) * P],
                                                qkov[:, hd, t0:t1], start=True, stop=True)
                else:
                    pe.wait_ge(sem("hn_ready"), hd + 1)
                    for j in range(NT):
                        last = transpose(acc[:, 1, z % 2, j * P:(j + 1) * P], h_tok[:, j, :])
                if z < len(ITEMS) - 1:
                    last.then_inc(sem("slot_full"), 1)
                if pending:
                    if pending[1] == 0 and hd:
                        pe.wait_ge(sem("sums_read"), hd)
                    weigh(*pending)
                pending = (hd, q) if kind == "S" else None
            last.then_inc(unit_done, 2)

            def ffn_and_norms(l, tokens, diag_count, sums, first_sq, stage, hid0):
                norm_y(U[f"n{1 + 3 * l}"], sums, tokens, diag_count)
                norm_x(U[f"m{1 + 3 * l}"], first_sq, tokens, diag_count + 1)
                segs = SEGS[tokens]
                r0 = 32
                for g, size in enumerate(FFN_GROUPS):
                    with pe.Fori(0, size // 2) as i:
                        for j in range(2):
                            product(pe, U[f"up{l}{g}"] + j, G[f"up{l}{g}"] + 2 * j, h, always if g else h_tiles(stage),
                                    segs=segs, i=i, ada=None if l else (r0 + 2 * j, 2, 4))
                    r0 += 2 * size
                    with pe.Fori(0, 2) as i:
                        for j in range(2):
                            product(pe, U[f"down{l}{g}"] + j, G[f"down{l}{g}"] + 2 * j, (hid_hi, hid_lo),
                                    lambda k: pe.wait_ge(sem("hid_ready"), hid0 + k // 2 + 1), ktiles=size, segs=segs, i=i,
                                    ada=None if l or g else (r0 + j, 1, 2))
                    if not g:
                        r0 += 4
                    hid0 += size // 2
                norm_y(U[f"n{2 + 3 * l}"], sums + 1, tokens, diag_count + 2)

            for j in range(4):
                product(pe, U["out0"] + j, G["out0"] + 2 * j, h, h_tiles(1), ada=(24 + 2 * j, 2, 4))
            ffn_and_norms(0, T, 4, 1, 8, 2, 0)
            norm_x(U["n3"], 16, T, 7)
            with pe.Fori(0, 2) as i:
                for j in range(2):
                    product(pe, U["in1"] + j, G["in1"] + 2 * j, h, h_tiles(3), segs=SEGS[LAT], i=i)
            product(pe, U["kin"], G["kin"], h, always)
            u, n = U["vin"], G["vin"]
            psum_free(pe, u)
            pe.wait_ge(low, n + 6)
            for j in range(NT):
                c = slice((j % 4) * 256, (j % 4) * 256 + 256)
                for k in range(KD):
                    slot = (n + k // 4) % 4
                    for q, (w, x) in enumerate(((w_hi, h_hi), (w_hi, h_lo), (w_lo, h_hi))):
                        last = nc.tensor.matmul(acc[:, u % 2, j // 4, c], x[:, k, j * P:(j + 1) * P], w[:, slot, k % 4, :],
                                                start=(k == 0 and q == 0), stop=(k == KD - 1 and q == 2))
            last.then_inc(unit_done, 1)
            u = U["qst"]
            psum_free(pe, u)
            for m in range(8):
                pe.wait_ge(sem("asq_ready"), m + 1)
                tiles, first = (NL, NL * m) if m < N_Q else (NT, NL * N_Q + NT * (m - N_Q))
                for j in range(tiles):
                    last = nc.tensor.matmul(acc[:, u % 2, 0, first + j:first + j + 1], asq[:, m % 2, j * P:(j + 1) * P],
                                            ones[:, 0:1], start=True, stop=True)
                last.then_inc(sem("asq_used") if m < 7 else unit_done, 1)
            pe.wait_ge(sem("rotw_ready"), 2)
            for v in range(4):
                u = U["rot"] + v
                psum_free(pe, u)
                for m in range(2):
                    x_ = inb[:, 2 + 2 * v + m, :] if v < 3 else kT[:, m, 0:LAT]
                    last = nc.tensor.matmul(acc[:, u % 2, m, 0:LAT], rotw[:, 1 + v // 3, :], x_, start=True, stop=True)
                last.then_inc(unit_done, 1)
            u = U["kb"]
            psum_free(pe, u)
            pe.wait_ge(sem("kdiag_ready"), 1)
            for m in range(2):
                for t0, t1 in SEGS[T]:
                    last = nc.tensor.matmul(acc[:, u % 2, m, t0:t1], ones[:, :], adiag[:, m, t0:t1], start=True, stop=True)
            last.then_inc(unit_done, 1)
            u = U["pool"]
            psum_free(pe, u)
            pe.wait_ge(sem("pooled"), 1)
            for m in range(2):
                last = nc.tensor.matmul(acc[:, u % 2, m, 0:LAT], poolw[:, m, :], pu[:, m, 8:8 + LAT], start=True, stop=True)
            last.then_inc(unit_done, 1)
            u = U["att"]
            psum_free(pe, u)
            psum_free(pe, u + 1)
            pe.wait_ge(sem("qk_ready"), 1)

            def scores(n):
                hd, i = divmod(n, NL)
                if n >= 2:
                    pe.wait_ge(sem("score_exp"), n - 1)
                for t0, t1 in SEGS[T]:
                    last = nc.tensor.matmul(acc[:, 0, n % 2, t0:t1], inb[:, 2 + hd, i * P:(i + 1) * P],
                                            kT[:, hd // 3, t0:t1], start=True, stop=True)
                last.then_inc(sem("score_full"), 1)

            scores(0)
            scores(1)
            for n in range(N_Q * NL):
                hd, i = divmod(n, NL)
                pe.wait_ge(sem("pn_ready"), n + 1)
                if n >= 1:
                    pe.wait_ge(sem("pT_ready"), n)
                for j in range(NT):
                    last = transpose(acc[:, 1, 0, j * P:(j + 1) * P], ptile[:, n % 2, j * P:(j + 1) * P])
                last.then_inc(sem("pT_full"), 1)
                if n + 2 < N_Q * NL:
                    scores(n + 2)
                pe.wait_ge(sem("pT_ready"), n + 1)
                if hd >= 2 and i == 0:
                    pe.wait_ge(h_ready, KD * 4 + 2 + hd - 1)
                c = (hd % 2) * 512 + i * P
                for j in range(NT):
                    last = nc.tensor.matmul(acc[:, 1, 1, c:c + P], v1[:, j, (hd // 3) * HD:(hd // 3 + 1) * HD],
                                            pT[:, n % 2, j * P:(j + 1) * P], start=(j == 0), stop=(j == NT - 1))
                if n < N_Q * NL - 1:
                    last.then_inc(sem("pv_done"), 1)
            last.then_inc(unit_done, 2)
            for j in range(4):
                product(pe, U["out1"] + j, G["out1"] + 2 * j, h, h_tiles(4), segs=SEGS[LAT])
            ffn_and_norms(1, LAT, 8, 3, 24, 5, FT // 2)
            pe.wait_ge(x_new, 4 * KD)
            for v in range(4):
                u = U["outT"] + v
                if v < 2:
                    psum_free(pe, u)
                else:
                    pe.wait_ge(sem("o_ready"), v - 1)
                for k in range(KD):
                    last = transpose(acc[:, u % 2, k // 4, (k % 4) * P:(k % 4 + 1) * P], xT[:, k, v * P:(v + 1) * P])
                last.then_inc(unit_done, 1)

        @block.scalar
        def _(act):
            sa = Steps(act, sem("act_step"))
            mods_flat = mods[:, :, :, :, :].rearrange("p l c k s -> p l (c k) s")

            def take_high(n, i=0):
                act.wait_ge(raw_full[n % 2], loaded(n, i))
                nc.scalar.activation(w_hi[:, n % 4], raw[:, n % 2], ACT.Copy).then_inc(high, 1)

            def next_high(u, n, i=0):
                if n + 2 < N_GRANULES:
                    act.wait_ge(unit_done, u + 2 * i)
                    take_high(n + 2, i)
                    take_high(n + 3, i)

            def take_ada(u, count, l, tile, i=0, per=4):
                vec = vec1 if l else vec0
                for q in range(count):
                    t = tile + q + per * i
                    last = nc.scalar.activation(mods_flat[:, l, bass.ds(t, 1), :],
                                                acc[:, u % 2, 0, 1008 + 2 * q:1010 + 2 * q].unsqueeze(1), ACT.Identity,
                                                bias=vec[:, bass.ds(t, 1)])
                last.then_inc(ada_out, 1)

            def square_x(first_new, norm, tokens):
                for m in range(KD):
                    if first_new is None:
                        psum_read(act, U["xt"] + m // 2)
                    else:
                        act.wait_ge(x_new, first_new + m + 1)
                    if m >= 2:
                        act.wait_ge(sq_used, 7 * norm + m - 1)
                    nc.scalar.activation(sq[:, m % 2, 0:tokens], xT[:, m, 0:tokens], ACT.Square).then_inc(sq_ready, 1)

            def square_y(u, first, tokens):
                psum_read(act, u)
                for m in (first, first + 1):
                    if m >= 2:
                        act.wait_ge(sem("ysq_used"), m - 1)
                    nc.scalar.activation(sq[:, m % 2, 0:tokens], y[:, m % KD, 0:tokens], ACT.Square
                                         ).then_inc(sem("ysq_ready"), 1)

            def roots(idx, nt):
                act.wait_ge(recip, idx)
                nc.scalar.activation(st[:, 1, 0:nt], st[:, 0, 0:nt], ACT.Sqrt).then_inc(root, 1)

            def modulate(use, l, comp, tokens):
                for m in range(KD):
                    act.wait_ge(t_ready, KD * use + m + 1)
                    for s, (t0, t1) in enumerate(SEGS[tokens]):
                        last = nc.scalar.activation(tbuf[:, m % 2, t0:t1], tbuf[:, m % 2, t0:t1], ACT.Identity,
                                                    bias=mods[:, l, comp, m, s:s + 1], scale=mods[:, l, comp + 1, m, s:s + 1])
                    sa.done(last)
                    sa.wait()
                    nc.scalar.activation(h_hi[:, m, 0:tokens], tbuf[:, m % 2, 0:tokens], ACT.Copy).then_inc(t_high, 1)

            act.wait_ge(unit_done, U["vec"] + 1)
            for s in range(2):
                last = nc.scalar.activation(cond[:, :, s], acc[:, 0, 0, 80 + KD * s:80 + KD * (s + 1)], ACT.Silu)
            last.then_inc(sem("cond_ready"), 1)
            for dst, m, col, n in ((vec0[:, :], 0, 0, 108), (vec1[:, :], 0, 128, 84), (ffn_cw[:, 0, :], 0, 256, 66),
                                   (ffn_cw[:, 1, :], 0, 384, 66),
                                   (dw_w[:, :, :].rearrange("p w j -> p (w j)"), 1, 0, 124)):
                last = nc.scalar.activation(dst, acc[:, 0, m, col:col + n], ACT.Copy)
            last.then_inc(set_free[U["vec"] % 2], 1)
            take_high(0)
            take_high(1)
            square_x(None, 0, T)
            roots(1, NT)
            modulate(0, 0, 0, T)
            act.wait_ge(sem("conv_zero"), 1)
            with act.Fori(0, 2) as i:
                u, n = U["conv"], G["conv"]
                next_high(u, n, i)
                psum_full(act, u, i)
                take_ada(u, 2, 0, 16, i)
                nc.scalar.activation(sig_b[:, bass.ds(2 * i, 2), :], acc[:, u % 2, :, 0:T], ACT.Sigmoid
                                     ).then_inc(set_free[u % 2], 1)
                u, n = u + 1, n + 2
                next_high(u, n, i)
                psum_full(act, u, i)
                take_ada(u, 2, 0, 18, i)
                for (t0, t1), c in zip(SEGS[T], (U_LAT, U_CTX)):
                    last = nc.scalar.activation(conv_u[:, bass.ds(2 * i + 1, 2), c:c + t1 - t0], acc[:, u % 2, :, t0:t1],
                                                ACT.Copy)
                last.then_inc(set_free[u % 2], 1)
            u = U["gate"]
            next_high(u, G["gate"])
            psum_full(act, u)
            act.wait_ge(sem("gate_b_in"), 64)
            nc.scalar.activation(rows[0:8, 2, :], acc[32:40, u % 2, 0, 0:T], ACT.Copy)
            nc.scalar.activation(rows[0:8, 0, :], acc[0:8, u % 2, 0, 0:T], ACT.Identity, bias=gate_b[0:8, 0:1]
                                 ).then_inc(set_free[u % 2], 1)
            psum_read(act, u)
            sa.done(nc.scalar.activation(rows[0:8, 1, :], rows[0:8, 0, :], ACT.Abs))
            sa.wait()
            sa.done(nc.scalar.activation(rows[0:8, 1, :], rows[0:8, 1, :], ACT.Exp, scale=-1.0))
            sa.wait()
            nc.scalar.activation(rows[0:8, 1, :], rows[0:8, 1, :], ACT.Ln, bias=1.0).then_inc(sem("gate_log"), 1)
            act.wait_ge(sem("sig_used"), 2)
            with act.Fori(0, 4) as i:
                for j in range(2):
                    u, n = U["qkov"] + j, G["qkov"] + 2 * j
                    next_high(u, n, i)
                    psum_full(act, u, i)
                    take_ada(u, 2, 0, 24 + 2 * j, i)
                    nc.scalar.activation(qkov[:, bass.ds(4 * i + 2 * j, 2), :], acc[:, u % 2, :, 0:T], ACT.Copy
                                         ).then_inc(set_free[u % 2], 1)
            psum_read(act, U["qkov"] + 7)
            nc.scalar.activation(qkov[:, 12:16, :], qkov[:, 12:16, :], ACT.Sigmoid).then_inc(sem("qkov_ready"), 1)
            u = U["gcol"]
            psum_full(act, u)
            nc.scalar.activation(gcols[:, 0:2].rearrange("p x j r -> p (x j r)"), acc[:, u % 2, 0, 0:96], ACT.Copy)
            nc.scalar.activation(gcols[:, 2:4].rearrange("p x j r -> p (x j r)"), acc[:, u % 2, 0, 96:192], ACT.Exp,
                                 scale=-1.0).then_inc(set_free[u % 2], 1)
            act.wait_ge(sem("m_out"), 32)
            for v in range(3):
                u = U["vt"] + v
                psum_full(act, u)
                for m in range(2):
                    last = nc.scalar.activation(v_tok[:, 2 * v + m, :, 0:HD],
                                                acc[:, u % 2, m, 0:512].rearrange("p (h d) -> p h d", h=HEADS), ACT.Copy)
                last.then_inc(set_free[u % 2], 1)
            conv_segs = tuple(zip(SEGS[T], (HALF, U_CTX)))
            for t in range(4):
                act.wait_ge(sem("conv_centred"), t + 1)
                if t >= 2:
                    act.wait_ge(sem("ln_sq_used"), t - 1)
                for (t0, t1), c in conv_segs:
                    last = nc.scalar.activation(ln_sq[:, t % 2, t0:t1], conv_u[:, t, c:c + t1 - t0], ACT.Square)
                last.then_inc(sem("ln_sq_ready"), 1)
            roots(2, NT)
            for t in range(4):
                act.wait_ge(sem("conv_normed"), t + 1)
                for (t0, t1), c in conv_segs:
                    last = nc.scalar.activation(conv_u[:, t, c:c + t1 - t0], conv_u[:, t, c:c + t1 - t0], ACT.Silu,
                                                bias=vec0[:, 100 + t:101 + t], scale=vec0[:, 96 + t:97 + t])
                sa.done(last)
                sa.wait()
                for (t0, t1), c in conv_segs:
                    last = nc.scalar.activation(h_hi[:, t, t0:t1], conv_u[:, t, c:c + t1 - t0], ACT.Copy)
                last.then_inc(sem("mix_high"), 1)

            def finish(hd):
                act.wait_ge(sem("sums_read"), hd + 1)
                for j in range(NT):
                    if hd and not j:
                        act.wait_ge(sem("hss_ready"), hd)
                    last = nc.scalar.activation(sq_junk[:, j, :], h_tok[:, j, :], ACT.Square, accum_out=hss[:, 0, j:j + 1])
                last.then_inc(sem("hss_ready"), 1)
                act.wait_ge(sem("hss_recip"), hd + 1)
                nc.scalar.activation(hss[:, 1, :], hss[:, 1, :], ACT.Sqrt).then_inc(sem("hss_root"), 1)

            for kind, hd, q in ITEMS:
                if kind == "S":
                    if q == 0:
                        act.wait_ge(sem(f"m_in{hd % 2}"), 16 * (hd // 2 + 1))
                    for e, (d, t0, t1) in STEPS[q]:
                        if 16 * hd + e >= 4:
                            act.wait_ge(sem("p_used"), 16 * hd + e - 3)
                        nc.scalar.activation(probs[:, e % 4, 0:t1 - t0], negM[:, hd % 2, d, t0:t1], ACT.Exp,
                                             bias=gcols[:, d, ORDER[q], hd + 4 * d:hd + 4 * d + 1]).then_inc(sem("e_ready"), 1)
                    if q == 0 and hd:
                        finish(hd - 1)
                    if q == 5:
                        act.wait_ge(sem("p_used"), 16 * (hd + 1))
                        nc.scalar.activation(den[:, 0], acc[:, 0].rearrange("p m (b c) -> p (m b) c", b=2)[:, :, HD:3 * VW:VW],
                                             ACT.Abs).then_inc(sem("den_abs"), 1)
                        if hd == HEADS - 1:
                            finish(hd)
                else:
                    act.wait_ge(sem("merged_ready"), hd + 1)
                    nc.scalar.activation(h_hi[:, 4 + hd, :], merged[:, :], ACT.Copy).then_inc(sem("mix_high"), 1)

            def ffn(l, norm_y, norm, tokens, idx):
                segs = SEGS[tokens]
                nt = tokens // P
                roots(idx, nt)
                square_x(16 * l, norm, tokens)
                roots(idx + 1, nt)
                modulate(1 + 2 * l, l, 3, tokens)
                tile, first_pair = 0, FT // 2 * l
                act.wait_ge(sem("pads_zero"), l + 1)
                for g, size in enumerate(FFN_GROUPS):
                    with act.Fori(0, size // 2) as i:
                        u, n = U[f"up{l}{g}"], G[f"up{l}{g}"]
                        next_high(u, n, i)
                        psum_full(act, u, i)
                        act.wait_ge(sem("ffn_conv"), first_pair + 1 + i)
                        if not l:
                            take_ada(u, 2, 1, tile, i)
                        for (t0, t1), c in zip(segs, (G_LAT, G_CTX)):
                            last = nc.scalar.activation(gpad[:, :, c:c + t1 - t0], acc[:, u % 2, :, t0:t1], ACT.Copy)
                        last.then_inc(set_free[u % 2], 1)
                        u, n = u + 1, n + 2
                        next_high(u, n, i)
                        act.wait_ge(sem("ffn_conv"), first_pair + 2 + i)
                        nc.scalar.activation(cbuf[:, :, 1:1 + CONV_LEN[tokens]],
                                             cbuf[:, :, 1:1 + CONV_LEN[tokens]], ACT.Silu
                                             ).then_inc(sem("ffn_silu"), 1)
                        if not l:
                            psum_full(act, u, i)
                            take_ada(u, 2, 1, tile + 2, i)
                        psum_read(act, u, i)
                        for (t0, t1), c in zip(segs, (G_LAT, G_CTX)):
                            last = nc.scalar.activation(hid_hi[:, bass.ds(2 * i, 2), t0:t1], cbuf[:, :, c:c + t1 - t0], ACT.Copy)
                        last.then_inc(sem("hid_high"), 1)
                    tile += 2 * size
                    first_pair += size // 2
                    last_group = g == len(FFN_GROUPS) - 1

                    def down(j, i=0):
                        u, n = U[f"down{l}{g}"] + j, G[f"down{l}{g}"] + 2 * j
                        next_high(u, n, i)
                        if not l and not g:
                            psum_full(act, u, i)
                            take_ada(u, 1, 1, tile + j, i, 2)
                        return u

                    if last_group:
                        for j in range(4):
                            u = down(j)
                            square_y(u, KD * norm_y + 2 * j, tokens)
                    else:
                        with act.Fori(0, 2) as i:
                            for j in range(2):
                                down(j, i)
                    if not l and not g:
                        tile += 4
                roots(idx + 2, nt)

            def mixer_out(l, norm_y, tokens):
                for j in range(4):
                    u, n = U[f"out{l}"] + j, G[f"out{l}"] + 2 * j
                    next_high(u, n)
                    if not l:
                        psum_full(act, u)
                        take_ada(u, 2, 0, 40 + 2 * j)
                    square_y(u, KD * norm_y + 2 * j, tokens)

            mixer_out(0, 0, T)
            ffn(0, 1, 1, T, 3)
            square_x(8, 2, T)
            roots(6, NT)
            modulate(2, 1, 0, T)
            with act.Fori(0, 2) as i:
                for j in range(2):
                    u, n = U["in1"] + j, G["in1"] + 2 * j
                    next_high(u, n, i)
                    psum_full(act, u, i)
                    nc.scalar.activation(inb[:, bass.ds(4 * i + 2 * j, 2), :], acc[:, u % 2, :, 0:LAT], ACT.Copy
                                         ).then_inc(set_free[u % 2], 1)
            u = U["kin"]
            next_high(u, G["kin"])
            psum_full(act, u)
            nc.scalar.activation(kT[:, :, :], acc[:, u % 2, :, 0:T], ACT.Copy).then_inc(set_free[u % 2], 1)
            u = U["vin"]
            next_high(u, G["vin"])
            psum_full(act, u)
            nc.scalar.activation(v1[:, 0:4, :], acc[:, u % 2, 0, :].rearrange("p (j c) -> p j c", c=256), ACT.Copy)
            nc.scalar.activation(v1[:, 4:6, :], acc[:, u % 2, 1, 0:512].rearrange("p (j c) -> p j c", c=256), ACT.Copy
                                 ).then_inc(set_free[u % 2], 1)
            psum_read(act, U["vin"])
            for m in range(8):
                if m >= 2:
                    act.wait_ge(sem("asq_used"), m - 1)
                src, tokens = (inb[:, 2 + m, :], LAT) if m < N_Q else (kT[:, m - N_Q, :], T)
                nc.scalar.activation(asq[:, m % 2, 0:tokens], src, ACT.Square).then_inc(sem("asq_ready"), 1)
            act.wait_ge(sem("tab_in"), 16 * 7)
            for q in range(2):
                nc.scalar.activation(rotw[:, 1 + q, :], rotw[:, 0, :], ACT.Copy, scale=vec1[:, 82 + q:83 + q]
                                     ).then_inc(sem("rotw_ready"), 1)
            act.wait_ge(recip, 7)
            nc.scalar.activation(acol[:, :], acol[:, :], ACT.Sqrt).then_inc(root, 1)
            act.wait_ge(sem("pool_float"), 1)
            nc.scalar.activation(h_hi[:, 0:2, 0:LAT], rt1[:, :, :], ACT.Copy).then_inc(sem("pool_high"), 1)

            def head_high(hd):
                if hd < N_Q - 1:
                    act.wait_ge(sem("pv_done"), NL * (hd + 1))
                else:
                    psum_full(act, U["att"] + 1)
                c = (hd % 2) * 512
                nc.scalar.activation(h_hi[:, 2 + hd, 0:LAT], acc[:, 1, 1, c:c + 512], ACT.Copy).then_inc(sem("o_high"), 1)

            for n in range(N_Q * NL):
                hd, i_ = divmod(n, NL)
                act.wait_ge(sem("score_max"), n + 1)
                if n >= 2:
                    act.wait_ge(sem("pT_full"), n - 1)
                nc.scalar.activation(ptile[:, n % 2, :], acc[:, 0, n % 2, 0:T], ACT.Exp, bias=arow[:, n, 1:2],
                                     scale=acol[:, n:n + 1], accum_out=arow[:, n, 2:3]).then_inc(sem("score_exp"), 1)
                if i_ == 1 and hd:
                    head_high(hd - 1)
            head_high(N_Q - 1)
            mixer_out(1, 2, LAT)
            ffn(1, 3, 3, LAT, 8)
            for v in range(4):
                u = U["outT"] + v
                psum_full(act, u)
                nc.scalar.activation(o_tok[:, v, :].rearrange("p (m c) -> p m c", m=2), acc[:, u % 2, :, 0:512], ACT.Copy
                                     ).then_inc(sem("o_ready"), 1)

        @block.vector
        def _(dve):
            sd = Steps(dve, sem("dve_step"))
            mods_flat = mods[:, :, :, :, :].rearrange("p l c k s -> p l (c k) s")

            def vt(out_, in0, in1, op):
                return nc.vector.tensor_tensor(out_, in0, in1, op)

            def gain_scale(l, comp, col):
                for s in range(2):
                    last = nc.vector.scalar_tensor_tensor(mods[:, l, comp, :, s], mods[:, l, comp, :, s], 1.0,
                                                          (vec1 if l else vec0)[:, col:col + KD], ALU.add, ALU.mult)
                return last

            def gain_gate(l, comp, col):
                for s in range(2):
                    last = vt(mods[:, l, comp, :, s], mods[:, l, comp, :, s], (vec1 if l else vec0)[:, col:col + KD], ALU.mult)
                return last

            def to_diagonals(dst, cols, nt, signal):
                for j in range(nt):
                    last = nc.vector.tensor_scalar(dst[:, j * P:(j + 1) * P], ident[:, :], cols[:, j:j + 1], None, ALU.mult)
                last.then_inc(signal, 1)

            def root_means(u, idx, nt, scale, dst):
                psum_full(dve, u)
                nc.vector.tensor_scalar(st[:, 0, 0:nt], acc[:, u % 2, 0, 0:nt], scale, EPS, ALU.mult, ALU.add
                                        ).then_inc(set_free[u % 2], 1)
                psum_read(dve, u)
                nc.vector.reciprocal(st[:, 0, 0:nt], st[:, 0, 0:nt]).then_inc(recip, 1)
                dve.wait_ge(root, idx)
                to_diagonals(dst, st[:, 1], nt, diag_ready)

            def give_back(u):
                nc.vector.tensor_copy(mark[:, u % 2:u % 2 + 1], acc[:, u % 2, 0, 0:1]).then_inc(set_free[u % 2], 1)

            def normed(u, use, stage, tokens):
                psum_full(dve, u)
                for m in range(KD):
                    if m >= 2:
                        dve.wait_ge(h_ready, KD * stage + m - 1)
                    vt(tbuf[:, m % 2, 0:tokens], xT[:, m, 0:tokens], acc[:, u % 2, 0, 0:tokens], ALU.mult).then_inc(t_ready, 1)
                give_back(u)

            def residual(u, l, comp, tokens):
                psum_full(dve, u)

                def add(m, value):
                    sd.wait(value)
                    for s, (t0, t1) in enumerate(SEGS[tokens]):
                        last = nc.vector.scalar_tensor_tensor(xT[:, m, t0:t1], y[:, m, t0:t1], mods[:, l, comp, m, s:s + 1],
                                                              xT[:, m, t0:t1], ALU.mult, ALU.add)
                    last.then_inc(x_new, 1)

                before = None
                for m in range(KD):
                    value = sd.done(vt(y[:, m, 0:tokens], y[:, m, 0:tokens], acc[:, u % 2, 0, 0:tokens], ALU.mult))
                    if m:
                        add(m - 1, before)
                    before = value
                add(KD - 1, before)
                give_back(u)

            def y_unit(u, tiles, tokens, add, i=0, adas=0):
                psum_full(dve, u, i)
                if adas:
                    dve.wait_ge(ada_out, adas + 2 * i)
                dst = y[:, tiles, 0:tokens]
                src = acc[:, u % 2, :, 0:tokens]
                (vt(dst, src, dst, ALU.add) if add else nc.vector.tensor_copy(dst, src)).then_inc(set_free[u % 2], 1)

            def add_squares(norm, m, tokens):
                c = KD * norm + m
                dve.wait_ge(sem("ysq_ready"), c + 1)
                if m:
                    dve.wait_ge(sem("ysq_used"), c)
                    ins = vt(sumsq[:, 0:tokens], sumsq[:, 0:tokens], sq[:, m % 2, 0:tokens], ALU.add)
                else:
                    ins = nc.vector.tensor_copy(sumsq[:, 0:tokens], sq[:, m % 2, 0:tokens])
                ins.then_inc(sem("ysq_used"), 1)

            def y_units(first, norm, tokens, add, adas=None):
                for j in range(4):
                    y_unit(first + j, slice(2 * j, 2 * j + 2), tokens, add, adas=adas[j] if adas else 0)
                    if j:
                        add_squares(norm, 2 * j - 2, tokens)
                        add_squares(norm, 2 * j - 1, tokens)
                add_squares(norm, KD - 2, tokens)
                add_squares(norm, KD - 1, tokens)

            nc.vector.memset(ones[:, :], 1.0).then_inc(sem("ones_set"), 1)
            nc.vector.memset(mark[:, 0:1], 0.0).then_inc(set_free[0], 1)
            nc.vector.memset(mark[:, 1:2], 0.0).then_inc(set_free[1], 1)
            nc.vector.memset(mods[:, 1, 0, 0, :], 0.0).then_inc(sem("ffn_conv"), 1)
            for v in range(4):
                u = U["xt"] + v
                psum_full(dve, u)
                nc.vector.tensor_copy(xT[:, 2 * v:2 * v + 2, :], acc[:, u % 2, :, 0:T]).then_inc(set_free[u % 2], 1)
            u = U["ada"]
            psum_full(dve, u)
            psum_read(dve, U["vec"])
            for s in range(2):
                last = vt(mods_flat[:, 0, 0:16, s], acc[:, u % 2, 0, s:32:2], vec0[:, 0:16], ALU.add)
            last.then_inc(set_free[u % 2], 1)
            psum_read(dve, u)
            sd.done(gain_scale(0, 1, 48))
            sd.wait()
            root_means(U["n0"], 1, NT, 1.0 / D, diag)
            normed(U["n0"] + 1, 0, 0, T)

            taps_len = LAT + HALF + CTX

            def gate_inputs(first):
                for t in (first, first + 1):
                    for (t0, t1), c in zip(SEGS[T], (U_LAT, U_CTX)):
                        last = vt(conv_u[:, t + 1, c:c + t1 - t0], conv_u[:, t + 1, c:c + t1 - t0], sig_b[:, t, t0:t1], ALU.mult)
                last.then_inc(sem("sig_used"), 1)

            def conv_pair(first):
                dve.wait_ge(sem("sig_used"), first // 2 + 1)
                with dve.Fori(0, 2) as t:
                    sd.loop(t, TAPS)
                    dst = conv_u[:, bass.ds(t + first, 1), HALF:HALF + taps_len]
                    for w in range(TAPS):
                        src = conv_u[:, bass.ds(t + (first + 1), 1), w:w + taps_len]
                        sd.wait()
                        tap = dw_w[:, w, bass.ds(t + first, 1)]
                        if w == 0:
                            ins = nc.vector.tensor_scalar(dst, src, tap, None, ALU.mult)
                        else:
                            ins = nc.vector.scalar_tensor_tensor(dst, src, tap, dst, ALU.mult, ALU.add)
                        sd.done(ins)
                    sd.end(2)
                sd.wait()

            psum_read(dve, U["conv"] + 1)
            gate_inputs(0)
            conv_pair(0)
            psum_read(dve, U["conv"] + 3)
            gate_inputs(2)
            r8 = [rows[0:8, q, :] for q in range(6)]
            lat, con = slice(0, LAT), slice(LAT, T)
            dve.wait_ge(sem("gate_log"), 1)
            sd.done(nc.vector.scalar_tensor_tensor(r8[0], r8[0], 0.0, r8[1], ALU.min, ALU.subtract))
            sd.wait()

            def scan(dst, src, op, other):
                sd.done(nc.vector.tensor_tensor_scan(dst[0][:, con], src[0][:, con], src[0][:, con], 0.0, op, other))
                back = sd.done(nc.vector.tensor_tensor_scan(dst[1][:, ::-1], src[1][:, ::-1], src[1][:, ::-1], 0.0, op, other))
                sd.wait(back)
                sd.done(nc.vector.tensor_tensor_scan(dst[0][:, lat], src[0][:, lat], src[0][:, lat],
                                                     dst[0][:, T - 1:T], op, other))
                sd.wait()

            scan((r8[3], r8[4]), (r8[0], r8[0]), ALU.add, ALU.bypass)
            b_i = gate_b[0:8, 1:2]
            sd.done(nc.vector.scalar_tensor_tensor(r8[5], r8[2], b_i, r8[3], ALU.add, ALU.subtract))
            sd.done(nc.vector.scalar_tensor_tensor(r8[0], r8[2], b_i, r8[4], ALU.add, ALU.subtract))
            sd.wait()
            scan((r8[1], r8[2]), (r8[5], r8[0]), ALU.max, ALU.bypass)
            sd.done(vt(r8[3], r8[3], r8[1], ALU.add))
            sd.done(vt(r8[4], r8[4], r8[2], ALU.add))
            sd.wait()
            nc.vector.tensor_scalar(r8[1], r8[1], -1.0, None, ALU.mult)
            nc.vector.tensor_scalar(r8[2], r8[2], -1.0, None, ALU.mult).then_inc(sem("rows_ready"), 1)
            conv_pair(2)
            nc.vector.tensor_copy(mark[:, 2:3], ident[:, 0:1]).then_inc(sem("conv_done"), 1)
            u = U["ln"]
            psum_full(dve, u)
            dve.wait_ge(sem("conv_done"), 1)
            nc.vector.tensor_scalar(st[:, 1, 0:NT], acc[:, u % 2, 0, 0:NT], 1.0 / 512, None, ALU.mult).then_inc(set_free[u % 2], 1)
            psum_read(dve, u)
            to_diagonals(ln_diag, st[:, 1], NT, diag_ready)
            conv_segs = tuple(zip(SEGS[T], (HALF, U_CTX)))

            def all_tiles(u, op, signal):
                psum_full(dve, u)
                for t in range(4):
                    for (t0, t1), c in conv_segs:
                        x_ = conv_u[:, t, c:c + t1 - t0]
                        last = vt(x_, x_, acc[:, u % 2, 0, t0:t1], op)
                    last.then_inc(signal, 1)
                give_back(u)

            all_tiles(u + 1, ALU.subtract, sem("conv_centred"))
            root_means(u + 2, 2, NT, 1.0 / 512, ln_diag)
            all_tiles(u + 3, ALU.mult, sem("conv_normed"))

            scale = float(HD) ** -0.5
            masked = 0
            dve.wait_ge(h_ready, KD + 4)
            for z, (kind, hd, q) in enumerate(ITEMS):
                if z < len(ITEMS) - 1:
                    dve.wait_ge(sem("slot_full"), z + 1)
                else:
                    psum_full(dve, U["mlstm"] + 1)
                if kind == "X":
                    if hd:
                        dve.wait_ge(h_ready, KD + 4 + hd)
                    nc.vector.scalar_tensor_tensor(merged[:, :], acc[:, 1, z % 2, 0:T], vec0[:, 104 + hd:105 + hd],
                                                   qkov[:, 12 + hd, :], ALU.mult, ALU.mult).then_inc(sem("merged_ready"), 1)
                    continue
                for e, (d, t0, t1) in STEPS[q]:
                    e += 16 * hd
                    s_tile = ORDER[q]
                    if t0 <= s_tile * P < t1:
                        masked += 1
                        dve.wait_ge(sem("e_masked"), masked)
                    else:
                        dve.wait_ge(sem("e_ready"), e + 1)
                    p_ = probs[:, e % 4, 0:t1 - t0]
                    nc.vector.scalar_tensor_tensor(p_, acc[:, 1, z % 2, t0:t1], scale, p_, ALU.mult, ALU.mult
                                                   ).then_inc(sem("p_ready"), 1)
                if q == 5:
                    dve.wait_ge(sem("den_abs"), hd + 1)
                    for d in range(2):
                        sd.done(vt(den[:, 1].rearrange("p b c -> p (b c)")[:, 6 * d:6 * d + 6],
                                   den[:, 0].rearrange("p b c -> p (b c)")[:, 6 * d:6 * d + 6],
                                   gcols[:, 2 + d, :, hd + 4 * d], ALU.max))
                    sd.wait()
                    sd.done(nc.vector.reciprocal(den[:, 1], den[:, 1]))
                    sd.wait()
                    w_ = den[:, 1].rearrange("p b c -> p (b c)")

                    def sums(d, t):
                        b, c = divmod(6 * d + t, 3)
                        c = (b % 2) * 512 + c * VW
                        return acc[:, 0, b // 2, c:c + HD]

                    if hd:
                        dve.wait_ge(sem("merged_ready"), hd)
                    for t in range(NT):
                        last = nc.vector.tensor_scalar(h_tok[:, t, :], sums(0, t), w_[:, t:t + 1], None, ALU.mult)
                    sd.done(last)
                    sd.wait()
                    for t in range(NT):
                        last = nc.vector.scalar_tensor_tensor(h_tok[:, t, :], sums(1, t), w_[:, 6 + t:7 + t], h_tok[:, t, :],
                                                              ALU.mult, ALU.add)
                    last.then_inc(sem("sums_read"), 1)
                    if hd < HEADS - 1:
                        continue
                if (q == 0 and hd) or q == 5:
                    of = hd if q == 5 else hd - 1
                    dve.wait_ge(sem("hss_ready"), of + 1)
                    sd.done(nc.vector.tensor_scalar(hss[:, 1, :], hss[:, 0, :], 1.0 / HD, EPS, ALU.mult, ALU.add))
                    sd.wait()
                    nc.vector.reciprocal(hss[:, 1, :], hss[:, 1, :]).then_inc(sem("hss_recip"), 1)
                    dve.wait_ge(sem("hss_root"), of + 1)
                    for t in range(NT):
                        last = nc.vector.tensor_scalar(h_tok[:, t, :], h_tok[:, t, :], hss[:, 1, t:t + 1], None, ALU.mult)
                    last.then_inc(sem("hn_ready"), 1)
            dve.wait_ge(sem("merged_ready"), HEADS)
            nc.vector.tensor_copy(mark[:, 3:4], ident[:, 0:1]).then_inc(set_free[0], 1)
            nc.vector.tensor_copy(mark[:, 4:5], ident[:, 0:1]).then_inc(set_free[1], 1)

            def ffn(l, norm, tokens, idx, stage):
                segs = tuple(zip(SEGS[tokens], (G_LAT, G_CTX)))
                nt = tokens // P
                length = CONV_LEN[tokens]
                root_means(U[f"n{1 + 3 * l}"], idx, nt, 1.0 / D, diag)
                if not l:
                    dve.wait_ge(ada_out, 16)
                    last = gain_gate(0, 2, 56)
                    last = gain_scale(0, 4, 64)
                    last = gain_gate(0, 5, 72)
                else:
                    last = gain_gate(1, 2, 56)
                    last = gain_scale(1, 4, 64)
                    last = gain_gate(1, 5, 72)
                sd.done(last)
                residual(U[f"n{1 + 3 * l}"] + 1, l, 2, tokens)
                root_means(U[f"m{1 + 3 * l}"], idx + 1, nt, 1.0 / D, diag)
                normed(U[f"m{1 + 3 * l}"] + 1, 1 + 2 * l, stage, tokens)
                for c in (0, LAT + 1, T + 2):
                    last = nc.vector.memset(gpad[:, :, c:c + 1], 0.0)
                last.then_inc(sem("pads_zero"), 1)
                tile, pair, adas = 0, FT // 2 * l, 16
                for g, size in enumerate(FFN_GROUPS):
                    with dve.Fori(0, size // 2) as i:
                        sd.loop(i, 5)
                        u = U[f"up{l}{g}"]
                        psum_read(dve, u, i)
                        for w in range(3):
                            for m in range(2):
                                c = ffn_cw[:, l, bass.ds(2 * i + (w * FT + tile + m), 1)]
                                src = gpad[:, m, w:w + length]
                                dst = cbuf[:, m, 1:1 + length]
                                if w:
                                    sd.wait(sd.value() - 1)
                                    ins = nc.vector.scalar_tensor_tensor(dst, src, c, dst, ALU.mult, ALU.add)
                                else:
                                    ins = nc.vector.tensor_scalar(dst, src, c, None, ALU.mult)
                                if w == 2 and m:
                                    ins.then_inc(sem("ffn_conv"), 1)
                                else:
                                    sd.done(ins)
                        u += 1
                        psum_full(dve, u, i)
                        dve.wait_ge(sem("ffn_silu"), pair + 1 + i)
                        if not l:
                            dve.wait_ge(ada_out, adas + 2 + 2 * i)
                        for (t0, t1), c in segs:
                            ins = vt(cbuf[:, :, c:c + t1 - t0], cbuf[:, :, c:c + t1 - t0], acc[:, u % 2, :, t0:t1], ALU.mult)
                        ins.then_inc(set_free[u % 2], 1)
                        dve.wait_ge(sem("hid_high"), pair + 1 + i)
                        for (t0, t1), c in segs:
                            k = bass.ds(2 * i, 2)
                            ins = vt(hid_lo[:, k, t0:t1], cbuf[:, :, c:c + t1 - t0], hid_hi[:, k, t0:t1].bitcast(F32), ALU.subtract)
                        ins.then_inc(sem("hid_ready"), 1)
                        dve.wait_ge(sem("hid_ready"), pair + 1 + i)
                        sd.end(size // 2)
                    tile += size
                    pair += size // 2
                    adas += size
                    first = U[f"down{l}{g}"]
                    if g == len(FFN_GROUPS) - 1:
                        y_units(first, norm + 1, tokens, True)
                    else:
                        with dve.Fori(0, 2) as i:
                            for j in range(2):
                                y_unit(first + j, bass.ds(4 * i + 2 * j, 2), tokens, g > 0, i,
                                       adas + 1 + j if not l and not g else 0)
                    if not g:
                        adas += 4
                root_means(U[f"n{2 + 3 * l}"], idx + 2, nt, 1.0 / D, diag)
                residual(U[f"n{2 + 3 * l}"] + 1, l, 5, tokens)

            y_units(U["out0"], 0, T, False, adas=(13, 14, 15, 16))
            ffn(0, 0, T, 3, 2)
            dve.wait_ge(ada_out, 42)
            sd.done(gain_scale(1, 1, 48))
            sd.wait()
            root_means(U["n3"], 6, NT, 1.0 / D, diag)
            normed(U["n3"] + 1, 2, 3, T)
            nc.vector.memset(poolw[:, :, :], 0.0).then_inc(sem("poolw_zero"), 1)
            sd.done(nc.vector.memset(pu[:, :, :], 0.0))
            u = U["qst"]
            psum_full(dve, u)
            nc.vector.tensor_scalar(acol[:, :], acc[:, u % 2, 0, 0:36], 1.0 / HD, EPS, ALU.mult, ALU.add
                                    ).then_inc(set_free[u % 2], 1)
            psum_read(dve, u)
            nc.vector.reciprocal(acol[:, :], acol[:, :]).then_inc(recip, 1)
            dve.wait_ge(sem("tab_in"), 16 * 7)
            for v in range(4):
                u = U["rot"] + v
                psum_full(dve, u)
                for m in range(2):
                    x_ = inb[:, 2 + 2 * v + m, :] if v < 3 else kT[:, m, 0:LAT]
                    g = vec1[:, 82 + v // 3:83 + v // 3]
                    sd.done(vt(rt1[:, m, :], acc[:, u % 2, m, 0:LAT], rope[:, 1, :], ALU.mult))
                    sd.done(nc.vector.scalar_tensor_tensor(x_, x_, g, rope[:, 0, :], ALU.mult, ALU.mult))
                    sd.wait()
                    last = vt(x_, x_, rt1[:, m, :], ALU.add)
                last.then_inc(set_free[u % 2], 1)
                psum_read(dve, u)
            g = vec1[:, 83:84]
            sd.done(nc.vector.tensor_scalar(kT[:, :, LAT:T], kT[:, :, LAT:T], g, None, ALU.mult))
            dve.wait_ge(root, 7)
            for m in range(2):
                for j in range(NT):
                    c = NL * N_Q + NT * m + j
                    last = nc.vector.tensor_scalar(adiag[:, m, j * P:(j + 1) * P], ident[:, :], acol[:, c:c + 1], None, ALU.mult)
            last.then_inc(sem("kdiag_ready"), 1)
            sd.done(nc.vector.tensor_scalar(acol[:, 0:NL * N_Q], acol[:, 0:NL * N_Q], scale, None, ALU.mult))
            sd.wait()
            sd.done(nc.vector.tensor_copy(pu[:, :, 8:8 + LAT], inb[:, 0:2, :]))
            sd.wait()
            sd.done(vt(ps2[:, :, 1:PW], pu[:, :, 0:PW - 1], pu[:, :, 1:PW], ALU.add))
            sd.wait()
            sd.done(vt(ps4[:, :, 2:PW - 1], ps2[:, :, 1:PW - 2], ps2[:, :, 3:PW], ALU.add))
            sd.wait()
            c8 = slice(8, 8 + LAT)
            sd.done(vt(ps2[0:64, 0, c8], ps2[0:64, 0, c8], icnt[0:64, 0, :], ALU.mult))
            sd.done(vt(ps2[64:128, 0, c8], ps4[64:128, 0, c8], icnt[64:128, 0, :], ALU.mult))
            sd.done(vt(ps2[:, 1, 4:PW - 3], ps4[:, 1, 2:PW - 5], ps4[:, 1, 6:PW - 1], ALU.add))
            sd.wait()
            sd.done(vt(ps4[:, 1, c8], ps2[:, 1, 4:4 + LAT], ps2[:, 1, 12:12 + LAT], ALU.add))
            sd.wait()
            sd.done(vt(ps4[64:128, 1, c8], ps4[64:128, 1, c8], icnt[64:128, 1, :], ALU.mult))
            sd.done(vt(ps4[0:64, 1, c8], ps2[0:64, 1, c8], icnt[0:64, 1, :], ALU.mult))
            sd.wait()
            vt(pu[:, 0, c8], ps2[:, 0, c8], pu[:, 0, c8], ALU.subtract)
            vt(pu[:, 1, c8], ps4[:, 1, c8], pu[:, 1, c8], ALU.subtract).then_inc(sem("pooled"), 1)
            u = U["kb"]
            psum_full(dve, u)
            nc.vector.tensor_tensor(kT[:, :, :], kT[:, :, :], acc[:, u % 2, :, 0:T], ALU.mult).then_inc(set_free[u % 2], 1)
            psum_read(dve, u)
            u = U["pool"]
            psum_full(dve, u)
            for m in range(2):
                last = nc.vector.tensor_scalar(rt1[:, m, :], acc[:, u % 2, m, 0:LAT], vec1[:, 80 + m:81 + m], None, ALU.mult)
            last.then_inc(set_free[u % 2], 1)
            psum_read(dve, u)
            nc.vector.tensor_copy(mark[:, 5:6], ident[:, 0:1]).then_inc(sem("qk_ready"), 1)
            nc.vector.tensor_copy(mark[:, 6:7], ident[:, 0:1]).then_inc(sem("pool_float"), 1)
            dve.wait_ge(sem("pool_high"), 1)
            vt(h_lo[:, 0:2, 0:LAT], rt1[:, :, :], h_hi[:, 0:2, 0:LAT].bitcast(F32), ALU.subtract).then_inc(h_ready, 2)

            def head_low(hd):
                dve.wait_ge(sem("o_high"), hd + 1)
                c = (hd % 2) * 512
                vt(h_lo[:, 2 + hd, 0:LAT], acc[:, 1, 1, c:c + 512], h_hi[:, 2 + hd, 0:LAT].bitcast(F32), ALU.subtract
                   ).then_inc(h_ready, 1)

            for n in range(N_Q * NL + 1):
                if n < N_Q * NL:
                    dve.wait_ge(sem("score_full"), n + 1)
                    sd.done(nc.vector.reduce_max(arow[:, n, 0:1], acc[:, 0, n % 2, 0:T], AX.X))
                    sd.wait()
                    nc.vector.tensor_scalar(arow[:, n, 1:2], arow[:, n, 0:1], acol[:, n:n + 1], -1.0, ALU.mult, ALU.mult
                                            ).then_inc(sem("score_max"), 1)
                if n >= 1:
                    dve.wait_ge(sem("pT_full"), n)
                    if n >= 3:
                        dve.wait_ge(sem("pv_done"), n - 2)
                    nc.vector.tensor_copy(pT[:, (n - 1) % 2, :], acc[:, 1, 0, 0:T]).then_inc(sem("pT_ready"), 1)
                if n < N_Q * NL:
                    dve.wait_ge(sem("score_exp"), n + 1)
                    sd.done(nc.vector.reciprocal(arow[:, n, 3:4], arow[:, n, 2:3]))
                    sd.wait()
                    nc.vector.tensor_scalar(ptile[:, n % 2, :], ptile[:, n % 2, :], arow[:, n, 3:4], None, ALU.mult
                                            ).then_inc(sem("pn_ready"), 1)
                    if n % NL == 2 and n > NL:
                        head_low(n // NL - 1)
            head_low(N_Q - 1)
            dve.wait_ge(h_ready, 5 * KD)
            nc.vector.tensor_copy(mark[:, 7:8], ident[:, 0:1]).then_inc(set_free[0], 1)
            nc.vector.tensor_copy(mark[:, 8:9], ident[:, 0:1]).then_inc(set_free[1], 1)
            y_units(U["out1"], 2, LAT, False)
            ffn(1, 2, LAT, 8, 5)

        @block.gpsimd
        def _(pool):
            def take_low(n, i=0):
                pool.wait_ge(high, n + 1 + 4 * i)
                nc.gpsimd.tensor_tensor(w_lo[:, n % 4], raw[:, n % 2], w_hi[:, n % 4].bitcast(F32), ALU.subtract).then_inc(low, 1)

            def take_lows(first, turns):
                with pool.Fori(0, turns) as i:
                    for j in range(4):
                        take_low(first + j, i)

            def h_lows(use, stage, tokens):
                for m in range(KD):
                    pool.wait_ge(t_high, KD * use + m + 1)
                    nc.gpsimd.tensor_tensor(h_lo[:, m, 0:tokens], tbuf[:, m % 2, 0:tokens], h_hi[:, m, 0:tokens].bitcast(F32),
                                            ALU.subtract).then_inc(h_ready, 1)

            nc.gpsimd.memset(conv_u[:, 0, 0:1], 0.0).then_inc(low, 4)
            take_low(0)
            take_low(1)
            h_lows(0, 0, T)
            pool.wait_ge(unit_done, U["n0"] + 2)
            nc.gpsimd.memset(conv_u[:, :, :], 0.0).then_inc(sem("conv_zero"), 1)
            n = G["conv"] + 2
            take_lows(n, 2)
            take_low(n + 8)
            take_low(n + 9)
            take_lows(n + 10, 4)
            pool.wait_ge(unit_done, U["gcol"] + 1)
            pool.wait_ge(sem("m_out"), 32)
            nc.gpsimd.memset(v_tok[:, :, :, HD:VW], 1.0).then_inc(sem("v_ones"), 1)
            for t in range(4):
                pool.wait_ge(sem("mix_high"), t + 1)
                for (t0, t1), c in zip(SEGS[T], (HALF, U_CTX)):
                    last = nc.gpsimd.tensor_tensor(h_lo[:, t, t0:t1], conv_u[:, t, c:c + t1 - t0],
                                                   h_hi[:, t, t0:t1].bitcast(F32), ALU.subtract)
                last.then_inc(h_ready, 1)
            for kind, hd, q in ITEMS:
                if kind == "X":
                    pool.wait_ge(sem("mix_high"), 5 + hd)
                    nc.gpsimd.tensor_tensor(h_lo[:, 4 + hd, :], merged[:, :], h_hi[:, 4 + hd, :].bitcast(F32), ALU.subtract
                                            ).then_inc(h_ready, 1)
                    continue
                s_tile = ORDER[q]
                for e, (d, t0, t1) in STEPS[q]:
                    if t0 <= s_tile * P < t1:
                        pool.wait_ge(sem("e_ready"), 16 * hd + e + 1)
                        block_ = probs[:, e % 4, s_tile * P - t0:s_tile * P - t0 + P]
                        sign = -1 if d else 1
                        nc.gpsimd.affine_select(out=block_, in_=block_, compare_op=ALU.is_ge, fill=0.0, base=0,
                                                pattern=[[sign, P]], channel_multiplier=-sign).then_inc(sem("e_masked"), 1)
            take_lows(G["out0"] + 2, 2)
            h_lows(1, 2, T)
            take_lows(G["up00"] + 2, 17)
            h_lows(2, 3, T)
            take_lows(G["in1"] + 2, 3)
            take_lows(G["out1"] + 2, 2)
            h_lows(3, 5, LAT)
            take_lows(G["up10"] + 2, 16)
            take_low(N_GRANULES - 2)
            take_low(N_GRANULES - 1)



_INS = ("x", "c", "ctx", "c_ctx", "ada_w", "ada_b", "mix_pre_g", "mix_post_g", "ffn_pre_g", "ffn_post_g", "ffn_w_in",
        "ffn_conv_w", "ffn_w_out", "even_w_in", "even_w_out", "conv_dw_w", "conv_ln_g", "conv_ln_b", "mlstm_gate_b",
        "mlstm_norm_g", "odd_w_in", "odd_w_out", "pool_w", "pool_scale", "q_norm_g", "k_norm_g")


def constants():
    freq = HD // 4
    inv = (10000.0 ** (-np.arange(freq, dtype=np.float32) / np.float32(freq))).astype(np.float32)
    t = np.arange(LAT)
    row, col = (t // 64).astype(np.float32), (t % 64).astype(np.float32)
    angle = np.concatenate([row[:, None] * inv, col[:, None] * inv], axis=-1).astype(np.float32)
    of_pair = np.arange(HD) // 2
    rope = np.stack([np.cos(angle)[:, of_pair].T, np.sin(angle)[:, of_pair].T]).astype(np.float32)
    rotate = np.zeros((P, P), np.float32)
    even = np.arange(0, P, 2)
    rotate[even + 1, even] = -1.0
    rotate[even, even + 1] = 1.0
    count = np.zeros((2, P, LAT), np.float32)
    for g, w in enumerate(WINDOWS):
        n = np.clip(t + w // 2, 0, LAT) - np.clip(t - w // 2, 0, LAT)
        count[g // 2, 64 * (g % 2):64 * (g % 2) + 64] = 1.0 / n
    return {"identity": np.eye(P, dtype=np.float32), "rope": rope, "rotate": rotate, "pool_count": count}


def kernel(**inputs):
    import concourse.bacc as bacc
    from concourse.bass_utils import run_bass_kernel_spmd

    nc = bacc.Bacc("TRN2", target_bir_lowering=False, num_devices=1)
    arrays, a = {}, {}
    for name, x in [(n, inputs[n]) for n in _INS] + list(constants().items()):
        x = np.ascontiguousarray(x)
        arrays[f"in_{name}"] = x
        a[name] = nc.dram_tensor(f"in_{name}", x.shape, mybir.dt.from_np(x.dtype), kind="ExternalInput").ap()
    out = nc.dram_tensor("out_x", (1, LAT, D), F32, kind="ExternalOutput").ap()
    build(nc, a, out)
    r = run_bass_kernel_spmd(nc, [arrays], core_ids=[0])
    return r.results[0]["out_x"]
```

```python
from contextlib import ExitStack

import numpy as np

import concourse.bass as bass
from concourse import mybir

F32 = mybir.dt.float32
F32R = mybir.dt.float32r
ALU = mybir.AluOpType
ACT = mybir.ActivationFunctionType
AX = mybir.AxisListType

P = 128
D = 1024
KD = D // P
LAT = 512
CTX = 256
T = LAT + CTX
NT = T // P
NL = LAT // P
EPS = 1e-6
D_FF = 2816
FT = D_FF // P
TAPS = 31
HEADS = 4
HD = 128
GATE_COL = 3072
VW = HD + 1
N_VECTORS = 19
N_Q, N_KV = 6, 2
D_POOL = 256
WINDOWS = (2, 4, 8, 16)
FFN_GROUPS = (8, 8, 6)
SEGS = {T: ((0, LAT), (LAT, T)), LAT: ((0, LAT),)}
HALF = TAPS // 2
U_LAT, U_CTX = HALF, 2 * HALF + LAT
U_LEN = 3 * HALF + T + 1
G_LAT, G_CTX = 1, LAT + 2
G_LEN = T + 4


class Steps:

    def __init__(self, eng, sem):
        self.eng, self.sem, self.count, self.reg, self.per, self.first = eng, sem, 0, None, 0, 0

    def done(self, ins):
        self.count += 1
        ins.then_inc(self.sem, 1)
        return self.value()

    def value(self):
        return self.count if self.reg is None else self.reg * self.per + self.count

    def wait(self, value=None):
        self.eng.wait_ge(self.sem, self.value() if value is None else value)

    def loop(self, reg, per):
        self.reg, self.per, self.first = reg, per, self.count

    def end(self, trips):
        assert self.count - self.first == self.per, (self.count - self.first, self.per)
        self.count = self.first + self.per * trips
        self.reg = None


def plan():
    order = [("cond", 1, 0), ("vec", 1, 0), ("xt", 4, 0), ("ada", 1, 0), ("n0", 2, 0), ("conv", 4, 2), ("gate", 1, 2), ("qkov", 8, 2),
             ("gcol", 1, 0), ("vt", 3, 0), ("ln", 4, 0), ("mlstm", 2, 0), ("out0", 4, 2)]
    for l in range(2):
        if l:
            order += [("n3", 2, 0), ("in1", 4, 2), ("kin", 1, 2), ("vin", 1, 2), ("qst", 1, 0), ("rot", 4, 0),
                      ("kb", 1, 0), ("pool", 1, 0), ("att", 2, 0), ("out1", 4, 2)]
        order += [(f"n{1 + 3 * l}", 2, 0), (f"m{1 + 3 * l}", 2, 0)]
        for g, size in enumerate(FFN_GROUPS):
            order += [(f"up{l}{g}", size, 2), (f"down{l}{g}", 4, 2)]
        order += [(f"n{2 + 3 * l}", 2, 0)]
    order += [("outT", 4, 0)]
    unit, granule, u, n = {}, {}, 0, 0
    for name, units, granules in order:
        unit[name], granule[name] = u, n
        u += units
        n += units * granules
    return unit, granule, n


ADA_UP = (((12, 2, 0, 40, 1), (13, 2, 1, 0, 1)), ((24, 2, 1, 16, 2), (25, 2, 1, 18, 2)), ((34, 2, 1, 36, 2), (35, 2, 1, 38, 2)))
ADA_DOWN = (((20, 2, 1, 8, 2), (21, 2, 1, 10, 2)), ((32, 1, 1, 32, 1), None), (None, None))

ORDER = (4, 5, 0, 1, 2, 3)


def mlstm_steps():
    steps, e = [], 0
    for s in ORDER:
        if s < NL:
            of_tile = [(0, s * P, LAT), (1, 0, (s + 1) * P)]
        else:
            of_tile = [(0, 0, LAT), (0, s * P, T), (1, 0, LAT), (1, LAT, (s + 1) * P)]
        steps.append([(e + n, x) for n, x in enumerate(of_tile)])
        e += len(of_tile)
    return steps


STEPS = mlstm_steps()
TOUCHES = [[(q, d, t) for q in range(NT) for _, (d, t0, t1) in STEPS[q] for t in range(t0 // P, t1 // P)
            if (6 * d + t) // 3 == b] for b in range(4)]
FIRST_TOUCH = [x[0] for x in TOUCHES]
LAST_TOUCH = [x[-1] for x in TOUCHES]
ITEMS = [("X", h - 1, 0) if q == "X" else ("S", h, q) for h in range(HEADS) for q in (0, 1, 2, "X", 3, 4, 5)
         if q != "X" or h] + [("X", HEADS - 1, 0)]


def build(nc, a, out):
    U, G, N_GRANULES = plan()
    ctx = ExitStack()
    with ctx:
        used = {}

        def sem(name):
            if name not in used:
                used[name] = ctx.enter_context(nc.semaphore(name))
            return used[name]

        base = (nc.sbuf_base + 31) // 32 * 32
        top = nc.sbuf_usable_end
        at = [base]

        def place(name, shape, dt=F32, offset=None):
            size = int(np.prod(shape[1:])) * 4
            if offset is None:
                offset = at[0]
                at[0] += (size + 31) // 32 * 32
                assert at[0] <= top, (name, at[0] - top)
            assert offset + size <= top, name
            return nc.alloc_sbuf_tensor_at(name, shape, dt, offset=offset)

        xT = place("xT", [P, KD, T])
        H0 = at[0]
        h_hi = place("h_hi", [P, KD, T], F32R)
        h_lo = place("h_lo", [P, KD, T], F32R)
        raw = place("raw", [P, 2, 4, 256])
        W_HI = at[0]
        w_hi = place("w_hi", [P, 4, 4, 256], F32R)
        W_LO = at[0]
        w_lo = place("w_lo", [P, 4, 4, 256], F32R)
        ident = place("ident", [P, P])
        ones = place("ones", [P, P])
        vec0 = place("vec0", [P, 92])
        vec1 = place("vec1", [P, 84])
        ffn_cw = place("ffn_cw", [P, 2, 66])
        dw_w = place("dw_w", [P, TAPS, 4])
        mods = place("mods", [P, 2, 6, KD, 2])
        cond = place("cond", [P, KD, 2])
        st = place("st", [P, 2, NT])
        gate_b = place("gate_b", [P, 2])
        mark = place("mark", [P, 16])
        ADA = at[0]
        ada_w = place("ada_w", [P, 2, 4, 256])
        ada_acc = place("ada_acc", [P, 2, 256])
        A0 = at[0]
        ARENA = top // 32 * 32 - A0
        assert ARENA >= 84000, ARENA

        qkov = place("qkov", [P, 16, T], offset=A0)
        negM = place("negM", [P, 2, 2, T], offset=A0 + 8 * T * 4)
        sig_b = place("sig_b", [P, 4, T], offset=A0 + 8 * T * 4)
        v_tok = place("v_tok", [P, NT, HEADS, VW], offset=A0 + 49152)
        EP0 = A0 + 49152 + 12384
        probs = place("probs", [P, 4, LAT], offset=EP0)
        rows = place("rows", [P, 6, T], offset=A0 + 49152)
        ln_sq = place("ln_sq", [P, 2, T], offset=EP0)
        U0 = EP0 + 6144
        conv_u = place("conv_u", [P, 5, U_LEN], offset=U0)
        ln_diag = place("ln_diag", [P, T], offset=U0 + 4 * U_LEN * 4)
        h_tok = place("h_tok", [P, NT, P], offset=EP0 + 8192)
        merged = place("merged", [P, T], offset=EP0 + 11264)
        sq_junk = place("sq_junk", [P, NT, P], offset=EP0 + 14336)
        gcols = place("gcols", [P, 4, NT, 8], offset=ADA)
        den = place("den", [P, 2, 4, 3], offset=ADA + 1024)
        hss = place("hss", [P, 2, NT], offset=ADA + 1280)
        hid_hi = place("hid_hi", [P, 8, T], F32R, offset=A0)
        hid_lo = place("hid_lo", [P, 8, T], F32R, offset=A0 + 24576)
        tbuf = place("tbuf", [P, 2, T], offset=A0)
        y = place("y", [P, KD, T], offset=A0 + 49152)
        SCR = A0 + 73728
        gpad = place("gpad", [P, 2, G_LEN], offset=SCR)
        hid = place("hid", [P, 8, T], offset=A0 + 24576)
        sq = place("sq", [P, 2, T], offset=SCR)
        sumsq = place("sumsq", [P, T], offset=SCR + 6144)
        diag = place("diag", [P, T], offset=A0 + 8192)
        x_tok = place("x_tok", [P, NT, D], offset=H0)
        ada_0 = place("ada_0", [P, 8, KD, 2 * P], offset=A0)
        vrows = place("vrows", [P, 6, P], offset=W_LO + 3 * 4096)
        ada_acc_b = place("ada_acc_b", [P, 2, 256], offset=A0 + 12288)
        ada_acc0 = place("ada_acc0", [P, 8, 2, 256], offset=W_HI)
        inb = place("inb", [P, 8, LAT], offset=A0)
        kT = place("kT", [P, N_KV, T], offset=A0 + 16384)
        v1 = place("v1", [P, NT, N_KV * HD], offset=A0 + 22528)
        rope = place("rope", [P, 2, LAT], offset=A0 + 28672)
        rotw = place("rotw", [P, 3, P], offset=A0 + 32768)
        icnt = place("icnt", [P, 2, LAT], offset=A0 + 34304)
        poolw = place("poolw", [P, 2, P], offset=A0 + 38400)
        PW = LAT + 16
        pu = place("pu", [P, 2, PW], offset=A0 + 39424)
        ps2 = place("ps2", [P, 2, PW], offset=A0 + 43648)
        ps4 = place("ps4", [P, 2, PW], offset=A0 + 47872)
        asq = place("asq", [P, 2, T], offset=A0 + 52096)
        adiag = place("adiag", [P, 2, T], offset=A0 + 58240)
        rt1 = place("rt1", [P, 2, LAT], offset=A0 + 64384)
        ptile = place("ptile", [P, 2, T], offset=A0 + 68480)
        pT = place("pT", [P, 2, T], offset=A0 + 74624)
        acol = place("acol", [P, 36], offset=ADA)
        arow = place("arow", [P, 24, 4], offset=ADA + 256)
        o_tok = place("o_tok", [P, NL, D], offset=A0)

        acc = ctx.enter_context(nc.psum_tensor("acc", [P, 2, 2, 2 * 512], F32))
        m_dram = nc.dram_tensor("m_rows", (2, HEADS, T), F32, kind="Internal").ap()

        ada0_in = [sem(f"ada0_in{q}") for q in range(8)]
        ada0_sums = sem("ada0_sums")
        x_in = [sem("x_in0"), sem("x_in1")]
        raw_full = [sem("raw_full0"), sem("raw_full1")]
        high, low = sem("w_high"), sem("w_low")
        unit_done = sem("unit_done")
        set_free = [sem("set0_free"), sem("set1_free")]
        ada_full = [sem("ada_full0"), sem("ada_full1")]
        ada_used, ada_out = sem("ada_used"), sem("ada_out")
        h_ready, sq_ready, sq_used = sem("h_ready"), sem("sq_ready"), sem("sq_used")
        recip, root, diag_ready = sem("recip"), sem("root"), sem("diag_ready")
        x_new, t_ready, t_high = sem("x_new"), sem("t_ready"), sem("t_high")

        def psum_free(eng, u, i=0):
            eng.wait_ge(set_free[u % 2], u // 2 + 1 + i)

        def psum_full(eng, u, i=0):
            eng.wait_ge(unit_done, u + 1 + 2 * i)

        def psum_read(eng, u, i=0):
            eng.wait_ge(set_free[u % 2], u // 2 + 2 + i)

        def loaded(n, i=0):
            return 16 * (n // 2 + 1) + 32 * i

        w_even = a["even_w_in"][0].rearrange("(k p) n -> p k n", p=P)
        w_even_out = a["even_w_out"][0].rearrange("(k p) n -> p k n", p=P)
        w_odd = a["odd_w_in"][0].rearrange("(k p) n -> p k n", p=P)
        w_odd_out = a["odd_w_out"][0].rearrange("(k p) n -> p k n", p=P)
        w_ffn_in = [a["ffn_w_in"][l].rearrange("(k p) n -> p k n", p=P) for l in range(2)]
        w_ffn_out = [a["ffn_w_out"][l].rearrange("(k p) n -> p k n", p=P) for l in range(2)]
        w_ada = [a["ada_w"][l].rearrange("(k p) n -> p k n", p=P) for l in range(2)]
        SPLIT = {8: (4, 4), 6: (4, 2)}

        block = ctx.enter_context(nc.Block())

        def load(sp, n, src, i=0):
            sp.wait_ge(low, n + 3 + 4 * i)
            kt = src.shape[1]
            sp.dma_start(raw[:, n % 2, 0:kt, :], src).then_inc(raw_full[n % 2], 16)

        def load_unit(sp, n, w, col, k0=0, ktiles=KD, i=0):
            for part, kt in enumerate(SPLIT[ktiles]):
                k = k0 + 4 * part
                load(sp, n + part, w[:, k:k + kt, bass.ds(col, 256)], i)

        def load_ada(sp, pair, l, of_layer, i=0, per=2):
            for half in range(2):
                sp.wait_ge(ada_used, 2 * pair + half + 1 + 2 * per * i)
                sp.dma_start(ada_w[:, half], w_ada[l][:, 4 * half:4 * half + 4, bass.ds(of_layer * 256, 256)]
                             ).then_inc(ada_full[half], 16)

        BY_PE = (1, 4, 7)
        BY_DVE = [q for q in range(8) if q not in BY_PE]

        @block.sync
        def _(sp):
            sp.dma_start(ident[:, :], a["identity"]).then_inc(sem("ident_in"), 16)
            tile_rows = [0] * 5

            def vector_rows(block_, src):
                r = tile_rows[block_]
                n = src.shape[0]
                sp.dma_start(vrows[r:r + n, block_, :], src).then_inc(sem("vec_in"), 16)
                tile_rows[block_] = r + n

            def load_ada_0(first, end):
                for q in range(first, end):
                    sp.dma_start(ada_0[:, q], w_ada[0][:, :, q * 256:(q + 1) * 256]).then_inc(ada0_in[q], 16)

            def load_x(first, end):
                for j in range(first, end):
                    src = a["x"][0, j * P:(j + 1) * P] if j < NL else a["ctx"][0, (j - NL) * P:(j - NL + 1) * P]
                    sp.dma_start(x_tok[:, j, :], src).then_inc(x_in[j // 3], 16)

            for s, name in enumerate(("c", "c_ctx")):
                src = a["c"][0] if name == "c" else a["c_ctx"]
                sp.dma_start(vrows[KD * s:KD * (s + 1), 5, :], src.rearrange("(r p) -> r p", p=P)).then_inc(sem("cond_in"), 16)
            load_ada_0(0, 2)
            gains = ("mix_pre_g", "mix_post_g", "ffn_pre_g", "ffn_post_g")
            for l in range(2):
                vector_rows(l, a["ada_b"][l].rearrange("(r p) -> r p", p=P))
                for g in gains:
                    vector_rows(l, a[g][l].rearrange("(r p) -> r p", p=P))
            for g in ("conv_ln_g", "conv_ln_b", "mlstm_norm_g"):
                vector_rows(0, a[g][0].rearrange("(r p) -> r p", p=P))
            for g in ("pool_scale", "q_norm_g", "k_norm_g"):
                vector_rows(1, a[g][0].rearrange("(r p) -> r p", p=P))
            for l in range(2):
                vector_rows(2 + l, a["ffn_conv_w"][l].rearrange("w (j p) -> (w j) p", p=P))
            vector_rows(4, a["conv_dw_w"][0].rearrange("w (j p) -> (w j) p", p=P))
            load_x(0, NT)
            load_ada_0(2, 8)
            for q in range(4):
                sp.dma_start(gate_b[4 * (q // 2):4 * (q // 2) + 4, 1 - q % 2:2 - q % 2],
                             a["mlstm_gate_b"][0, q].rearrange("(h o) -> h o", o=1)).then_inc(sem("gate_b_in"), 16)
            for i in range(2):
                n = G["conv"] + 4 * i
                load_unit(sp, n, w_even, i * 256 + 512)
                if not i:
                    load_ada(sp, 0, 0, 8)
                    load_ada(sp, 1, 0, 9)
                load_unit(sp, n + 2, w_even, i * 256)
                if not i:
                    load_ada(sp, 2, 0, 10)
                    load_ada(sp, 3, 0, 11)
            for part in range(2):
                n = G["gate"] + part
                sp.wait_ge(low, n + 3)
                for q, (dst, src) in enumerate(((0, 4), (4, 12), (32, 0), (36, 8))):
                    if q == 3:
                        sp.wait_ge(sem("gate_parts"), 48 * (part + 1))
                    sp.dma_start(raw[:, n % 2, :, dst:dst + 4],
                                 w_even[:, 4 * part:4 * part + 4, GATE_COL + src:GATE_COL + src + 4]
                                 ).then_inc(raw_full[n % 2] if q == 3 else sem("gate_parts"), 16)
            with sp.Fori(0, 4) as i:
                for j in range(2):
                    load_unit(sp, G["qkov"] + 2 * j, w_even, i * 512 + (1024 + 256 * j), i=i)
            sp.wait_ge(sem("rows_ready"), 1)
            for d in range(2):
                sp.dma_start(m_dram[d], rows[4 * d:4 * d + 4, 1 + d, :]).then_inc(sem("m_out"), 16)
            n = G["out0"]
            load_unit(sp, n, w_even_out, 0)
            sp.wait_ge(sem("m_out"), 32)
            psum_read(sp, U["vt"] + 2)
            for h in range(HEADS):
                if h >= 2:
                    sp.wait_ge(sem("p_used"), 16 * (h - 1))
                sp.dma_start(negM[:, h % 2], m_dram[:, h, :].partition_broadcast(P)).then_inc(sem(f"m_in{h % 2}"), 16)
            sp.wait_ge(unit_done, U["out0"])
            for j in range(4):
                if j:
                    load_unit(sp, n + 2 * j, w_even_out, 256 * j)
                load_ada(sp, 4 + 2 * j, 0, 12 + 2 * j)
                load_ada(sp, 5 + 2 * j, 0, 13 + 2 * j)
            for l in range(2):
                if l:
                    w = w_odd
                    with sp.Fori(0, 2) as i:
                        for j in range(2):
                            load_unit(sp, G["in1"] + 2 * j, w, i * 512 + 256 * j, i=i)
                    sp.wait_ge(unit_done, U["n3"] + 2)
                    for dst, name in ((rope, "rope"), (icnt, "pool_count")):
                        sp.dma_start(dst[:, :, :], a[name].rearrange("a p t -> p a t")).then_inc(sem("tab_in"), 16)
                    sp.dma_start(rotw[:, 0, :], a["rotate"]).then_inc(sem("tab_in"), 16)
                    sp.wait_ge(sem("poolw_zero"), 1)
                    for g in range(4):
                        lo = 64 * (g % 2)
                        sp.dma_start(poolw[lo:lo + 64, g // 2, lo:lo + 64], a["pool_w"][0, g]).then_inc(sem("tab_in"), 16)
                    load_unit(sp, G["kin"], w, 1024)
                    load_unit(sp, G["vin"], w, 1280)
                    for j in range(4):
                        load_unit(sp, G["out1"] + 2 * j, w_odd_out, 256 * j)
                first = 0
                for g, size in enumerate(FFN_GROUPS):
                    n = G[f"up{l}{g}"]
                    with sp.Fori(0, size // 2) as i:
                        for j in range(2):
                            load_unit(sp, n + 2 * j, w_ffn_in[l], i * 256 + (first * P + j * D_FF), i=i)
                            if not l:
                                pair, per, layer, tiles, step = ADA_UP[g][j]
                                load_ada(sp, pair, layer, step * i + tiles // 2, i, per)
                    n = G[f"down{l}{g}"]
                    with sp.Fori(0, 2) as i:
                        for j in range(2):
                            load_unit(sp, n + 2 * j, w_ffn_out[l], i * 512 + 256 * j, first, size, i)
                            if not l and ADA_DOWN[g][j]:
                                pair, per, layer, tiles, step = ADA_DOWN[g][j]
                                load_ada(sp, pair, layer, step * i + tiles // 2, i, per)
                    first += size
            for j in range(NL):
                sp.wait_ge(sem("o_ready"), j + 1)
                sp.dma_start(out[0, j * P:(j + 1) * P], o_tok[:, j, :]).then_inc(sem("out_done"), 16)
            sp.wait_ge(sem("out_done"), 16 * NL)

        def product(pe, u, n, rhs, ready, ktiles=KD, segs=SEGS[T], i=0, ada=None, pairs=1, halves=(0, 1)):
            s = u % 2
            psum_free(pe, u, i)
            k = 0
            for part, kt in enumerate(SPLIT[ktiles]):
                slot = (n + part) % 4
                pe.wait_ge(low, n + part + 5 + 4 * i)
                for kk in range(kt):
                    ready(k)
                    for m in halves:
                        c = slice(m * P, (m + 1) * P)
                        for q, (w, x) in enumerate(((w_hi, rhs[0]), (w_hi, rhs[1]), (w_lo, rhs[0]))):
                            for t0, t1 in segs:
                                last = nc.tensor.matmul(acc[:, s, m, t0:t1], w[:, slot, kk, c], x[:, k, t0:t1],
                                                        start=(k == 0 and q == 0), stop=(k == ktiles - 1 and q == 2))
                    k += 1
            if ada:
                pair, per = ada[:2]
                for x in range(pairs):
                    pe.wait_ge(ada_used, 2 * (pair + x) + 4 + 2 * per * i)
                    for q in range(2):
                        for c in range(2):
                            at_ = 1008 + 4 * x + 2 * q + c
                            last = nc.tensor.matmul(acc[:, s, 0, at_:at_ + 1], (ada_acc, ada_acc_b)[x][:, c, q * P:(q + 1) * P],
                                                    ones[:, 0:1], start=True, stop=True)
            last.then_inc(unit_done, 1)

        @block.tensor
        def _(pe):
            def always(k):
                pass

            def h_tiles(stage):
                return lambda k: pe.wait_ge(h_ready, KD * stage + k + 1)

            def transpose(dst, src, rows_=P):
                return nc.tensor.transpose(dst, src, ident[0:rows_, 0:rows_])

            def column_sums(u, sources, tiles, wait, after):
                s = u % 2
                psum_free(pe, u)
                for m, src in enumerate(sources):
                    wait(m)
                    for j in range(tiles):
                        last = nc.tensor.matmul(acc[:, s, 0, j:j + 1], src(j), ones[:, 0:1],
                                                start=(m == 0 and j == 0),
                                                stop=(m == len(sources) - 1 and j == tiles - 1), skip_group_check=True)
                    if after is not None and m < len(sources) - 1:
                        last.then_inc(after, 1)
                last.then_inc(unit_done, 1)

            def spread(u, diagonal, tokens, count):
                psum_free(pe, u)
                pe.wait_ge(diag_ready, count)
                for t0, t1 in SEGS[tokens]:
                    last = nc.tensor.matmul(acc[:, u % 2, 0, t0:t1], ones[:, :], diagonal[:, t0:t1], start=True, stop=True)
                last.then_inc(unit_done, 1)

            def norm_x(u, first_sq, tokens, diag_count):
                column_sums(u, [(lambda j, m=m: sq[:, m % 2, j * P:(j + 1) * P]) for m in range(KD)], tokens // P,
                            lambda m: pe.wait_ge(sq_ready, first_sq + m + 1), sq_used)
                spread(u + 1, diag, tokens, diag_count)

            def norm_y(u, sums, tokens, diag_count):
                column_sums(u, [lambda j: sumsq[:, j * P:(j + 1) * P]], tokens // P,
                            lambda m: pe.wait_ge(sem("ysq_used"), KD * sums), None)
                spread(u + 1, diag, tokens, diag_count)

            pe.wait_ge(sem("ident_in"), 16)
            pe.wait_ge(sem("cond_in"), 32)
            psum_free(pe, U["cond"])
            transpose(acc[:, U["cond"] % 2, 0, 0:2 * KD], vrows[0:2 * KD, 5, :], 2 * KD).then_inc(unit_done, 1)
            pe.wait_ge(sem("vec_in"), 16 * N_VECTORS)
            pe.wait_ge(sem("ones_set"), 1)
            psum_free(pe, U["vec"])
            for b, (n, m, col) in enumerate(((92, 0, 0), (84, 0, 128), (66, 0, 256), (66, 0, 384), (124, 1, 0))):
                last = transpose(acc[:, U["vec"] % 2, m, col:col + n], vrows[0:n, b, :], n)
            last.then_inc(unit_done, 1)
            for q in range(2):
                pe.wait_ge(x_in[q], 16 * 3)
            for v in range(4):
                u = U["xt"] + v
                psum_free(pe, u)
                for m in range(2):
                    for j in range(NT):
                        last = transpose(acc[:, u % 2, m, j * P:(j + 1) * P],
                                         x_tok[:, j, (2 * v + m) * P:(2 * v + m + 1) * P])
                last.then_inc(unit_done, 1)
            u = U["ada"]
            psum_free(pe, u)
            psum_read(pe, U["cond"])
            for q in range(8):
                if q in BY_PE:
                    pe.wait_ge(ada0_in[q], 16)
                    for m in (0, 1):
                        for k in range(KD):
                            nc.tensor.matmul(acc[:, u % 2, 0, 4 * q + 2 * m:4 * q + 2 * m + 2],
                                             ada_0[:, q, k, m * P:(m + 1) * P], cond[:, k, :], start=(k == 0), stop=(k == KD - 1))
            for q in BY_DVE:
                pe.wait_ge(ada0_sums, BY_DVE.index(q) + 1)
                for m in (2 * q, 2 * q + 1):
                    for c in range(2):
                        last = nc.tensor.matmul(acc[:, u % 2, 0, 2 * m + c:2 * m + c + 1],
                                                ada_acc0[:, q, c, (m % 2) * P:(m % 2 + 1) * P], ones[:, 0:1],
                                                start=True, stop=True)
            last.then_inc(unit_done, 1)
            norm_x(U["n0"], 0, T, 1)
            h = (h_hi, h_lo)
            for j in range(4):
                product(pe, U["conv"] + j, G["conv"] + 2 * j, h, always if j else h_tiles(0), ada=(2 * j, 0) if j < 2 else None,
                        pairs=2)
            product(pe, U["gate"], G["gate"], h, always, halves=(0,))
            with pe.Fori(0, 4) as i:
                for j in range(2):
                    product(pe, U["qkov"] + j, G["qkov"] + 2 * j, h, always, i=i)
            u = U["gcol"]
            psum_free(pe, u)
            pe.wait_ge(sem("rows_ready"), 1)
            for x_, row in enumerate((5, 0, 3, 4)):
                for j in range(NT):
                    c = (x_ * NT + j) * 8
                    last = transpose(acc[:, u % 2, 0, c:c + 8], rows[0:8, row, j * P:(j + 1) * P], 8)
            last.then_inc(unit_done, 1)
            for v in range(3):
                u = U["vt"] + v
                psum_free(pe, u)
                for m in range(2):
                    j = 2 * v + m
                    for hd in range(HEADS):
                        last = transpose(acc[:, u % 2, m, hd * P:(hd + 1) * P], qkov[:, 8 + hd, j * P:(j + 1) * P])
                last.then_inc(unit_done, 1)
            def conv_cols(tile):
                return lambda j: conv_u[:, tile, (HALF + j * P if j < NL else U_CTX + (j - NL) * P):
                                        (HALF + j * P if j < NL else U_CTX + (j - NL) * P) + P]

            u = U["ln"]
            column_sums(u, [conv_cols(t) for t in range(4)], NT, lambda m: pe.wait_ge(sem("conv_done"), 1), None)
            spread(u + 1, ln_diag, T, 2)
            column_sums(u + 2, [(lambda j, m=m: ln_sq[:, m % 2, j * P:(j + 1) * P]) for m in range(4)], NT,
                        lambda m: pe.wait_ge(sem("ln_sq_ready"), m + 1), sem("ln_sq_used"))
            spread(u + 3, ln_diag, T, 3)
            u = U["mlstm"]
            psum_free(pe, u)
            psum_free(pe, u + 1)
            psum_read(pe, U["vt"] + 2)
            pe.wait_ge(sem("v_ones"), 1)

            def weigh(hd, q):
                for e, (d, t0, t1) in STEPS[q]:
                    pe.wait_ge(sem("p_ready"), 16 * hd + e + 1)
                    for t in range(t0 // P, t1 // P):
                        b, c = divmod(6 * d + t, 3)
                        dst = acc[:, 0, b // 2, (b % 2) * 512 + c * VW:(b % 2) * 512 + (c + 1) * VW]
                        last = nc.tensor.matmul(dst, probs[:, e % 4, t * P - t0:t * P - t0 + P], v_tok[:, ORDER[q], hd, :],
                                                start=(q, d, t) == FIRST_TOUCH[b], stop=(q, d, t) == LAST_TOUCH[b],
                                                skip_group_check=True)
                    last.then_inc(sem("p_used"), 1)

            pending = None
            pe.wait_ge(sem("qkov_ready"), 1)
            for z, (kind, hd, q) in enumerate(ITEMS):
                if kind == "X" and pending:
                    weigh(*pending)
                    pending = None
                if z >= 2:
                    was, of, q_ = ITEMS[z - 2]
                    if was == "S":
                        pe.wait_ge(sem("p_ready"), 16 * of + STEPS[q_][-1][0] + 1)
                    else:
                        pe.wait_ge(sem("merged_ready"), of + 1)
                if kind == "S":
                    for t0, t1 in (SEGS[T] if ORDER[q] >= NL else SEGS[LAT]):
                        last = nc.tensor.matmul(acc[:, 1, z % 2, t0:t1], qkov[:, 4 + hd, ORDER[q] * P:(ORDER[q] + 1) * P],
                                                qkov[:, hd, t0:t1], start=True, stop=True)
                else:
                    pe.wait_ge(sem("hn_ready"), hd + 1)
                    for j in range(NT):
                        last = transpose(acc[:, 1, z % 2, j * P:(j + 1) * P], h_tok[:, j, :])
                if z < len(ITEMS) - 1:
                    last.then_inc(sem("slot_full"), 1)
                if pending:
                    if pending[1] == 0 and hd:
                        pe.wait_ge(sem("sums_read"), hd)
                    weigh(*pending)
                pending = (hd, q) if kind == "S" else None
            last.then_inc(unit_done, 2)

            def ffn_and_norms(l, tokens, diag_count, sums, first_sq, stage, hid0):
                norm_y(U[f"n{1 + 3 * l}"], sums, tokens, diag_count)
                norm_x(U[f"m{1 + 3 * l}"], first_sq, tokens, diag_count + 1)
                segs = SEGS[tokens]
                for g, size in enumerate(FFN_GROUPS):
                    with pe.Fori(0, size // 2) as i:
                        for j in range(2):
                            product(pe, U[f"up{l}{g}"] + j, G[f"up{l}{g}"] + 2 * j, h, always if g else h_tiles(stage),
                                    segs=segs, i=i, ada=None if l else ADA_UP[g][j])
                    with pe.Fori(0, 2) as i:
                        for j in range(2):
                            product(pe, U[f"down{l}{g}"] + j, G[f"down{l}{g}"] + 2 * j, (hid_hi, hid_lo),
                                    lambda k: pe.wait_ge(sem("hid_ready"), hid0 + k // 2 + 1), ktiles=size, segs=segs, i=i,
                                    ada=None if l else ADA_DOWN[g][j])
                    hid0 += size // 2
                norm_y(U[f"n{2 + 3 * l}"], sums + 1, tokens, diag_count + 2)

            for j in range(4):
                product(pe, U["out0"] + j, G["out0"] + 2 * j, h, h_tiles(1), ada=(4 + 2 * j, 0), pairs=2)
            ffn_and_norms(0, T, 4, 1, 8, 2, 0)
            norm_x(U["n3"], 16, T, 7)
            with pe.Fori(0, 2) as i:
                for j in range(2):
                    product(pe, U["in1"] + j, G["in1"] + 2 * j, h, h_tiles(3), segs=SEGS[LAT], i=i)
            product(pe, U["kin"], G["kin"], h, always)
            u, n = U["vin"], G["vin"]
            psum_free(pe, u)
            pe.wait_ge(low, n + 6)
            for j in range(NT):
                c = slice((j % 4) * 256, (j % 4) * 256 + 256)
                for k in range(KD):
                    slot = (n + k // 4) % 4
                    for q, (w, x) in enumerate(((w_hi, h_hi), (w_hi, h_lo), (w_lo, h_hi))):
                        last = nc.tensor.matmul(acc[:, u % 2, j // 4, c], x[:, k, j * P:(j + 1) * P], w[:, slot, k % 4, :],
                                                start=(k == 0 and q == 0), stop=(k == KD - 1 and q == 2))
            last.then_inc(unit_done, 1)
            u = U["qst"]
            psum_free(pe, u)
            for m in range(8):
                pe.wait_ge(sem("asq_ready"), m + 1)
                tiles, first = (NL, NL * m) if m < N_Q else (NT, NL * N_Q + NT * (m - N_Q))
                for j in range(tiles):
                    last = nc.tensor.matmul(acc[:, u % 2, 0, first + j:first + j + 1], asq[:, m % 2, j * P:(j + 1) * P],
                                            ones[:, 0:1], start=True, stop=True)
                last.then_inc(sem("asq_used") if m < 7 else unit_done, 1)
            pe.wait_ge(sem("rotw_ready"), 2)
            for v in range(4):
                u = U["rot"] + v
                psum_free(pe, u)
                for m in range(2):
                    x_ = inb[:, 2 + 2 * v + m, :] if v < 3 else kT[:, m, 0:LAT]
                    last = nc.tensor.matmul(acc[:, u % 2, m, 0:LAT], rotw[:, 1 + v // 3, :], x_, start=True, stop=True)
                last.then_inc(unit_done, 1)
            u = U["kb"]
            psum_free(pe, u)
            pe.wait_ge(sem("kdiag_ready"), 1)
            for m in range(2):
                for t0, t1 in SEGS[T]:
                    last = nc.tensor.matmul(acc[:, u % 2, m, t0:t1], ones[:, :], adiag[:, m, t0:t1], start=True, stop=True)
            last.then_inc(unit_done, 1)
            u = U["pool"]
            psum_free(pe, u)
            pe.wait_ge(sem("pooled"), 1)
            for m in range(2):
                last = nc.tensor.matmul(acc[:, u % 2, m, 0:LAT], poolw[:, m, :], pu[:, m, 8:8 + LAT], start=True, stop=True)
            last.then_inc(unit_done, 1)
            u = U["att"]
            psum_free(pe, u)
            psum_free(pe, u + 1)
            pe.wait_ge(sem("qk_ready"), 1)

            def scores(n):
                hd, i = divmod(n, NL)
                if n >= 2:
                    pe.wait_ge(sem("score_exp"), n - 1)
                for t0, t1 in SEGS[T]:
                    last = nc.tensor.matmul(acc[:, 0, n % 2, t0:t1], inb[:, 2 + hd, i * P:(i + 1) * P],
                                            kT[:, hd // 3, t0:t1], start=True, stop=True)
                last.then_inc(sem("score_full"), 1)

            scores(0)
            scores(1)
            for n in range(N_Q * NL):
                hd, i = divmod(n, NL)
                pe.wait_ge(sem("pn_ready"), n + 1)
                if n >= 1:
                    pe.wait_ge(sem("pT_ready"), n)
                for j in range(NT):
                    last = transpose(acc[:, 1, 0, j * P:(j + 1) * P], ptile[:, n % 2, j * P:(j + 1) * P])
                last.then_inc(sem("pT_full"), 1)
                if n + 2 < N_Q * NL:
                    scores(n + 2)
                pe.wait_ge(sem("pT_ready"), n + 1)
                if hd >= 2 and i == 0:
                    pe.wait_ge(h_ready, KD * 4 + 2 + hd - 1)
                c = (hd % 2) * 512 + i * P
                for j in range(NT):
                    last = nc.tensor.matmul(acc[:, 1, 1, c:c + P], v1[:, j, (hd // 3) * HD:(hd // 3 + 1) * HD],
                                            pT[:, n % 2, j * P:(j + 1) * P], start=(j == 0), stop=(j == NT - 1))
                if n < N_Q * NL - 1:
                    last.then_inc(sem("pv_done"), 1)
            last.then_inc(unit_done, 2)
            for j in range(4):
                product(pe, U["out1"] + j, G["out1"] + 2 * j, h, h_tiles(4), segs=SEGS[LAT])
            ffn_and_norms(1, LAT, 8, 3, 24, 5, FT // 2)
            pe.wait_ge(x_new, 4 * KD)
            for v in range(4):
                u = U["outT"] + v
                if v < 2:
                    psum_free(pe, u)
                else:
                    pe.wait_ge(sem("o_ready"), v - 1)
                for k in range(KD):
                    last = transpose(acc[:, u % 2, k // 4, (k % 4) * P:(k % 4 + 1) * P], xT[:, k, v * P:(v + 1) * P])
                last.then_inc(unit_done, 1)

        @block.scalar
        def _(act):
            sa = Steps(act, sem("act_step"))
            mods_flat = mods[:, :, :, :, :].rearrange("p l c k s -> p l (c k) s")

            def take_high(n, i=0):
                act.wait_ge(raw_full[n % 2], loaded(n, i))
                nc.scalar.activation(w_hi[:, n % 4], raw[:, n % 2], ACT.Copy).then_inc(high, 1)

            def next_high(u, n, i=0):
                if n + 2 < N_GRANULES:
                    act.wait_ge(unit_done, u + 2 * i)
                    take_high(n + 2, i)
                    take_high(n + 3, i)

            def take_ada(u, l, tile, i=0, per=4, tiles=2):
                vec = vec1 if l else vec0
                for q in range(tiles):
                    t = tile + q + per * i
                    last = nc.scalar.activation(mods_flat[:, l, bass.ds(t, 1), :],
                                                acc[:, u % 2, 0, 1008 + 2 * q:1010 + 2 * q].unsqueeze(1), ACT.Identity,
                                                bias=vec[:, bass.ds(t, 1)])
                last.then_inc(ada_out, 1)

            def square_x(first_new, norm, tokens):
                for m in range(KD):
                    if first_new is None:
                        psum_read(act, U["xt"] + m // 2)
                    else:
                        act.wait_ge(x_new, first_new + m + 1)
                    if m >= 2:
                        act.wait_ge(sq_used, 7 * norm + m - 1)
                    nc.scalar.activation(sq[:, m % 2, 0:tokens], xT[:, m, 0:tokens], ACT.Square).then_inc(sq_ready, 1)

            def square_y(u, first, tokens):
                psum_read(act, u)
                for m in (first, first + 1):
                    if m >= 2:
                        act.wait_ge(sem("ysq_used"), m - 1)
                    nc.scalar.activation(sq[:, m % 2, 0:tokens], y[:, m % KD, 0:tokens], ACT.Square
                                         ).then_inc(sem("ysq_ready"), 1)

            def roots(idx, nt):
                act.wait_ge(recip, idx)
                nc.scalar.activation(st[:, 1, 0:nt], st[:, 0, 0:nt], ACT.Sqrt).then_inc(root, 1)

            def modulate(use, l, comp, tokens):
                for m in range(KD):
                    act.wait_ge(t_ready, KD * use + m + 1)
                    for s, (t0, t1) in enumerate(SEGS[tokens]):
                        last = nc.scalar.activation(tbuf[:, m % 2, t0:t1], tbuf[:, m % 2, t0:t1], ACT.Identity,
                                                    bias=mods[:, l, comp, m, s:s + 1], scale=mods[:, l, comp + 1, m, s:s + 1])
                    sa.done(last)
                    sa.wait()
                    nc.scalar.activation(h_hi[:, m, 0:tokens], tbuf[:, m % 2, 0:tokens], ACT.Copy).then_inc(t_high, 1)

            psum_full(act, U["cond"])
            nc.scalar.activation(cond[:, :, :].rearrange("p k s -> p s k"),
                                 acc[:, U["cond"] % 2, 0, 0:2 * KD].rearrange("p (s k) -> p s k", s=2), ACT.Silu
                                 ).then_inc(set_free[U["cond"] % 2], 1)
            psum_full(act, U["vec"])
            for dst, m, col, n in ((vec0[:, :], 0, 0, 92), (vec1[:, :], 0, 128, 84), (ffn_cw[:, 0, :], 0, 256, 66),
                                   (ffn_cw[:, 1, :], 0, 384, 66),
                                   (dw_w[:, :, :].rearrange("p w j -> p (w j)"), 1, 0, 124)):
                last = nc.scalar.activation(dst, acc[:, U["vec"] % 2, m, col:col + n], ACT.Copy)
            last.then_inc(set_free[U["vec"] % 2], 1)
            for v in range(4):
                u = U["xt"] + v
                psum_full(act, u)
                nc.scalar.activation(xT[:, 2 * v:2 * v + 2, :], acc[:, u % 2, :, 0:T], ACT.Copy).then_inc(set_free[u % 2], 1)
            square_x(None, 0, T)
            roots(1, NT)
            modulate(0, 0, 0, T)
            take_high(0)
            take_high(1)
            act.wait_ge(sem("conv_zero"), 1)
            for i in range(2):
                u, n = U["conv"] + 2 * i, G["conv"] + 4 * i
                next_high(u, n)
                psum_full(act, u)
                if not i:
                    take_ada(u, 0, 16, tiles=4)
                nc.scalar.activation(sig_b[:, 2 * i:2 * i + 2, :], acc[:, u % 2, :, 0:T], ACT.Sigmoid
                                     ).then_inc(set_free[u % 2], 1)
                u, n = u + 1, n + 2
                next_high(u, n)
                psum_full(act, u)
                if not i:
                    take_ada(u, 0, 20, tiles=4)
                for (t0, t1), c in zip(SEGS[T], (U_LAT, U_CTX)):
                    last = nc.scalar.activation(conv_u[:, 2 * i + 1:2 * i + 3, c:c + t1 - t0], acc[:, u % 2, :, t0:t1],
                                                ACT.Copy)
                last.then_inc(set_free[u % 2], 1)
            u = U["gate"]
            next_high(u, G["gate"])
            psum_full(act, u)
            act.wait_ge(sem("gate_b_in"), 64)
            nc.scalar.activation(rows[0:8, 2, :], acc[32:40, u % 2, 0, 0:T], ACT.Copy)
            nc.scalar.activation(rows[0:8, 0, :], acc[0:8, u % 2, 0, 0:T], ACT.Identity, bias=gate_b[0:8, 0:1]
                                 ).then_inc(set_free[u % 2], 1)
            psum_read(act, u)
            sa.done(nc.scalar.activation(rows[0:8, 1, :], rows[0:8, 0, :], ACT.Abs))
            sa.wait()
            sa.done(nc.scalar.activation(rows[0:8, 1, :], rows[0:8, 1, :], ACT.Exp, scale=-1.0))
            sa.wait()
            nc.scalar.activation(rows[0:8, 1, :], rows[0:8, 1, :], ACT.Ln, bias=1.0).then_inc(sem("gate_log"), 1)
            act.wait_ge(sem("sig_used"), 2)
            with act.Fori(0, 4) as i:
                for j in range(2):
                    u, n = U["qkov"] + j, G["qkov"] + 2 * j
                    next_high(u, n, i)
                    psum_full(act, u, i)
                    nc.scalar.activation(qkov[:, bass.ds(4 * i + 2 * j, 2), :], acc[:, u % 2, :, 0:T], ACT.Copy
                                         ).then_inc(set_free[u % 2], 1)
            psum_read(act, U["qkov"] + 7)
            nc.scalar.activation(qkov[:, 12:16, :], qkov[:, 12:16, :], ACT.Sigmoid).then_inc(sem("qkov_ready"), 1)
            u = U["gcol"]
            psum_full(act, u)
            nc.scalar.activation(gcols[:, 0:2].rearrange("p x j r -> p (x j r)"), acc[:, u % 2, 0, 0:96], ACT.Copy)
            nc.scalar.activation(gcols[:, 2:4].rearrange("p x j r -> p (x j r)"), acc[:, u % 2, 0, 96:192], ACT.Exp,
                                 scale=-1.0).then_inc(set_free[u % 2], 1)
            act.wait_ge(sem("m_out"), 32)
            for v in range(3):
                u = U["vt"] + v
                psum_full(act, u)
                for m in range(2):
                    last = nc.scalar.activation(v_tok[:, 2 * v + m, :, 0:HD],
                                                acc[:, u % 2, m, 0:512].rearrange("p (h d) -> p h d", h=HEADS), ACT.Copy)
                last.then_inc(set_free[u % 2], 1)
            conv_segs = tuple(zip(SEGS[T], (HALF, U_CTX)))
            for t in range(4):
                act.wait_ge(sem("conv_centred"), t + 1)
                if t >= 2:
                    act.wait_ge(sem("ln_sq_used"), t - 1)
                for (t0, t1), c in conv_segs:
                    last = nc.scalar.activation(ln_sq[:, t % 2, t0:t1], conv_u[:, t, c:c + t1 - t0], ACT.Square)
                last.then_inc(sem("ln_sq_ready"), 1)
            roots(2, NT)
            for t in range(4):
                act.wait_ge(sem("conv_normed"), t + 1)
                for (t0, t1), c in conv_segs:
                    last = nc.scalar.activation(conv_u[:, t, c:c + t1 - t0], conv_u[:, t, c:c + t1 - t0], ACT.Silu,
                                                bias=vec0[:, 84 + t:85 + t], scale=vec0[:, 80 + t:81 + t])
                sa.done(last)
                sa.wait()
                for (t0, t1), c in conv_segs:
                    last = nc.scalar.activation(h_hi[:, t, t0:t1], conv_u[:, t, c:c + t1 - t0], ACT.Copy)
                last.then_inc(sem("mix_high"), 1)

            def finish(hd):
                act.wait_ge(sem("sums_read"), hd + 1)
                for j in range(NT):
                    if hd and not j:
                        act.wait_ge(sem("hss_ready"), hd)
                    last = nc.scalar.activation(sq_junk[:, j, :], h_tok[:, j, :], ACT.Square, accum_out=hss[:, 0, j:j + 1])
                last.then_inc(sem("hss_ready"), 1)
                act.wait_ge(sem("hss_recip"), hd + 1)
                nc.scalar.activation(hss[:, 1, :], hss[:, 1, :], ACT.Sqrt).then_inc(sem("hss_root"), 1)

            for kind, hd, q in ITEMS:
                if kind == "S":
                    if q == 0:
                        act.wait_ge(sem(f"m_in{hd % 2}"), 16 * (hd // 2 + 1))
                    for e, (d, t0, t1) in STEPS[q]:
                        if 16 * hd + e == 3:
                            act.wait_ge(h_ready, KD + 4)
                        if 16 * hd + e >= 4:
                            act.wait_ge(sem("p_used"), 16 * hd + e - 3)
                        nc.scalar.activation(probs[:, e % 4, 0:t1 - t0], negM[:, hd % 2, d, t0:t1], ACT.Exp,
                                             bias=gcols[:, d, ORDER[q], hd + 4 * d:hd + 4 * d + 1]).then_inc(sem("e_ready"), 1)
                    if q == 0 and hd:
                        finish(hd - 1)
                    if q == 5:
                        act.wait_ge(sem("p_used"), 16 * (hd + 1))
                        nc.scalar.activation(den[:, 0], acc[:, 0].rearrange("p m (b c) -> p (m b) c", b=2)[:, :, HD:3 * VW:VW],
                                             ACT.Abs).then_inc(sem("den_abs"), 1)
                        if hd == HEADS - 1:
                            finish(hd)
                else:
                    act.wait_ge(sem("merged_ready"), hd + 1)
                    nc.scalar.activation(h_hi[:, 4 + hd, :], merged[:, :], ACT.Copy).then_inc(sem("mix_high"), 1)

            def take_up(u, g, j, i):
                layer, tile, step = ADA_UP[g][j][2:]
                take_ada(u, layer, tile, i, 2 * step)

            def ffn(l, norm_y, norm, tokens, idx):
                segs = SEGS[tokens]
                nt = tokens // P
                roots(idx, nt)
                square_x(16 * l, norm, tokens)
                roots(idx + 1, nt)
                modulate(1 + 2 * l, l, 3, tokens)
                first_pair = FT // 2 * l
                act.wait_ge(sem("pads_zero"), l + 1)
                for g, size in enumerate(FFN_GROUPS):
                    with act.Fori(0, size // 2) as i:
                        u, n = U[f"up{l}{g}"], G[f"up{l}{g}"]
                        next_high(u, n, i)
                        psum_full(act, u, i)
                        act.wait_ge(sem("ffn_conv"), first_pair + 1 + i)
                        if not l:
                            take_up(u, g, 0, i)
                        for (t0, t1), c in zip(segs, (G_LAT, G_CTX)):
                            last = nc.scalar.activation(gpad[:, :, c:c + t1 - t0], acc[:, u % 2, :, t0:t1], ACT.Copy)
                        last.then_inc(set_free[u % 2], 1)
                        u, n = u + 1, n + 2
                        next_high(u, n, i)
                        act.wait_ge(sem("ffn_conv"), first_pair + 2 + i)
                        k = bass.ds(2 * i, 2)
                        nc.scalar.activation(hid[:, k, 0:tokens], hid[:, k, 0:tokens], ACT.Silu).then_inc(sem("ffn_silu"), 1)
                        if not l:
                            psum_full(act, u, i)
                            take_up(u, g, 1, i)
                        psum_read(act, u, i)
                        nc.scalar.activation(hid_hi[:, k, 0:tokens], hid[:, k, 0:tokens], ACT.Copy
                                             ).then_inc(sem("hid_high"), 1)
                    first_pair += size // 2
                    last_group = g == len(FFN_GROUPS) - 1

                    def down(j, i=0):
                        u, n = U[f"down{l}{g}"] + j, G[f"down{l}{g}"] + 2 * j
                        next_high(u, n, i)
                        if not l and ADA_DOWN[g][j % 2]:
                            psum_full(act, u, i)
                            layer, tile, step = ADA_DOWN[g][j % 2][2:]
                            take_ada(u, layer, tile, i, 2 * step)
                        return u

                    if last_group:
                        for j in range(4):
                            u = down(j)
                            square_y(u, KD * norm_y + 2 * j, tokens)
                    else:
                        with act.Fori(0, 2) as i:
                            for j in range(2):
                                down(j, i)
                roots(idx + 2, nt)

            def mixer_out(l, norm_y, tokens):
                for j in range(4):
                    u, n = U[f"out{l}"] + j, G[f"out{l}"] + 2 * j
                    next_high(u, n)
                    if not l:
                        psum_full(act, u)
                        take_ada(u, 0, 24 + 4 * j, tiles=4)
                    square_y(u, KD * norm_y + 2 * j, tokens)

            mixer_out(0, 0, T)
            ffn(0, 1, 1, T, 3)
            square_x(8, 2, T)
            roots(6, NT)
            modulate(2, 1, 0, T)
            with act.Fori(0, 2) as i:
                for j in range(2):
                    u, n = U["in1"] + j, G["in1"] + 2 * j
                    next_high(u, n, i)
                    psum_full(act, u, i)
                    nc.scalar.activation(inb[:, bass.ds(4 * i + 2 * j, 2), :], acc[:, u % 2, :, 0:LAT], ACT.Copy
                                         ).then_inc(set_free[u % 2], 1)
            u = U["kin"]
            next_high(u, G["kin"])
            psum_full(act, u)
            nc.scalar.activation(kT[:, :, :], acc[:, u % 2, :, 0:T], ACT.Copy).then_inc(set_free[u % 2], 1)
            u = U["vin"]
            next_high(u, G["vin"])
            psum_full(act, u)
            nc.scalar.activation(v1[:, 0:4, :], acc[:, u % 2, 0, :].rearrange("p (j c) -> p j c", c=256), ACT.Copy)
            nc.scalar.activation(v1[:, 4:6, :], acc[:, u % 2, 1, 0:512].rearrange("p (j c) -> p j c", c=256), ACT.Copy
                                 ).then_inc(set_free[u % 2], 1)
            psum_read(act, U["vin"])
            for m in range(8):
                if m >= 2:
                    act.wait_ge(sem("asq_used"), m - 1)
                src, tokens = (inb[:, 2 + m, :], LAT) if m < N_Q else (kT[:, m - N_Q, :], T)
                nc.scalar.activation(asq[:, m % 2, 0:tokens], src, ACT.Square).then_inc(sem("asq_ready"), 1)
            act.wait_ge(sem("tab_in"), 16 * 7)
            for q in range(2):
                nc.scalar.activation(rotw[:, 1 + q, :], rotw[:, 0, :], ACT.Copy, scale=vec1[:, 82 + q:83 + q]
                                     ).then_inc(sem("rotw_ready"), 1)
            act.wait_ge(recip, 7)
            nc.scalar.activation(acol[:, :], acol[:, :], ACT.Sqrt).then_inc(root, 1)
            act.wait_ge(sem("pool_float"), 1)
            nc.scalar.activation(h_hi[:, 0:2, 0:LAT], rt1[:, :, :], ACT.Copy).then_inc(sem("pool_high"), 1)

            def head_high(hd):
                if hd < N_Q - 1:
                    act.wait_ge(sem("pv_done"), NL * (hd + 1))
                else:
                    psum_full(act, U["att"] + 1)
                c = (hd % 2) * 512
                nc.scalar.activation(h_hi[:, 2 + hd, 0:LAT], acc[:, 1, 1, c:c + 512], ACT.Copy).then_inc(sem("o_high"), 1)

            for n in range(N_Q * NL):
                hd, i_ = divmod(n, NL)
                act.wait_ge(sem("score_max"), n + 1)
                if n >= 2:
                    act.wait_ge(sem("pT_full"), n - 1)
                nc.scalar.activation(ptile[:, n % 2, :], acc[:, 0, n % 2, 0:T], ACT.Exp, bias=arow[:, n, 1:2],
                                     scale=acol[:, n:n + 1], accum_out=arow[:, n, 2:3]).then_inc(sem("score_exp"), 1)
                if i_ == 1 and hd:
                    head_high(hd - 1)
            head_high(N_Q - 1)
            mixer_out(1, 2, LAT)
            ffn(1, 3, 3, LAT, 8)
            for v in range(4):
                u = U["outT"] + v
                psum_full(act, u)
                nc.scalar.activation(o_tok[:, v, :].rearrange("p (m c) -> p m c", m=2), acc[:, u % 2, :, 0:512], ACT.Copy
                                     ).then_inc(sem("o_ready"), 1)

        @block.vector
        def _(dve):
            sd = Steps(dve, sem("dve_step"))
            mods_flat = mods[:, :, :, :, :].rearrange("p l c k s -> p l (c k) s")

            def vt(out_, in0, in1, op):
                return nc.vector.tensor_tensor(out_, in0, in1, op)

            def row_sums(w, dst, ready, signals):
                for k in range(KD):
                    if ready:
                        ready(k)
                    for c in range(2):
                        scale = cond[:, k, c:c + 1]
                        if not k:
                            ins = nc.vector.tensor_scalar(dst[:, c, :], w(k), scale, None, ALU.mult)
                        else:
                            if k - 1 in signals:
                                dve.wait_ge(*signals[k - 1])
                            else:
                                sd.wait(sd.value() - 1)
                            ins = nc.vector.scalar_tensor_tensor(dst[:, c, :], w(k), scale, dst[:, c, :], ALU.mult, ALU.add)
                        if k in signals and c:
                            ins.then_inc(signals[k][0], 1)
                        else:
                            sd.done(ins)

            def ada_sums(u, pair, i=0, per=2, pairs=1):
                dve.wait_ge(unit_done, u + 2 * i)
                for x in range(pairs):
                    p_ = pair + x

                    def ready(k):
                        if k % 4 == 0:
                            dve.wait_ge(ada_full[k // 4], 16 * (p_ + 1) + 16 * per * i)

                    row_sums(lambda k: ada_w[:, k // 4, k % 4, :], (ada_acc, ada_acc_b)[x], ready,
                             {3: (ada_used, 2 * p_ + 3 + 2 * per * i), 7: (ada_used, 2 * p_ + 4 + 2 * per * i)})

            def gain_scale(l, comp, col):
                for s in range(2):
                    last = nc.vector.scalar_tensor_tensor(mods[:, l, comp, :, s], mods[:, l, comp, :, s], 1.0,
                                                          (vec1 if l else vec0)[:, col:col + KD], ALU.add, ALU.mult)
                return last

            def gain_gate(l, comp, col):
                for s in range(2):
                    last = vt(mods[:, l, comp, :, s], mods[:, l, comp, :, s], (vec1 if l else vec0)[:, col:col + KD], ALU.mult)
                return last

            def to_diagonals(dst, cols, nt, signal):
                for j in range(nt):
                    last = nc.vector.tensor_scalar(dst[:, j * P:(j + 1) * P], ident[:, :], cols[:, j:j + 1], None, ALU.mult)
                last.then_inc(signal, 1)

            def root_means(u, idx, nt, scale, dst):
                psum_full(dve, u)
                nc.vector.tensor_scalar(st[:, 0, 0:nt], acc[:, u % 2, 0, 0:nt], scale, EPS, ALU.mult, ALU.add
                                        ).then_inc(set_free[u % 2], 1)
                psum_read(dve, u)
                nc.vector.reciprocal(st[:, 0, 0:nt], st[:, 0, 0:nt]).then_inc(recip, 1)
                dve.wait_ge(root, idx)
                to_diagonals(dst, st[:, 1], nt, diag_ready)

            def give_back(u):
                nc.vector.tensor_copy(mark[:, u % 2:u % 2 + 1], acc[:, u % 2, 0, 0:1]).then_inc(set_free[u % 2], 1)

            def normed(u, use, stage, tokens):
                psum_full(dve, u)
                for m in range(KD):
                    if m >= 2:
                        dve.wait_ge(h_ready, KD * stage + m - 1)
                    vt(tbuf[:, m % 2, 0:tokens], xT[:, m, 0:tokens], acc[:, u % 2, 0, 0:tokens], ALU.mult).then_inc(t_ready, 1)
                give_back(u)

            def residual(u, l, comp, tokens):
                psum_full(dve, u)

                def add(m, value):
                    sd.wait(value)
                    for s, (t0, t1) in enumerate(SEGS[tokens]):
                        last = nc.vector.scalar_tensor_tensor(xT[:, m, t0:t1], y[:, m, t0:t1], mods[:, l, comp, m, s:s + 1],
                                                              xT[:, m, t0:t1], ALU.mult, ALU.add)
                    last.then_inc(x_new, 1)

                before = None
                for m in range(KD):
                    value = sd.done(vt(y[:, m, 0:tokens], y[:, m, 0:tokens], acc[:, u % 2, 0, 0:tokens], ALU.mult))
                    if m:
                        add(m - 1, before)
                    before = value
                add(KD - 1, before)
                give_back(u)

            def y_unit(u, tiles, tokens, add, i=0, adas=0, per=2):
                psum_full(dve, u, i)
                if adas:
                    dve.wait_ge(ada_out, adas + per * i)
                dst = y[:, tiles, 0:tokens]
                src = acc[:, u % 2, :, 0:tokens]
                (vt(dst, src, dst, ALU.add) if add else nc.vector.tensor_copy(dst, src)).then_inc(set_free[u % 2], 1)

            def add_squares(norm, m, tokens):
                c = KD * norm + m
                dve.wait_ge(sem("ysq_ready"), c + 1)
                if m:
                    dve.wait_ge(sem("ysq_used"), c)
                    ins = vt(sumsq[:, 0:tokens], sumsq[:, 0:tokens], sq[:, m % 2, 0:tokens], ALU.add)
                else:
                    ins = nc.vector.tensor_copy(sumsq[:, 0:tokens], sq[:, m % 2, 0:tokens])
                ins.then_inc(sem("ysq_used"), 1)

            def y_units(first, norm, tokens, add, adas=None):
                if adas:
                    ada_sums(first, 4, pairs=2)
                for j in range(4):
                    y_unit(first + j, slice(2 * j, 2 * j + 2), tokens, add, adas=adas[j] if adas else 0)
                    if adas and j < 3:
                        ada_sums(first + j + 1, 6 + 2 * j, pairs=2)
                    if j:
                        add_squares(norm, 2 * j - 2, tokens)
                        add_squares(norm, 2 * j - 1, tokens)
                add_squares(norm, KD - 2, tokens)
                add_squares(norm, KD - 1, tokens)

            nc.vector.memset(ones[:, :], 1.0).then_inc(sem("ones_set"), 1)
            nc.vector.memset(mark[:, 0:1], 0.0).then_inc(set_free[0], 1)
            nc.vector.memset(mark[:, 1:2], 0.0).then_inc(set_free[1], 1)
            nc.vector.memset(mods[:, 1, 0, 0, :], 0.0).then_inc(sem("ffn_conv"), 1)
            psum_read(dve, U["cond"])
            for n, q in enumerate(BY_DVE):
                dve.wait_ge(ada0_in[q], 16)
                row_sums(lambda k: ada_0[:, q, k, :], ada_acc0[:, q], None, {KD - 1: (ada0_sums, n + 1)})
            u = U["ada"]
            psum_full(dve, u)
            psum_read(dve, U["vec"])
            for s in range(2):
                last = vt(mods_flat[:, 0, 0:16, s], acc[:, u % 2, 0, s:32:2], vec0[:, 0:16], ALU.add)
            last.then_inc(set_free[u % 2], 1)
            psum_read(dve, u)
            sd.done(gain_scale(0, 1, 48))
            sd.wait()
            root_means(U["n0"], 1, NT, 1.0 / D, diag)
            normed(U["n0"] + 1, 0, 0, T)

            taps_len = LAT + HALF + CTX

            def gate_inputs(first):
                for t in (first, first + 1):
                    for (t0, t1), c in zip(SEGS[T], (U_LAT, U_CTX)):
                        last = vt(conv_u[:, t + 1, c:c + t1 - t0], conv_u[:, t + 1, c:c + t1 - t0], sig_b[:, t, t0:t1], ALU.mult)
                last.then_inc(sem("sig_used"), 1)

            def conv_pair(first):
                dve.wait_ge(sem("sig_used"), first // 2 + 1)
                with dve.Fori(0, 2) as t:
                    sd.loop(t, TAPS)
                    dst = conv_u[:, bass.ds(t + first, 1), HALF:HALF + taps_len]
                    for w in range(TAPS):
                        src = conv_u[:, bass.ds(t + (first + 1), 1), w:w + taps_len]
                        sd.wait()
                        tap = dw_w[:, w, bass.ds(t + first, 1)]
                        if w == 0:
                            ins = nc.vector.tensor_scalar(dst, src, tap, None, ALU.mult)
                        else:
                            ins = nc.vector.scalar_tensor_tensor(dst, src, tap, dst, ALU.mult, ALU.add)
                        sd.done(ins)
                    sd.end(2)
                sd.wait()

            ada_sums(U["conv"], 0, pairs=2)
            ada_sums(U["conv"] + 1, 2, pairs=2)
            psum_read(dve, U["conv"] + 1)
            gate_inputs(0)
            conv_pair(0)
            psum_read(dve, U["conv"] + 3)
            gate_inputs(2)
            r8 = [rows[0:8, q, :] for q in range(6)]
            lat, con = slice(0, LAT), slice(LAT, T)
            dve.wait_ge(sem("gate_log"), 1)
            sd.done(nc.vector.scalar_tensor_tensor(r8[0], r8[0], 0.0, r8[1], ALU.min, ALU.subtract))
            sd.wait()

            def scan(dst, src, op, other):
                sd.done(nc.vector.tensor_tensor_scan(dst[0][:, con], src[0][:, con], src[0][:, con], 0.0, op, other))
                back = sd.done(nc.vector.tensor_tensor_scan(dst[1][:, ::-1], src[1][:, ::-1], src[1][:, ::-1], 0.0, op, other))
                sd.wait(back)
                sd.done(nc.vector.tensor_tensor_scan(dst[0][:, lat], src[0][:, lat], src[0][:, lat],
                                                     dst[0][:, T - 1:T], op, other))
                sd.wait()

            scan((r8[3], r8[4]), (r8[0], r8[0]), ALU.add, ALU.bypass)
            b_i = gate_b[0:8, 1:2]
            sd.done(nc.vector.scalar_tensor_tensor(r8[5], r8[2], b_i, r8[3], ALU.add, ALU.subtract))
            sd.done(nc.vector.scalar_tensor_tensor(r8[0], r8[2], b_i, r8[4], ALU.add, ALU.subtract))
            sd.wait()
            scan((r8[1], r8[2]), (r8[5], r8[0]), ALU.max, ALU.bypass)
            sd.done(vt(r8[3], r8[3], r8[1], ALU.add))
            sd.done(vt(r8[4], r8[4], r8[2], ALU.add))
            sd.wait()
            nc.vector.tensor_scalar(r8[1], r8[1], -1.0, None, ALU.mult)
            nc.vector.tensor_scalar(r8[2], r8[2], -1.0, None, ALU.mult).then_inc(sem("rows_ready"), 1)
            conv_pair(2)
            nc.vector.tensor_copy(mark[:, 2:3], ident[:, 0:1]).then_inc(sem("conv_done"), 1)
            u = U["ln"]
            psum_full(dve, u)
            dve.wait_ge(sem("conv_done"), 1)
            nc.vector.tensor_scalar(st[:, 1, 0:NT], acc[:, u % 2, 0, 0:NT], 1.0 / 512, None, ALU.mult).then_inc(set_free[u % 2], 1)
            psum_read(dve, u)
            to_diagonals(ln_diag, st[:, 1], NT, diag_ready)
            conv_segs = tuple(zip(SEGS[T], (HALF, U_CTX)))

            def all_tiles(u, op, signal):
                psum_full(dve, u)
                for t in range(4):
                    for (t0, t1), c in conv_segs:
                        x_ = conv_u[:, t, c:c + t1 - t0]
                        last = vt(x_, x_, acc[:, u % 2, 0, t0:t1], op)
                    last.then_inc(signal, 1)
                give_back(u)

            all_tiles(u + 1, ALU.subtract, sem("conv_centred"))
            root_means(u + 2, 2, NT, 1.0 / 512, ln_diag)
            all_tiles(u + 3, ALU.mult, sem("conv_normed"))

            scale = float(HD) ** -0.5
            masked = 0
            dve.wait_ge(h_ready, KD + 4)
            for z, (kind, hd, q) in enumerate(ITEMS):
                if z < len(ITEMS) - 1:
                    dve.wait_ge(sem("slot_full"), z + 1)
                else:
                    psum_full(dve, U["mlstm"] + 1)
                if kind == "X":
                    if hd:
                        dve.wait_ge(h_ready, KD + 4 + hd)
                    nc.vector.scalar_tensor_tensor(merged[:, :], acc[:, 1, z % 2, 0:T], vec0[:, 88 + hd:89 + hd],
                                                   qkov[:, 12 + hd, :], ALU.mult, ALU.mult).then_inc(sem("merged_ready"), 1)
                    continue
                for e, (d, t0, t1) in STEPS[q]:
                    e += 16 * hd
                    s_tile = ORDER[q]
                    if t0 <= s_tile * P < t1:
                        masked += 1
                        dve.wait_ge(sem("e_masked"), masked)
                    else:
                        dve.wait_ge(sem("e_ready"), e + 1)
                    p_ = probs[:, e % 4, 0:t1 - t0]
                    nc.vector.scalar_tensor_tensor(p_, acc[:, 1, z % 2, t0:t1], scale, p_, ALU.mult, ALU.mult
                                                   ).then_inc(sem("p_ready"), 1)
                if q == 5:
                    dve.wait_ge(sem("den_abs"), hd + 1)
                    for d in range(2):
                        sd.done(vt(den[:, 1].rearrange("p b c -> p (b c)")[:, 6 * d:6 * d + 6],
                                   den[:, 0].rearrange("p b c -> p (b c)")[:, 6 * d:6 * d + 6],
                                   gcols[:, 2 + d, :, hd + 4 * d], ALU.max))
                    sd.wait()
                    sd.done(nc.vector.reciprocal(den[:, 1], den[:, 1]))
                    sd.wait()
                    w_ = den[:, 1].rearrange("p b c -> p (b c)")

                    def sums(d, t):
                        b, c = divmod(6 * d + t, 3)
                        c = (b % 2) * 512 + c * VW
                        return acc[:, 0, b // 2, c:c + HD]

                    if hd:
                        dve.wait_ge(sem("merged_ready"), hd)
                    for t in range(NT):
                        last = nc.vector.tensor_scalar(h_tok[:, t, :], sums(0, t), w_[:, t:t + 1], None, ALU.mult)
                    sd.done(last)
                    sd.wait()
                    for t in range(NT):
                        last = nc.vector.scalar_tensor_tensor(h_tok[:, t, :], sums(1, t), w_[:, 6 + t:7 + t], h_tok[:, t, :],
                                                              ALU.mult, ALU.add)
                    last.then_inc(sem("sums_read"), 1)
                    if hd < HEADS - 1:
                        continue
                if (q == 0 and hd) or q == 5:
                    of = hd if q == 5 else hd - 1
                    dve.wait_ge(sem("hss_ready"), of + 1)
                    sd.done(nc.vector.tensor_scalar(hss[:, 1, :], hss[:, 0, :], 1.0 / HD, EPS, ALU.mult, ALU.add))
                    sd.wait()
                    nc.vector.reciprocal(hss[:, 1, :], hss[:, 1, :]).then_inc(sem("hss_recip"), 1)
                    dve.wait_ge(sem("hss_root"), of + 1)
                    for t in range(NT):
                        last = nc.vector.tensor_scalar(h_tok[:, t, :], h_tok[:, t, :], hss[:, 1, t:t + 1], None, ALU.mult)
                    last.then_inc(sem("hn_ready"), 1)
            dve.wait_ge(sem("merged_ready"), HEADS)
            nc.vector.tensor_copy(mark[:, 3:4], ident[:, 0:1]).then_inc(set_free[0], 1)
            nc.vector.tensor_copy(mark[:, 4:5], ident[:, 0:1]).then_inc(set_free[1], 1)

            def ffn(l, norm, tokens, idx, stage):
                segs = tuple(zip(SEGS[tokens], (G_LAT, G_CTX)))
                nt = tokens // P
                root_means(U[f"n{1 + 3 * l}"], idx, nt, 1.0 / D, diag)
                if not l:
                    dve.wait_ge(ada_out, 6)
                    last = gain_gate(0, 2, 56)
                    last = gain_scale(0, 4, 64)
                else:
                    last = gain_gate(1, 2, 56)
                    last = gain_scale(1, 4, 64)
                    last = gain_gate(1, 5, 72)
                sd.done(last)
                residual(U[f"n{1 + 3 * l}"] + 1, l, 2, tokens)
                root_means(U[f"m{1 + 3 * l}"], idx + 1, nt, 1.0 / D, diag)
                normed(U[f"m{1 + 3 * l}"] + 1, 1 + 2 * l, stage, tokens)
                for c in (0, LAT + 1, T + 2):
                    last = nc.vector.memset(gpad[:, :, c:c + 1], 0.0)
                last.then_inc(sem("pads_zero"), 1)
                tile, pair, adas = 0, FT // 2 * l, 6
                for g, size in enumerate(FFN_GROUPS):
                    with dve.Fori(0, size // 2) as i:
                        sd.loop(i, 5 if l else 5 + 2 * 14)
                        u = U[f"up{l}{g}"]
                        if not l:
                            ada_sums(u, ADA_UP[g][0][0], i)
                        psum_read(dve, u, i)
                        for w in range(3):
                            for m in range(2):
                                c = ffn_cw[:, l, bass.ds(2 * i + (w * FT + tile + m), 1)]
                                if w:
                                    sd.wait(sd.value() - 1)
                                for (t0, t1), c0 in segs:
                                    src = gpad[:, m, c0 - 1 + w:c0 - 1 + w + t1 - t0]
                                    dst = hid[:, bass.ds(2 * i + m, 1), t0:t1]
                                    if w:
                                        ins = nc.vector.scalar_tensor_tensor(dst, src, c, dst, ALU.mult, ALU.add)
                                    else:
                                        ins = nc.vector.tensor_scalar(dst, src, c, None, ALU.mult)
                                if w == 2 and m:
                                    ins.then_inc(sem("ffn_conv"), 1)
                                else:
                                    sd.done(ins)
                        u += 1
                        if not l:
                            ada_sums(u, ADA_UP[g][1][0], i)
                        psum_full(dve, u, i)
                        dve.wait_ge(sem("ffn_silu"), pair + 1 + i)
                        if not l:
                            dve.wait_ge(ada_out, adas + 2 + 2 * i)
                        k = bass.ds(2 * i, 2)
                        hid_ = hid[:, k, 0:tokens]
                        vt(hid_, hid_, acc[:, u % 2, :, 0:tokens], ALU.mult).then_inc(set_free[u % 2], 1)
                        dve.wait_ge(sem("hid_high"), pair + 1 + i)
                        vt(hid_lo[:, k, 0:tokens], hid_, hid_hi[:, k, 0:tokens].bitcast(F32), ALU.subtract
                           ).then_inc(sem("hid_ready"), 1)
                        sd.end(size // 2)
                    tile += size
                    pair += size // 2
                    adas += size
                    first = U[f"down{l}{g}"]
                    if g == len(FFN_GROUPS) - 1:
                        y_units(first, norm + 1, tokens, True)
                    else:
                        with dve.Fori(0, 2) as i:
                            carry = [ADA_DOWN[g][j] if not l else None for j in range(2)]
                            count = sum(x is not None for x in carry)
                            sd.loop(i, 14 * count)
                            for j in range(2):
                                if carry[j]:
                                    ada_sums(first + j, carry[j][0], i, count)
                                y_unit(first + j, bass.ds(4 * i + 2 * j, 2), tokens, g > 0, i,
                                       adas + 1 + j if carry[j] else 0, count)
                            sd.end(2)
                        adas += 2 * count
                if not l:
                    sd.done(gain_gate(0, 5, 72))
                root_means(U[f"n{2 + 3 * l}"], idx + 2, nt, 1.0 / D, diag)
                residual(U[f"n{2 + 3 * l}"] + 1, l, 5, tokens)

            y_units(U["out0"], 0, T, False, adas=(3, 4, 5, 6))
            ffn(0, 0, T, 3, 2)
            dve.wait_ge(ada_out, 34)
            sd.done(gain_scale(1, 1, 48))
            sd.wait()
            root_means(U["n3"], 6, NT, 1.0 / D, diag)
            normed(U["n3"] + 1, 2, 3, T)
            nc.vector.memset(poolw[:, :, :], 0.0).then_inc(sem("poolw_zero"), 1)
            sd.done(nc.vector.memset(pu[:, :, :], 0.0))
            u = U["qst"]
            psum_full(dve, u)
            nc.vector.tensor_scalar(acol[:, :], acc[:, u % 2, 0, 0:36], 1.0 / HD, EPS, ALU.mult, ALU.add
                                    ).then_inc(set_free[u % 2], 1)
            psum_read(dve, u)
            nc.vector.reciprocal(acol[:, :], acol[:, :]).then_inc(recip, 1)
            dve.wait_ge(sem("tab_in"), 16 * 7)
            for v in range(4):
                u = U["rot"] + v
                psum_full(dve, u)
                for m in range(2):
                    x_ = inb[:, 2 + 2 * v + m, :] if v < 3 else kT[:, m, 0:LAT]
                    g = vec1[:, 82 + v // 3:83 + v // 3]
                    sd.done(vt(rt1[:, m, :], acc[:, u % 2, m, 0:LAT], rope[:, 1, :], ALU.mult))
                    sd.done(nc.vector.scalar_tensor_tensor(x_, x_, g, rope[:, 0, :], ALU.mult, ALU.mult))
                    sd.wait()
                    last = vt(x_, x_, rt1[:, m, :], ALU.add)
                last.then_inc(set_free[u % 2], 1)
                psum_read(dve, u)
            g = vec1[:, 83:84]
            sd.done(nc.vector.tensor_scalar(kT[:, :, LAT:T], kT[:, :, LAT:T], g, None, ALU.mult))
            dve.wait_ge(root, 7)
            for m in range(2):
                for j in range(NT):
                    c = NL * N_Q + NT * m + j
                    last = nc.vector.tensor_scalar(adiag[:, m, j * P:(j + 1) * P], ident[:, :], acol[:, c:c + 1], None, ALU.mult)
            last.then_inc(sem("kdiag_ready"), 1)
            sd.done(nc.vector.tensor_scalar(acol[:, 0:NL * N_Q], acol[:, 0:NL * N_Q], scale, None, ALU.mult))
            sd.wait()
            sd.done(nc.vector.tensor_copy(pu[:, :, 8:8 + LAT], inb[:, 0:2, :]))
            sd.wait()
            sd.done(vt(ps2[:, :, 1:PW], pu[:, :, 0:PW - 1], pu[:, :, 1:PW], ALU.add))
            sd.wait()
            sd.done(vt(ps4[:, :, 2:PW - 1], ps2[:, :, 1:PW - 2], ps2[:, :, 3:PW], ALU.add))
            sd.wait()
            c8 = slice(8, 8 + LAT)
            sd.done(vt(ps2[0:64, 0, c8], ps2[0:64, 0, c8], icnt[0:64, 0, :], ALU.mult))
            sd.done(vt(ps2[64:128, 0, c8], ps4[64:128, 0, c8], icnt[64:128, 0, :], ALU.mult))
            sd.done(vt(ps2[:, 1, 4:PW - 3], ps4[:, 1, 2:PW - 5], ps4[:, 1, 6:PW - 1], ALU.add))
            sd.wait()
            sd.done(vt(ps4[:, 1, c8], ps2[:, 1, 4:4 + LAT], ps2[:, 1, 12:12 + LAT], ALU.add))
            sd.wait()
            sd.done(vt(ps4[64:128, 1, c8], ps4[64:128, 1, c8], icnt[64:128, 1, :], ALU.mult))
            sd.done(vt(ps4[0:64, 1, c8], ps2[0:64, 1, c8], icnt[0:64, 1, :], ALU.mult))
            sd.wait()
            vt(pu[:, 0, c8], ps2[:, 0, c8], pu[:, 0, c8], ALU.subtract)
            vt(pu[:, 1, c8], ps4[:, 1, c8], pu[:, 1, c8], ALU.subtract).then_inc(sem("pooled"), 1)
            u = U["kb"]
            psum_full(dve, u)
            nc.vector.tensor_tensor(kT[:, :, :], kT[:, :, :], acc[:, u % 2, :, 0:T], ALU.mult).then_inc(set_free[u % 2], 1)
            psum_read(dve, u)
            u = U["pool"]
            psum_full(dve, u)
            for m in range(2):
                last = nc.vector.tensor_scalar(rt1[:, m, :], acc[:, u % 2, m, 0:LAT], vec1[:, 80 + m:81 + m], None, ALU.mult)
            last.then_inc(set_free[u % 2], 1)
            psum_read(dve, u)
            nc.vector.tensor_copy(mark[:, 5:6], ident[:, 0:1]).then_inc(sem("qk_ready"), 1)
            nc.vector.tensor_copy(mark[:, 6:7], ident[:, 0:1]).then_inc(sem("pool_float"), 1)
            dve.wait_ge(sem("pool_high"), 1)
            vt(h_lo[:, 0:2, 0:LAT], rt1[:, :, :], h_hi[:, 0:2, 0:LAT].bitcast(F32), ALU.subtract).then_inc(h_ready, 2)

            def head_low(hd):
                dve.wait_ge(sem("o_high"), hd + 1)
                c = (hd % 2) * 512
                vt(h_lo[:, 2 + hd, 0:LAT], acc[:, 1, 1, c:c + 512], h_hi[:, 2 + hd, 0:LAT].bitcast(F32), ALU.subtract
                   ).then_inc(h_ready, 1)

            for n in range(N_Q * NL + 1):
                if n < N_Q * NL:
                    dve.wait_ge(sem("score_full"), n + 1)
                    sd.done(nc.vector.reduce_max(arow[:, n, 0:1], acc[:, 0, n % 2, 0:T], AX.X))
                    sd.wait()
                    nc.vector.tensor_scalar(arow[:, n, 1:2], arow[:, n, 0:1], acol[:, n:n + 1], -1.0, ALU.mult, ALU.mult
                                            ).then_inc(sem("score_max"), 1)
                if n >= 1:
                    dve.wait_ge(sem("pT_full"), n)
                    if n >= 3:
                        dve.wait_ge(sem("pv_done"), n - 2)
                    nc.vector.tensor_copy(pT[:, (n - 1) % 2, :], acc[:, 1, 0, 0:T]).then_inc(sem("pT_ready"), 1)
                if n < N_Q * NL:
                    dve.wait_ge(sem("score_exp"), n + 1)
                    sd.done(nc.vector.reciprocal(arow[:, n, 3:4], arow[:, n, 2:3]))
                    sd.wait()
                    nc.vector.tensor_scalar(ptile[:, n % 2, :], ptile[:, n % 2, :], arow[:, n, 3:4], None, ALU.mult
                                            ).then_inc(sem("pn_ready"), 1)
                    if n % NL == 2 and n > NL:
                        head_low(n // NL - 1)
            head_low(N_Q - 1)
            dve.wait_ge(h_ready, 5 * KD)
            nc.vector.tensor_copy(mark[:, 7:8], ident[:, 0:1]).then_inc(set_free[0], 1)
            nc.vector.tensor_copy(mark[:, 8:9], ident[:, 0:1]).then_inc(set_free[1], 1)
            y_units(U["out1"], 2, LAT, False)
            ffn(1, 2, LAT, 8, 5)

        @block.gpsimd
        def _(pool):
            def take_low(n, i=0):
                pool.wait_ge(high, n + 1 + 4 * i)
                nc.gpsimd.tensor_tensor(w_lo[:, n % 4], raw[:, n % 2], w_hi[:, n % 4].bitcast(F32), ALU.subtract).then_inc(low, 1)

            def take_lows(first, turns):
                with pool.Fori(0, turns) as i:
                    for j in range(4):
                        take_low(first + j, i)

            def h_lows(use, stage, tokens):
                for m in range(KD):
                    pool.wait_ge(t_high, KD * use + m + 1)
                    nc.gpsimd.tensor_tensor(h_lo[:, m, 0:tokens], tbuf[:, m % 2, 0:tokens], h_hi[:, m, 0:tokens].bitcast(F32),
                                            ALU.subtract).then_inc(h_ready, 1)

            nc.gpsimd.memset(mark[:, 9:10], 0.0).then_inc(low, 4)
            nc.gpsimd.memset(mark[:, 10:11], 0.0).then_inc(ada_used, 2)
            h_lows(0, 0, T)
            take_low(0)
            take_low(1)
            pool.wait_ge(unit_done, U["n0"] + 2)
            nc.gpsimd.memset(conv_u[:, :, :], 0.0).then_inc(sem("conv_zero"), 1)
            n = G["conv"] + 2
            take_lows(n, 2)
            take_low(n + 8)
            take_low(n + 9)
            take_lows(n + 10, 4)
            pool.wait_ge(unit_done, U["gcol"] + 1)
            pool.wait_ge(sem("m_out"), 32)
            nc.gpsimd.memset(v_tok[:, :, :, HD:VW], 1.0).then_inc(sem("v_ones"), 1)
            for t in range(4):
                pool.wait_ge(sem("mix_high"), t + 1)
                for (t0, t1), c in zip(SEGS[T], (HALF, U_CTX)):
                    last = nc.gpsimd.tensor_tensor(h_lo[:, t, t0:t1], conv_u[:, t, c:c + t1 - t0],
                                                   h_hi[:, t, t0:t1].bitcast(F32), ALU.subtract)
                last.then_inc(h_ready, 1)
            for kind, hd, q in ITEMS:
                if kind == "X":
                    pool.wait_ge(sem("mix_high"), 5 + hd)
                    nc.gpsimd.tensor_tensor(h_lo[:, 4 + hd, :], merged[:, :], h_hi[:, 4 + hd, :].bitcast(F32), ALU.subtract
                                            ).then_inc(h_ready, 1)
                    continue
                s_tile = ORDER[q]
                for e, (d, t0, t1) in STEPS[q]:
                    if t0 <= s_tile * P < t1:
                        pool.wait_ge(sem("e_ready"), 16 * hd + e + 1)
                        block_ = probs[:, e % 4, s_tile * P - t0:s_tile * P - t0 + P]
                        sign = -1 if d else 1
                        nc.gpsimd.affine_select(out=block_, in_=block_, compare_op=ALU.is_ge, fill=0.0, base=0,
                                                pattern=[[sign, P]], channel_multiplier=-sign).then_inc(sem("e_masked"), 1)
            take_lows(G["out0"] + 2, 2)
            h_lows(1, 2, T)
            take_lows(G["up00"] + 2, 17)
            h_lows(2, 3, T)
            take_lows(G["in1"] + 2, 3)
            take_lows(G["out1"] + 2, 2)
            h_lows(3, 5, LAT)
            take_lows(G["up10"] + 2, 16)
            take_low(N_GRANULES - 2)
            take_low(N_GRANULES - 1)



_INS = ("x", "c", "ctx", "c_ctx", "ada_w", "ada_b", "mix_pre_g", "mix_post_g", "ffn_pre_g", "ffn_post_g", "ffn_w_in",
        "ffn_conv_w", "ffn_w_out", "even_w_in", "even_w_out", "conv_dw_w", "conv_ln_g", "conv_ln_b", "mlstm_gate_b",
        "mlstm_norm_g", "odd_w_in", "odd_w_out", "pool_w", "pool_scale", "q_norm_g", "k_norm_g")


def constants():
    freq = HD // 4
    inv = (10000.0 ** (-np.arange(freq, dtype=np.float32) / np.float32(freq))).astype(np.float32)
    t = np.arange(LAT)
    row, col = (t // 64).astype(np.float32), (t % 64).astype(np.float32)
    angle = np.concatenate([row[:, None] * inv, col[:, None] * inv], axis=-1).astype(np.float32)
    of_pair = np.arange(HD) // 2
    rope = np.stack([np.cos(angle)[:, of_pair].T, np.sin(angle)[:, of_pair].T]).astype(np.float32)
    rotate = np.zeros((P, P), np.float32)
    even = np.arange(0, P, 2)
    rotate[even + 1, even] = -1.0
    rotate[even, even + 1] = 1.0
    count = np.zeros((2, P, LAT), np.float32)
    for g, w in enumerate(WINDOWS):
        n = np.clip(t + w // 2, 0, LAT) - np.clip(t - w // 2, 0, LAT)
        count[g // 2, 64 * (g % 2):64 * (g % 2) + 64] = 1.0 / n
    return {"identity": np.eye(P, dtype=np.float32), "rope": rope, "rotate": rotate, "pool_count": count}


def kernel(**inputs):
    import concourse.bacc as bacc
    from concourse.bass_utils import run_bass_kernel_spmd

    nc = bacc.Bacc("TRN2", target_bir_lowering=False, num_devices=1)
    arrays, a = {}, {}
    for name, x in [(n, inputs[n]) for n in _INS] + list(constants().items()):
        x = np.ascontiguousarray(x)
        arrays[f"in_{name}"] = x
        a[name] = nc.dram_tensor(f"in_{name}", x.shape, mybir.dt.from_np(x.dtype), kind="ExternalInput").ap()
    out = nc.dram_tensor("out_x", (1, LAT, D), F32, kind="ExternalOutput").ap()
    build(nc, a, out)
    r = run_bass_kernel_spmd(nc, [arrays], core_ids=[0])
    return r.results[0]["out_x"]
```

```python
from contextlib import ExitStack

import numpy as np

import concourse.bass as bass
from concourse import mybir

F32 = mybir.dt.float32
F32R = mybir.dt.float32r
ALU = mybir.AluOpType
ACT = mybir.ActivationFunctionType
AX = mybir.AxisListType

P = 128
D = 1024
KD = D // P
LAT = 512
CTX = 256
T = LAT + CTX
NT = T // P
NL = LAT // P
EPS = 1e-6
D_FF = 2816
FT = D_FF // P
TAPS = 31
HEADS = 4
HD = 128
GATE_COL = 3072
VW = HD + 1
N_VECTORS = 19
N_Q, N_KV = 6, 2
WINDOWS = (2, 4, 8, 16)
FFN_GROUPS = (8, 8, 6)
SEGS = {T: ((0, LAT), (LAT, T)), LAT: ((0, LAT),)}
HALF = TAPS // 2
U_LAT, U_CTX = HALF, 2 * HALF + LAT
U_LEN = 3 * HALF + T + 1
G_LAT, G_CTX = 1, LAT + 2
G_LEN = T + 4


class Steps:

    def __init__(self, eng, sem):
        self.eng, self.sem, self.count, self.reg, self.per, self.first = eng, sem, 0, None, 0, 0

    def done(self, ins):
        self.count += 1
        ins.then_inc(self.sem, 1)
        return self.value()

    def value(self):
        return self.count if self.reg is None else self.reg * self.per + self.count

    def wait(self, value=None):
        self.eng.wait_ge(self.sem, self.value() if value is None else value)

    def loop(self, reg, per):
        self.reg, self.per, self.first = reg, per, self.count

    def end(self, trips):
        assert self.count - self.first == self.per, (self.count - self.first, self.per)
        self.count = self.first + self.per * trips
        self.reg = None


def plan():
    order = [("cond", 1, 0), ("vec", 1, 0), ("xt", 4, 0), ("ada", 1, 0), ("n0", 2, 0), ("conv", 4, 2), ("gate", 1, 2), ("qkov", 8, 2),
             ("gcol", 1, 0), ("vt", 3, 0), ("mlstm", 2, 0), ("out0", 4, 2)]
    for l in range(2):
        if l:
            order += [("n3", 2, 0), ("in1", 4, 2), ("kin", 1, 2), ("qst", 1, 0), ("rot0", 2, 0), ("pool", 1, 0),
                      ("vin", 1, 2), ("kst", 1, 0), ("rot2", 2, 0), ("kb", 1, 0), ("att", 2, 0), ("out1", 4, 2)]
        order += [(f"n{1 + 3 * l}", 2, 0), (f"m{1 + 3 * l}", 2, 0)]
        for g, size in enumerate(FFN_GROUPS):
            order += [(f"up{l}{g}", size, 2), (f"down{l}{g}", 4, 2)]
        order += [(f"n{2 + 3 * l}", 2, 0)]
    order += [("outT", 2, 0)]
    unit, granule, u, n = {}, {}, 0, 0
    for name, units, granules in order:
        unit[name], granule[name] = u, n
        u += units
        n += units * granules
    return unit, granule, n


ADA_UP = (((12, 2, 0, 40, 1), (13, 2, 1, 0, 1)), ((24, 2, 1, 16, 2), (25, 2, 1, 18, 2)), ((34, 2, 1, 36, 2), (35, 2, 1, 38, 2)))
ADA_DOWN = (((20, 2, 1, 8, 2), (21, 2, 1, 10, 2)), ((32, 1, 1, 32, 1), None), (None, None))

ORDER = (4, 5, 0, 1, 2, 3)


def mlstm_steps():
    steps, e = [], 0
    for s in ORDER:
        if s < NL:
            of_tile = [(0, s * P, LAT), (1, 0, (s + 1) * P)]
        else:
            of_tile = [(0, 0, LAT), (0, s * P, T), (1, 0, LAT), (1, LAT, (s + 1) * P)]
        steps.append([(e + n, x) for n, x in enumerate(of_tile)])
        e += len(of_tile)
    return steps


STEPS = mlstm_steps()
TOUCHES = [[(q, d, t) for q in range(NT) for _, (d, t0, t1) in STEPS[q] for t in range(t0 // P, t1 // P)
            if (6 * d + t) // 3 == b] for b in range(4)]
FIRST_TOUCH = [x[0] for x in TOUCHES]
LAST_TOUCH = [x[-1] for x in TOUCHES]
ITEMS = [("S", 0, 0), ("L", 0, 0), ("S", 0, 1), ("L", 0, 1), ("S", 0, 2), ("L", 0, 2), ("S", 0, 3), ("L", 0, 3),
         ("S", 0, 4), ("S", 0, 5)]
ITEMS += [("X", h - 1, 0) if q == "X" else ("S", h, q) for h in range(1, HEADS) for q in (0, 1, 2, "X", 3, 4, 5)]
ITEMS += [("X", HEADS - 1, 0)]


def build(nc, a, out):
    U, G, N_GRANULES = plan()
    ctx = ExitStack()
    with ctx:
        used = {}

        def sem(name):
            if name not in used:
                used[name] = ctx.enter_context(nc.semaphore(name))
            return used[name]

        base = (nc.sbuf_base + 31) // 32 * 32
        top = nc.sbuf_usable_end
        at = [base]

        def place(name, shape, dt=F32, offset=None):
            size = int(np.prod(shape[1:])) * 4
            if offset is None:
                offset = at[0]
                at[0] += (size + 31) // 32 * 32
                assert at[0] <= top, (name, at[0] - top)
            assert offset + size <= top, name
            return nc.alloc_sbuf_tensor_at(name, shape, dt, offset=offset)

        xT = place("xT", [P, KD, T])
        H0 = at[0]
        h_hi = place("h_hi", [P, KD, T], F32R)
        h_lo = place("h_lo", [P, KD, T], F32R)
        raw = place("raw", [P, 2, 4, 256])
        W_HI = at[0]
        w_hi = place("w_hi", [P, 4, 4, 256], F32R)
        W_LO = at[0]
        w_lo = place("w_lo", [P, 4, 4, 256], F32R)
        ident = place("ident", [P, P])
        ones = place("ones", [P, P])
        vec0 = place("vec0", [P, 92])
        vec1 = place("vec1", [P, 84])
        ffn_cw = place("ffn_cw", [P, 2, 66])
        dw_w = place("dw_w", [P, TAPS, 4])
        mods = place("mods", [P, 2, 6, KD, 2])
        cond = place("cond", [P, KD, 2])
        st = place("st", [P, 2, NT])
        gate_b = place("gate_b", [P, 2])
        mark = place("mark", [P, 16])
        ADA = at[0]
        ada_w = place("ada_w", [P, 2, 4, 256])
        ada_acc = place("ada_acc", [P, 2, 256])
        A0 = at[0]
        ARENA = top // 32 * 32 - A0
        assert ARENA >= 84000, ARENA

        qkov = place("qkov", [P, 16, T], offset=A0)
        negM = place("negM", [P, 2, 2, T], offset=A0 + 8 * T * 4)
        sig_b = place("sig_b", [P, 4, T], offset=A0 + 8 * T * 4)
        v_tok = place("v_tok", [P, NT, HEADS, VW], offset=A0 + 49152)
        EP0 = A0 + 49152 + 12384
        probs_012 = place("probs_012", [P, 3, LAT], offset=EP0)
        rows = place("rows", [P, 6, T], offset=A0 + 49152)
        ln_sq = place("ln_sq", [P, 2, T], offset=H0 + 6 * T * 4)
        U0 = EP0 + 6144
        conv_u = place("conv_u", [P, 5, U_LEN], offset=U0)
        ln_diag = place("ln_diag", [P, T], offset=ADA + 2048)
        probs_3 = place("probs_3", [P, LAT], offset=U0 + 4 * U_LEN * 4)
        probs = [probs_012[:, 0, :], probs_012[:, 1, :], probs_012[:, 2, :], probs_3[:, :]]
        h_tok = place("h_tok", [P, NT, P], offset=ADA + 5120)
        merged = place("merged", [P, T], offset=EP0 + 11264)
        sq_junk = place("sq_junk", [P, NT, P], offset=EP0 + 14336)
        gcols = place("gcols", [P, 4, NT, 8], offset=ADA)
        den = place("den", [P, 2, 4, 3], offset=ADA + 1024)
        hss = place("hss", [P, 2, NT], offset=ADA + 1280)
        hid_hi = place("hid_hi", [P, 8, T], F32R, offset=A0)
        hid_lo = place("hid_lo", [P, 8, T], F32R, offset=A0 + 24576)
        tbuf = place("tbuf", [P, 3, T], offset=A0)
        y = place("y", [P, KD, T], offset=A0 + 49152)
        SCR = A0 + 73728
        gpad = place("gpad", [P, 2, G_LEN], offset=SCR)
        hid = place("hid", [P, 8, T], offset=A0 + 24576)
        sq = place("sq", [P, 2, T], offset=SCR)
        sumsq = place("sumsq", [P, T], offset=SCR + 6144)
        diag = place("diag", [P, T], offset=A0 + 9216)
        x_tok = place("x_tok", [P, NT, D], offset=H0)
        ada_0 = place("ada_0", [P, 8, KD, 2 * P], offset=A0)
        vrows = place("vrows", [P, 6, P], offset=W_LO + 3 * 4096)
        ada_acc_b = place("ada_acc_b", [P, 2, 256], offset=A0 + 12288)
        ada_acc0 = place("ada_acc0", [P, 8, 2, 256], offset=W_HI)
        inb = place("inb", [P, 8, LAT], offset=A0)
        kT = place("kT", [P, N_KV, T], offset=A0 + 16384)
        v1 = place("v1", [P, NT, N_KV * HD], offset=A0 + 22528)
        rope = place("rope", [P, 2, LAT], offset=A0 + 28672)
        rotw = place("rotw", [P, 3, P], offset=A0 + 32768)
        icnt = place("icnt", [P, 2, LAT], offset=A0 + 34304)
        poolw = place("poolw", [P, 2, P], offset=A0 + 38400)
        PW = LAT + 16
        pu = place("pu", [P, 2, PW], offset=A0 + 39424)
        ps2 = place("ps2", [P, 2, PW], offset=A0 + 43648)
        ps4 = place("ps4", [P, 2, PW], offset=A0 + 47872)
        asq = place("asq", [P, 2, T], offset=A0 + 52096)
        adiag = place("adiag", [P, 2, T], offset=A0 + 58240)
        rt1 = place("rt1", [P, 2, LAT], offset=A0 + 64384)
        ptile = place("ptile", [P, 2, T], offset=A0 + 68480)
        pT = place("pT", [P, 2, T], offset=A0 + 74624)
        acol = place("acol", [P, 36], offset=ADA)
        arow = place("arow", [P, 24, 4], offset=ADA + 256)
        o_tok = place("o_tok", [P, NL, D], offset=A0)

        acc = ctx.enter_context(nc.psum_tensor("acc", [P, 2, 2, 2 * 512], F32))
        m_dram = nc.dram_tensor("m_rows", (2, HEADS, T), F32, kind="Internal").ap()

        ada0_in = [sem(f"ada0_in{q}") for q in range(8)]
        ada0_sums = sem("ada0_sums")
        x_in = [sem("x_in0"), sem("x_in1")]
        raw_full = [sem("raw_full0"), sem("raw_full1")]
        high, low = sem("w_high"), sem("w_low")
        unit_done = sem("unit_done")
        set_free = [sem("set0_free"), sem("set1_free")]
        ada_full = [sem("ada_full0"), sem("ada_full1")]
        ada_used, ada_out = sem("ada_used"), sem("ada_out")
        h_ready, sq_ready, sq_used = sem("h_ready"), sem("sq_ready"), sem("sq_used")
        recip, root, diag_ready = sem("recip"), sem("root"), sem("diag_ready")
        x_new, t_ready, t_high = sem("x_new"), sem("t_ready"), sem("t_high")

        def psum_free(eng, u, i=0):
            eng.wait_ge(set_free[u % 2], u // 2 + 1 + i)

        def psum_full(eng, u, i=0):
            eng.wait_ge(unit_done, u + 1 + 2 * i)

        def psum_read(eng, u, i=0):
            eng.wait_ge(set_free[u % 2], u // 2 + 2 + i)

        def loaded(n, i=0):
            return 16 * (n // 2 + 1) + 32 * i

        w_even = a["even_w_in"][0].rearrange("(k p) n -> p k n", p=P)
        w_even_out = a["even_w_out"][0].rearrange("(k p) n -> p k n", p=P)
        w_odd = a["odd_w_in"][0].rearrange("(k p) n -> p k n", p=P)
        w_odd_out = a["odd_w_out"][0].rearrange("(k p) n -> p k n", p=P)
        w_ffn_in = [a["ffn_w_in"][l].rearrange("(k p) n -> p k n", p=P) for l in range(2)]
        w_ffn_out = [a["ffn_w_out"][l].rearrange("(k p) n -> p k n", p=P) for l in range(2)]
        w_ada = [a["ada_w"][l].rearrange("(k p) n -> p k n", p=P) for l in range(2)]
        SPLIT = {8: (4, 4), 6: (4, 2)}

        block = ctx.enter_context(nc.Block())

        def load(sp, n, src, i=0):
            sp.wait_ge(low, n + 3 + 4 * i)
            kt = src.shape[1]
            sp.dma_start(raw[:, n % 2, 0:kt, :], src).then_inc(raw_full[n % 2], 16)

        def load_unit(sp, n, w, col, k0=0, ktiles=KD, i=0):
            for part, kt in enumerate(SPLIT[ktiles]):
                k = k0 + 4 * part
                load(sp, n + part, w[:, k:k + kt, bass.ds(col, 256)], i)

        def load_ada(sp, pair, l, of_layer, i=0, per=2):
            for half in range(2):
                sp.wait_ge(ada_used, 2 * pair + half + 1 + 2 * per * i)
                sp.dma_start(ada_w[:, half], w_ada[l][:, 4 * half:4 * half + 4, bass.ds(of_layer * 256, 256)]
                             ).then_inc(ada_full[half], 16)

        BY_PE = (4, 6)
        BY_DVE = [q for q in range(8) if q not in BY_PE]

        @block.sync
        def _(sp):
            sp.dma_start(ident[:, :], a["identity"]).then_inc(sem("ident_in"), 16)
            tile_rows = [0] * 5

            def vector_rows(block_, src):
                r = tile_rows[block_]
                n = src.shape[0]
                sp.dma_start(vrows[r:r + n, block_, :], src).then_inc(sem("vec_in"), 16)
                tile_rows[block_] = r + n

            def load_ada_0(first, end):
                for q in range(first, end):
                    sp.dma_start(ada_0[:, q], w_ada[0][:, :, q * 256:(q + 1) * 256]).then_inc(ada0_in[q], 16)

            def load_x(first, end):
                for j in range(first, end):
                    src = a["x"][0, j * P:(j + 1) * P] if j < NL else a["ctx"][0, (j - NL) * P:(j - NL + 1) * P]
                    sp.dma_start(x_tok[:, j, :], src).then_inc(x_in[j // 3], 16)

            for s, name in enumerate(("c", "c_ctx")):
                src = a["c"][0] if name == "c" else a["c_ctx"]
                sp.dma_start(vrows[KD * s:KD * (s + 1), 5, :], src.rearrange("(r p) -> r p", p=P)).then_inc(sem("cond_in"), 16)
            load_ada_0(0, 3)
            gains = ("mix_pre_g", "mix_post_g", "ffn_pre_g", "ffn_post_g")
            for l in range(2):
                vector_rows(l, a["ada_b"][l].rearrange("(r p) -> r p", p=P))
                for g in gains:
                    vector_rows(l, a[g][l].rearrange("(r p) -> r p", p=P))
            for g in ("conv_ln_g", "conv_ln_b", "mlstm_norm_g"):
                vector_rows(0, a[g][0].rearrange("(r p) -> r p", p=P))
            for g in ("pool_scale", "q_norm_g", "k_norm_g"):
                vector_rows(1, a[g][0].rearrange("(r p) -> r p", p=P))
            for l in range(2):
                vector_rows(2 + l, a["ffn_conv_w"][l].rearrange("w (j p) -> (w j) p", p=P))
            vector_rows(4, a["conv_dw_w"][0].rearrange("w (j p) -> (w j) p", p=P))
            load_x(0, NT)
            load_ada_0(3, 8)
            for q in range(4):
                sp.dma_start(gate_b[4 * (q // 2):4 * (q // 2) + 4, 1 - q % 2:2 - q % 2],
                             a["mlstm_gate_b"][0, q].rearrange("(h o) -> h o", o=1)).then_inc(sem("gate_b_in"), 16)
            for i in range(2):
                n = G["conv"] + 4 * i
                load_unit(sp, n, w_even, i * 256 + 512)
                if not i:
                    load_ada(sp, 0, 0, 8)
                    load_ada(sp, 1, 0, 9)
                load_unit(sp, n + 2, w_even, i * 256)
                if not i:
                    load_ada(sp, 2, 0, 10)
                    load_ada(sp, 3, 0, 11)
            for part in range(2):
                n = G["gate"] + part
                sp.wait_ge(low, n + 3)
                for q, (dst, src) in enumerate(((0, 4), (4, 12), (32, 0), (36, 8))):
                    if q == 3:
                        sp.wait_ge(sem("gate_parts"), 48 * (part + 1))
                    sp.dma_start(raw[:, n % 2, :, dst:dst + 4],
                                 w_even[:, 4 * part:4 * part + 4, GATE_COL + src:GATE_COL + src + 4]
                                 ).then_inc(raw_full[n % 2] if q == 3 else sem("gate_parts"), 16)
            with sp.Fori(0, 4) as i:
                for j in range(2):
                    load_unit(sp, G["qkov"] + 2 * j, w_even, i * 512 + (1024 + 256 * j), i=i)
            sp.wait_ge(sem("rows_ready"), 1)
            for d in range(2):
                sp.dma_start(m_dram[d], rows[4 * d:4 * d + 4, 1 + d, :]).then_inc(sem("m_out"), 16)
            n = G["out0"]
            load_unit(sp, n, w_even_out, 0)
            sp.wait_ge(sem("m_out"), 32)
            psum_read(sp, U["vt"] + 2)
            for h in range(HEADS):
                if h >= 2:
                    sp.wait_ge(sem("p_used"), 16 * (h - 1))
                sp.dma_start(negM[:, h % 2], m_dram[:, h, :].partition_broadcast(P)).then_inc(sem(f"m_in{h % 2}"), 16)
            sp.wait_ge(unit_done, U["out0"])
            for j in range(4):
                if j:
                    load_unit(sp, n + 2 * j, w_even_out, 256 * j)
                load_ada(sp, 4 + 2 * j, 0, 12 + 2 * j)
                load_ada(sp, 5 + 2 * j, 0, 13 + 2 * j)
            for l in range(2):
                if l:
                    w = w_odd
                    with sp.Fori(0, 2) as i:
                        for j in range(2):
                            load_unit(sp, G["in1"] + 2 * j, w, i * 512 + 256 * j, i=i)
                    sp.wait_ge(unit_done, U["n3"] + 2)
                    for dst, name in ((rope, "rope"), (icnt, "pool_count")):
                        sp.dma_start(dst[:, :, :], a[name].rearrange("a p t -> p a t")).then_inc(sem("tab_in"), 16)
                    sp.dma_start(rotw[:, 0, :], a["rotate"]).then_inc(sem("tab_in"), 16)
                    sp.wait_ge(sem("poolw_zero"), 1)
                    for g in range(4):
                        lo = 64 * (g % 2)
                        sp.dma_start(poolw[lo:lo + 64, g // 2, lo:lo + 64], a["pool_w"][0, g]).then_inc(sem("tab_in"), 16)
                    load_unit(sp, G["kin"], w, 1024)
                    load_unit(sp, G["vin"], w, 1280)
                    for j in range(4):
                        load_unit(sp, G["out1"] + 2 * j, w_odd_out, 256 * j)
                first = 0
                for g, size in enumerate(FFN_GROUPS):
                    n = G[f"up{l}{g}"]
                    with sp.Fori(0, size // 2) as i:
                        for j in range(2):
                            load_unit(sp, n + 2 * j, w_ffn_in[l], i * 256 + (first * P + j * D_FF), i=i)
                            if not l:
                                pair, per, layer, tiles, step = ADA_UP[g][j]
                                load_ada(sp, pair, layer, step * i + tiles // 2, i, per)
                    n = G[f"down{l}{g}"]
                    with sp.Fori(0, 2) as i:
                        for j in range(2):
                            load_unit(sp, n + 2 * j, w_ffn_out[l], i * 512 + 256 * j, first, size, i)
                            if not l and ADA_DOWN[g][j]:
                                pair, per, layer, tiles, step = ADA_DOWN[g][j]
                                load_ada(sp, pair, layer, step * i + tiles // 2, i, per)
                    first += size
            for j in range(NL):
                sp.wait_ge(sem("o_ready"), j + 1)
                sp.dma_start(out[0, j * P:(j + 1) * P], o_tok[:, j, :]).then_inc(sem("out_done"), 16)
            sp.wait_ge(sem("out_done"), 16 * NL)

        def product(pe, u, n, rhs, ready, ktiles=KD, segs=SEGS[T], i=0, ada=None, pairs=1, halves=(0, 1),
                    parts=(0, 1)):
            s = u % 2
            if parts != (0,):
                psum_free(pe, u, i)
            k = 4 * parts[0]
            for part, kt in enumerate(SPLIT[ktiles]):
                if part not in parts:
                    continue
                slot = (n + part) % 4
                pe.wait_ge(low, n + part + 5 + 4 * i)
                for kk in range(kt):
                    ready(k)
                    for m in halves:
                        c = slice(m * P, (m + 1) * P)
                        for q, (w, x) in enumerate(((w_hi, rhs[0]), (w_hi, rhs[1]), (w_lo, rhs[0]))):
                            for t0, t1 in segs:
                                last = nc.tensor.matmul(acc[:, s, m, t0:t1], w[:, slot, kk, c], x[:, k, t0:t1],
                                                        start=(k == 0 and q == 0), stop=(k == ktiles - 1 and q == 2))
                    k += 1
            if parts == (0,):
                return
            if ada:
                pair, per = ada[:2]
                for x in range(pairs):
                    pe.wait_ge(ada_used, 2 * (pair + x) + 4 + 2 * per * i)
                    for q in range(2):
                        for c in range(2):
                            at_ = 1008 + 4 * x + 2 * q + c
                            last = nc.tensor.matmul(acc[:, s, 0, at_:at_ + 1], (ada_acc, ada_acc_b)[x][:, c, q * P:(q + 1) * P],
                                                    ones[:, 0:1], start=True, stop=True)
            last.then_inc(unit_done, 1)

        @block.tensor
        def _(pe):
            def always(k):
                pass

            def h_tiles(stage):
                return lambda k: pe.wait_ge(h_ready, KD * stage + k + 1)

            def transpose(dst, src, rows_=P):
                return nc.tensor.transpose(dst, src, ident[0:rows_, 0:rows_])

            def column_sums(u, sources, tiles, wait, after):
                s = u % 2
                psum_free(pe, u)
                for m, src in enumerate(sources):
                    wait(m)
                    for j in range(tiles):
                        last = nc.tensor.matmul(acc[:, s, 0, j:j + 1], src(j), ones[:, 0:1],
                                                start=(m == 0 and j == 0),
                                                stop=(m == len(sources) - 1 and j == tiles - 1), skip_group_check=True)
                    if after is not None and m < len(sources) - 1:
                        last.then_inc(after, 1)
                last.then_inc(unit_done, 1)

            def spread(u, diagonal, tokens, count):
                psum_free(pe, u)
                pe.wait_ge(diag_ready, count)
                for t0, t1 in SEGS[tokens]:
                    last = nc.tensor.matmul(acc[:, u % 2, 0, t0:t1], ones[:, :], diagonal[:, t0:t1], start=True, stop=True)
                last.then_inc(unit_done, 1)

            def keep_clock(u, count):
                for _ in range(count):
                    nc.tensor.matmul(acc[:, u % 2, 1, 512:512 + P], ones[:, :], ident[:, :], start=True, stop=True)

            def norm_x(u, norm, tokens, diag_count):
                if norm:
                    psum_free(pe, u)
                    keep_clock(u, 70 * tokens // T)
                waits = ((sq_used, 6 * (norm + 1)), (sq_ready, KD * (norm + 1)))
                column_sums(u, [lambda j: sumsq[:, j * P:(j + 1) * P], lambda j: sq[:, 1, j * P:(j + 1) * P]], tokens // P,
                            lambda m: pe.wait_ge(*waits[m]), None)
                keep_clock(u, 6)
                spread(u + 1, diag, tokens, diag_count)
                keep_clock(u + 1, 12)

            def norm_y(u, norm, tokens, diag_count):
                psum_free(pe, u)
                keep_clock(u, 6)
                waits = ((sem("ysq_used"), 6 * (norm + 1)), (sem("ysq_ready"), KD * norm + 7),
                         (sem("ysq_ready"), KD * norm + 8))
                column_sums(u, [lambda j: sumsq[:, j * P:(j + 1) * P], lambda j: sq[:, 0, j * P:(j + 1) * P],
                                lambda j: sq[:, 1, j * P:(j + 1) * P]], tokens // P, lambda m: pe.wait_ge(*waits[m]), None)
                spread(u + 1, diag, tokens, diag_count)

            pe.wait_ge(sem("ident_in"), 16)
            pe.wait_ge(sem("cond_in"), 32)
            psum_free(pe, U["cond"])
            transpose(acc[:, U["cond"] % 2, 0, 0:2 * KD], vrows[0:2 * KD, 5, :], 2 * KD).then_inc(unit_done, 1)
            pe.wait_ge(sem("vec_in"), 16 * N_VECTORS)
            pe.wait_ge(sem("ones_set"), 1)
            psum_free(pe, U["vec"])
            for b, (n, m, col) in enumerate(((92, 0, 0), (84, 0, 128), (66, 0, 256), (66, 0, 384), (124, 1, 0))):
                last = transpose(acc[:, U["vec"] % 2, m, col:col + n], vrows[0:n, b, :], n)
            last.then_inc(unit_done, 1)
            for q in range(2):
                pe.wait_ge(x_in[q], 16 * 3)
            for v in range(4):
                u = U["xt"] + v
                psum_free(pe, u)
                for m in range(2):
                    for j in range(NT):
                        last = transpose(acc[:, u % 2, m, j * P:(j + 1) * P],
                                         x_tok[:, j, (2 * v + m) * P:(2 * v + m + 1) * P])
                last.then_inc(unit_done, 1)
            u = U["ada"]
            psum_free(pe, u)
            psum_read(pe, U["cond"])
            for q in range(8):
                if q in BY_PE:
                    pe.wait_ge(ada0_in[q], 16)
                    for m in (0, 1):
                        for k in range(KD):
                            nc.tensor.matmul(acc[:, u % 2, 0, 4 * q + 2 * m:4 * q + 2 * m + 2],
                                             ada_0[:, q, k, m * P:(m + 1) * P], cond[:, k, :], start=(k == 0), stop=(k == KD - 1))
                    continue
                pe.wait_ge(ada0_sums, BY_DVE.index(q) + 1)
                for m in (2 * q, 2 * q + 1):
                    for c in range(2):
                        last = nc.tensor.matmul(acc[:, u % 2, 0, 2 * m + c:2 * m + c + 1],
                                                ada_acc0[:, q, c, (m % 2) * P:(m % 2 + 1) * P], ones[:, 0:1],
                                                start=True, stop=True)
            last.then_inc(unit_done, 1)
            norm_x(U["n0"], 0, T, 1)
            h = (h_hi, h_lo)
            for j in range(4):
                product(pe, U["conv"] + j, G["conv"] + 2 * j, h, always if j else h_tiles(0), ada=(2 * j, 0) if j < 2 else None,
                        pairs=2)
            product(pe, U["gate"], G["gate"], h, always, halves=(0,))
            with pe.Fori(0, 4) as i:
                for j in range(2):
                    product(pe, U["qkov"] + j, G["qkov"] + 2 * j, h, always, i=i)
            u = U["gcol"]
            psum_free(pe, u)
            pe.wait_ge(sem("rows_ready"), 1)
            for x_, row in enumerate((5, 0, 3, 4)):
                for j in range(NT):
                    c = (x_ * NT + j) * 8
                    last = transpose(acc[:, u % 2, 0, c:c + 8], rows[0:8, row, j * P:(j + 1) * P], 8)
            last.then_inc(unit_done, 1)
            for v in range(3):
                u = U["vt"] + v
                psum_free(pe, u)
                for m in range(2):
                    j = 2 * v + m
                    for hd in range(HEADS):
                        last = transpose(acc[:, u % 2, m, hd * P:(hd + 1) * P], qkov[:, 8 + hd, j * P:(j + 1) * P])
                last.then_inc(unit_done, 1)
            def conv_cols(tile, j):
                c = HALF + j * P if j < NL else U_CTX + (j - NL) * P
                return conv_u[:, tile, c:c + P]

            def conv_norm_step(step, slot):
                if step % 2:
                    pe.wait_ge(diag_ready, 2 + step // 2)
                    for t0, t1 in SEGS[T]:
                        last = nc.tensor.matmul(acc[:, 1, slot, t0:t1], ones[:, :], ln_diag[:, t0:t1], start=True, stop=True)
                    return last
                for m in range(4):
                    if step:
                        pe.wait_ge(sem("ln_sq_ready"), m + 1)
                    elif not m:
                        pe.wait_ge(sem("conv_done"), 1)
                    for j in range(NT):
                        src = ln_sq[:, m % 2, j * P:(j + 1) * P] if step else conv_cols(m, j)
                        last = nc.tensor.matmul(acc[:, 1, slot, j:j + 1], src, ones[:, 0:1], start=(m == 0 and j == 0),
                                                stop=(m == 3 and j == NT - 1), skip_group_check=True)
                    if step and m < 3:
                        last.then_inc(sem("ln_sq_used"), 1)
                return last

            LN_READ = ((sem("ln_cols"), 1), (sem("conv_centred"), 4), (sem("ln_cols"), 2), (sem("conv_normed"), 4))
            u = U["mlstm"]
            psum_free(pe, u)
            psum_free(pe, u + 1)
            psum_read(pe, U["vt"] + 2)
            pe.wait_ge(sem("v_ones"), 1)

            def weigh(hd, q):
                for e, (d, t0, t1) in STEPS[q]:
                    pe.wait_ge(sem("p_ready"), 16 * hd + e + 1)
                    for t in range(t0 // P, t1 // P):
                        b, c = divmod(6 * d + t, 3)
                        dst = acc[:, 0, b // 2, (b % 2) * 512 + c * VW:(b % 2) * 512 + (c + 1) * VW]
                        last = nc.tensor.matmul(dst, probs[e % 4][:, t * P - t0:t * P - t0 + P], v_tok[:, ORDER[q], hd, :],
                                                start=(q, d, t) == FIRST_TOUCH[b], stop=(q, d, t) == LAST_TOUCH[b],
                                                skip_group_check=True)
                    last.then_inc(sem("p_used"), 1)

            pending = None
            pe.wait_ge(sem("qkov_ready"), 1)
            for z, (kind, hd, q) in enumerate(ITEMS):
                if kind == "X" and pending:
                    weigh(*pending)
                    pending = None
                if z == len(ITEMS) - 1:
                    assert U["out0"] % 2 == 0
                    pe.wait_ge(sem("sums_read"), HEADS)
                    product(pe, U["out0"], G["out0"], h, h_tiles(1), parts=(0,))
                if z >= 2:
                    was, of, q_ = ITEMS[z - 2]
                    if was == "S":
                        pe.wait_ge(sem("p_ready"), 16 * of + STEPS[q_][-1][0] + 1)
                    elif was == "L":
                        pe.wait_ge(*LN_READ[q_])
                    else:
                        pe.wait_ge(sem("merged_ready"), of + 1)
                if kind == "S":
                    for t0, t1 in (SEGS[T] if ORDER[q] >= NL else SEGS[LAT]):
                        last = nc.tensor.matmul(acc[:, 1, z % 2, t0:t1], qkov[:, 4 + hd, ORDER[q] * P:(ORDER[q] + 1) * P],
                                                qkov[:, hd, t0:t1], start=True, stop=True)
                elif kind == "L":
                    last = conv_norm_step(q, z % 2)
                else:
                    pe.wait_ge(sem("hn_ready"), hd + 1)
                    for j in range(NT):
                        last = transpose(acc[:, 1, z % 2, j * P:(j + 1) * P], h_tok[:, j, :])
                if z < len(ITEMS) - 1:
                    last.then_inc(sem("slot_full"), 1)
                if pending:
                    if pending[1] == 0 and hd:
                        pe.wait_ge(sem("sums_read"), hd)
                    weigh(*pending)
                pending = (hd, q) if kind == "S" else None
            last.then_inc(unit_done, 2)

            def ffn_and_norms(l, tokens, diag_count, norm_of_y, norm_of_x, stage, hid0):
                norm_y(U[f"n{1 + 3 * l}"], norm_of_y, tokens, diag_count)
                norm_x(U[f"m{1 + 3 * l}"], norm_of_x, tokens, diag_count + 1)
                segs = SEGS[tokens]
                for g, size in enumerate(FFN_GROUPS):
                    with pe.Fori(0, size // 2) as i:
                        for j in range(2):
                            product(pe, U[f"up{l}{g}"] + j, G[f"up{l}{g}"] + 2 * j, h, always if g else h_tiles(stage),
                                    segs=segs, i=i, ada=None if l else ADA_UP[g][j])
                    with pe.Fori(0, 2) as i:
                        for j in range(2):
                            product(pe, U[f"down{l}{g}"] + j, G[f"down{l}{g}"] + 2 * j, (hid_hi, hid_lo),
                                    lambda k: pe.wait_ge(sem("hid_ready"), hid0 + k // 2 + 1), ktiles=size, segs=segs, i=i,
                                    ada=None if l else ADA_DOWN[g][j])
                    hid0 += size // 2
                norm_y(U[f"n{2 + 3 * l}"], norm_of_y + 1, tokens, diag_count + 2)

            for j in range(4):
                product(pe, U["out0"] + j, G["out0"] + 2 * j, h, h_tiles(1), parts=(0, 1) if j else (1,), ada=(4 + 2 * j, 0), pairs=2)
            ffn_and_norms(0, T, 4, 0, 1, 2, 0)
            norm_x(U["n3"], 2, T, 7)
            with pe.Fori(0, 2) as i:
                for j in range(2):
                    product(pe, U["in1"] + j, G["in1"] + 2 * j, h, h_tiles(3), segs=SEGS[LAT], i=i)
            product(pe, U["kin"], G["kin"], h, always)

            def head_sums(u, first_tile, end_tile):
                psum_free(pe, u)
                for m in range(first_tile, end_tile):
                    pe.wait_ge(sem("asq_ready"), m + 1)
                    tiles, first = (NL, NL * m) if m < N_Q else (NT, NT * (m - N_Q))
                    for j in range(tiles):
                        last = nc.tensor.matmul(acc[:, u % 2, 0, first + j:first + j + 1], asq[:, m % 2, j * P:(j + 1) * P],
                                                ones[:, 0:1], start=True, stop=True)
                    last.then_inc(sem("asq_used") if m < end_tile - 1 else unit_done, 1)

            def rotated(v):
                u = U[f"rot{v // 2 * 2}"] + v % 2
                psum_free(pe, u)
                for m in range(2):
                    x_ = inb[:, 2 + 2 * v + m, :] if v < 3 else kT[:, m, 0:LAT]
                    last = nc.tensor.matmul(acc[:, u % 2, m, 0:LAT], rotw[:, 1 + v // 3, :], x_, start=True, stop=True)
                last.then_inc(unit_done, 1)

            head_sums(U["qst"], 0, N_Q)
            pe.wait_ge(sem("rotw_ready"), 2)
            rotated(0)
            rotated(1)
            u = U["pool"]
            psum_free(pe, u)
            pe.wait_ge(sem("pooled"), 1)
            for m in range(2):
                last = nc.tensor.matmul(acc[:, u % 2, m, 0:LAT], poolw[:, m, :], pu[:, m, 8:8 + LAT], start=True, stop=True)
            last.then_inc(unit_done, 1)
            u, n = U["vin"], G["vin"]
            psum_free(pe, u)
            pe.wait_ge(low, n + 6)
            for j in range(NT):
                c = slice((j % 4) * 256, (j % 4) * 256 + 256)
                for k in range(KD):
                    slot = (n + k // 4) % 4
                    for q, (w, x) in enumerate(((w_hi, h_hi), (w_hi, h_lo), (w_lo, h_hi))):
                        last = nc.tensor.matmul(acc[:, u % 2, j // 4, c], x[:, k, j * P:(j + 1) * P], w[:, slot, k % 4, :],
                                                start=(k == 0 and q == 0), stop=(k == KD - 1 and q == 2))
            last.then_inc(unit_done, 1)
            head_sums(U["kst"], N_Q, N_Q + N_KV)
            rotated(2)
            rotated(3)
            u = U["kb"]
            psum_free(pe, u)
            pe.wait_ge(sem("kdiag_ready"), 2)
            for m in range(2):
                for t0, t1 in SEGS[T]:
                    last = nc.tensor.matmul(acc[:, u % 2, m, t0:t1], ones[:, :], adiag[:, m, t0:t1], start=True, stop=True)
            last.then_inc(unit_done, 1)
            u = U["att"]
            psum_free(pe, u)
            psum_free(pe, u + 1)
            pe.wait_ge(sem("qk_ready"), 1)

            def scores(n):
                hd, i = divmod(n, NL)
                if n >= 2:
                    pe.wait_ge(sem("score_exp"), n - 1)
                for t0, t1 in SEGS[T]:
                    last = nc.tensor.matmul(acc[:, 0, n % 2, t0:t1], inb[:, 2 + hd, i * P:(i + 1) * P],
                                            kT[:, hd // 3, t0:t1], start=True, stop=True)
                last.then_inc(sem("score_full"), 1)

            scores(0)
            scores(1)
            for n in range(N_Q * NL):
                hd, i = divmod(n, NL)
                pe.wait_ge(sem("pn_ready"), n + 1)
                if n >= 1:
                    pe.wait_ge(sem("pT_ready"), n)
                for j in range(NT):
                    last = transpose(acc[:, 1, 0, j * P:(j + 1) * P], ptile[:, n % 2, j * P:(j + 1) * P])
                last.then_inc(sem("pT_full"), 1)
                if n + 2 < N_Q * NL:
                    scores(n + 2)
                pe.wait_ge(sem("pT_ready"), n + 1)
                if hd >= 2 and i == 0:
                    pe.wait_ge(h_ready, KD * 4 + 2 + hd - 1)
                c = (hd % 2) * 512 + i * P
                for j in range(NT):
                    last = nc.tensor.matmul(acc[:, 1, 1, c:c + P], v1[:, j, (hd // 3) * HD:(hd // 3 + 1) * HD],
                                            pT[:, n % 2, j * P:(j + 1) * P], start=(j == 0), stop=(j == NT - 1))
                if n < N_Q * NL - 1:
                    last.then_inc(sem("pv_done"), 1)
            last.then_inc(unit_done, 2)
            for j in range(4):
                product(pe, U["out1"] + j, G["out1"] + 2 * j, h, h_tiles(4), segs=SEGS[LAT])
            ffn_and_norms(1, LAT, 8, 2, 3, 5, FT // 2)
            for v in range(2):
                u = U["outT"] + v
                psum_free(pe, u)
                for k in range(KD):
                    pe.wait_ge(x_new, 3 * KD + k + 1)
                    for m in range(2):
                        last = transpose(acc[:, u % 2, m, k * P:(k + 1) * P], xT[:, k, (2 * v + m) * P:(2 * v + m + 1) * P])
                last.then_inc(unit_done, 1)

        @block.scalar
        def _(act):
            sa = Steps(act, sem("act_step"))
            mods_flat = mods[:, :, :, :, :].rearrange("p l c k s -> p l (c k) s")

            def take_high(n, i=0):
                act.wait_ge(raw_full[n % 2], loaded(n, i))
                nc.scalar.activation(w_hi[:, n % 4], raw[:, n % 2], ACT.Copy).then_inc(high, 1)

            def next_high(u, n, i=0):
                if n + 2 < N_GRANULES:
                    act.wait_ge(unit_done, u + 2 * i)
                    take_high(n + 2, i)
                    take_high(n + 3, i)

            def take_ada(u, l, tile, i=0, per=4, tiles=2):
                vec = vec1 if l else vec0
                for q in range(tiles):
                    t = tile + q + per * i
                    last = nc.scalar.activation(mods_flat[:, l, bass.ds(t, 1), :],
                                                acc[:, u % 2, 0, 1008 + 2 * q:1010 + 2 * q].unsqueeze(1), ACT.Identity,
                                                bias=vec[:, bass.ds(t, 1)])
                last.then_inc(ada_out, 1)

            def square_x(first_new, norm, tokens):
                for m in range(KD):
                    if first_new is None:
                        psum_read(act, U["xt"] + m // 2)
                    else:
                        act.wait_ge(x_new, first_new + m + 1)
                    if m >= 2:
                        act.wait_ge(sq_used, 6 * norm + max(1, m - 2))
                    nc.scalar.activation(sq[:, m % 2, 0:tokens], xT[:, m, 0:tokens], ACT.Square).then_inc(sq_ready, 1)

            def square_y(u, norm, j, tokens):
                for m in (2 * j, 2 * j + 1):
                    if m == KD - 2:
                        act.wait_ge(sem("y_first"), norm + 1)
                    else:
                        psum_read(act, u)
                    if m >= 2:
                        act.wait_ge(sem("ysq_used"), 6 * norm + m - 1)
                    nc.scalar.activation(sq[:, m % 2, 0:tokens], y[:, m, 0:tokens], ACT.Square
                                         ).then_inc(sem("ysq_ready"), 1)

            def roots(idx, nt):
                act.wait_ge(recip, idx)
                nc.scalar.activation(st[:, 1, 0:nt], st[:, 0, 0:nt], ACT.Sqrt).then_inc(root, 1)

            def modulate(use, l, comp, tokens):
                for m in range(KD):
                    act.wait_ge(t_ready, KD * use + m + 1)
                    for s, (t0, t1) in enumerate(SEGS[tokens]):
                        last = nc.scalar.activation(h_hi[:, m, t0:t1], tbuf[:, m % 3, t0:t1], ACT.Identity,
                                                    bias=mods[:, l, comp, m, s:s + 1])
                    last.then_inc(t_high, 1)

            psum_full(act, U["cond"])
            nc.scalar.activation(cond[:, :, :].rearrange("p k s -> p s k"),
                                 acc[:, U["cond"] % 2, 0, 0:2 * KD].rearrange("p (s k) -> p s k", s=2), ACT.Silu
                                 ).then_inc(set_free[U["cond"] % 2], 1)
            psum_full(act, U["vec"])
            for dst, m, col, n in ((vec0[:, :], 0, 0, 92), (vec1[:, :], 0, 128, 84), (ffn_cw[:, 0, :], 0, 256, 66),
                                   (ffn_cw[:, 1, :], 0, 384, 66),
                                   (dw_w[:, :, :].rearrange("p w j -> p (w j)"), 1, 0, 124)):
                last = nc.scalar.activation(dst, acc[:, U["vec"] % 2, m, col:col + n], ACT.Copy)
            last.then_inc(set_free[U["vec"] % 2], 1)
            for v in range(4):
                u = U["xt"] + v
                psum_full(act, u)
                nc.scalar.activation(xT[:, 2 * v:2 * v + 2, :], acc[:, u % 2, :, 0:T], ACT.Copy).then_inc(set_free[u % 2], 1)
            square_x(None, 0, T)
            psum_full(act, U["ada"])
            take_high(0)
            take_high(1)
            roots(1, NT)
            modulate(0, 0, 0, T)
            act.wait_ge(sem("conv_zero"), 1)
            for i in range(2):
                u, n = U["conv"] + 2 * i, G["conv"] + 4 * i
                next_high(u, n)
                psum_full(act, u)
                if not i:
                    take_ada(u, 0, 16, tiles=4)
                nc.scalar.activation(sig_b[:, 2 * i:2 * i + 2, :], acc[:, u % 2, :, 0:T], ACT.Sigmoid
                                     ).then_inc(set_free[u % 2], 1)
                u, n = u + 1, n + 2
                next_high(u, n)
                psum_full(act, u)
                if not i:
                    take_ada(u, 0, 20, tiles=4)
                for (t0, t1), c in zip(SEGS[T], (U_LAT, U_CTX)):
                    last = nc.scalar.activation(conv_u[:, 2 * i + 1:2 * i + 3, c:c + t1 - t0], acc[:, u % 2, :, t0:t1],
                                                ACT.Copy)
                last.then_inc(set_free[u % 2], 1)
            u = U["gate"]
            next_high(u, G["gate"])
            psum_full(act, u)
            act.wait_ge(sem("gate_b_in"), 64)
            nc.scalar.activation(rows[0:8, 2, :], acc[32:40, u % 2, 0, 0:T], ACT.Copy)
            nc.scalar.activation(rows[0:8, 0, :], acc[0:8, u % 2, 0, 0:T], ACT.Identity, bias=gate_b[0:8, 0:1]
                                 ).then_inc(set_free[u % 2], 1)
            psum_read(act, u)
            sa.done(nc.scalar.activation(rows[0:8, 1, :], rows[0:8, 0, :], ACT.Abs))
            sa.wait()
            sa.done(nc.scalar.activation(rows[0:8, 1, :], rows[0:8, 1, :], ACT.Exp, scale=-1.0))
            sa.wait()
            nc.scalar.activation(rows[0:8, 1, :], rows[0:8, 1, :], ACT.Ln, bias=1.0).then_inc(sem("gate_log"), 1)
            for half in range(2):
                if half:
                    act.wait_ge(sem("sig_used"), 2)
                with act.Fori(0, 2) as i:
                    for j in range(2):
                        u, n = U["qkov"] + 4 * half + j, G["qkov"] + 8 * half + 2 * j
                        next_high(u, n, i)
                        psum_full(act, u, i)
                        nc.scalar.activation(qkov[:, bass.ds(4 * i + (8 * half + 2 * j), 2), :], acc[:, u % 2, :, 0:T], ACT.Copy
                                             ).then_inc(set_free[u % 2], 1)
            psum_read(act, U["qkov"] + 7)
            nc.scalar.activation(qkov[:, 12:16, :], qkov[:, 12:16, :], ACT.Sigmoid).then_inc(sem("qkov_ready"), 1)
            u = U["gcol"]
            psum_full(act, u)
            nc.scalar.activation(gcols[:, 0:2].rearrange("p x j r -> p (x j r)"), acc[:, u % 2, 0, 0:96], ACT.Copy)
            nc.scalar.activation(gcols[:, 2:4].rearrange("p x j r -> p (x j r)"), acc[:, u % 2, 0, 96:192], ACT.Exp,
                                 scale=-1.0).then_inc(set_free[u % 2], 1)
            act.wait_ge(sem("m_out"), 32)
            for v in range(3):
                u = U["vt"] + v
                psum_full(act, u)
                for m in range(2):
                    last = nc.scalar.activation(v_tok[:, 2 * v + m, :, 0:HD],
                                                acc[:, u % 2, m, 0:512].rearrange("p (h d) -> p h d", h=HEADS), ACT.Copy)
                last.then_inc(set_free[u % 2], 1)
            conv_segs = tuple(zip(SEGS[T], (HALF, U_CTX)))

            def conv_norm_squares():
                for t in range(4):
                    act.wait_ge(sem("conv_centred"), t + 1)
                    if t >= 2:
                        act.wait_ge(sem("ln_sq_used"), t - 1)
                    for (t0, t1), c in conv_segs:
                        last = nc.scalar.activation(ln_sq[:, t % 2, t0:t1], conv_u[:, t, c:c + t1 - t0], ACT.Square)
                    last.then_inc(sem("ln_sq_ready"), 1)

            def conv_norm_out():
                for t in range(4):
                    act.wait_ge(sem("conv_normed"), t + 1)
                    for (t0, t1), c in conv_segs:
                        last = nc.scalar.activation(conv_u[:, t, c:c + t1 - t0], conv_u[:, t, c:c + t1 - t0], ACT.Silu,
                                                    bias=vec0[:, 84 + t:85 + t], scale=vec0[:, 80 + t:81 + t])
                    sa.done(last)
                    sa.wait()
                    for (t0, t1), c in conv_segs:
                        last = nc.scalar.activation(h_hi[:, t, t0:t1], conv_u[:, t, c:c + t1 - t0], ACT.Copy)
                    last.then_inc(sem("mix_high"), 1)

            def finish(hd):
                act.wait_ge(sem("sums_read"), hd + 1)
                if not hd:
                    act.wait_ge(h_ready, KD + 4)
                for j in range(NT):
                    if hd and not j:
                        act.wait_ge(sem("hss_ready"), hd)
                    last = nc.scalar.activation(sq_junk[:, j, :], h_tok[:, j, :], ACT.Square, accum_out=hss[:, 0, j:j + 1])
                last.then_inc(sem("hss_ready"), 1)
                act.wait_ge(sem("hss_recip"), hd + 1)
                nc.scalar.activation(hss[:, 1, :], hss[:, 1, :], ACT.Sqrt).then_inc(sem("hss_root"), 1)

            def head_out(hd):
                act.wait_ge(sem("merged_ready"), hd + 1)
                nc.scalar.activation(h_hi[:, 4 + hd, :], merged[:, :], ACT.Copy).then_inc(sem("mix_high"), 1)

            for kind, hd, q in ITEMS:
                if kind == "L":
                    if q == 1:
                        conv_norm_squares()
                    elif q == 2:
                        roots(2, NT)
                    elif q == 3:
                        conv_norm_out()
                elif kind == "S":
                    if q == 0:
                        act.wait_ge(sem(f"m_in{hd % 2}"), 16 * (hd // 2 + 1))
                    for e, (d, t0, t1) in STEPS[q]:
                        if 16 * hd + e == 3:
                            act.wait_ge(sem("conv_done"), 1)
                        if 16 * hd + e >= 4:
                            act.wait_ge(sem("p_used"), 16 * hd + e - 3)
                        nc.scalar.activation(probs[e % 4][:, 0:t1 - t0], negM[:, hd % 2, d, t0:t1], ACT.Exp,
                                             bias=gcols[:, d, ORDER[q], hd + 4 * d:hd + 4 * d + 1]).then_inc(sem("e_ready"), 1)
                    if q == 0 and hd:
                        finish(hd - 1)
                    if q == 3 and hd:
                        head_out(hd - 1)
                    if q == 5:
                        act.wait_ge(sem("p_used"), 16 * (hd + 1))
                        nc.scalar.activation(den[:, 0], acc[:, 0].rearrange("p m (b c) -> p (m b) c", b=2)[:, :, HD:3 * VW:VW],
                                             ACT.Abs).then_inc(sem("den_abs"), 1)
                        if hd == HEADS - 1:
                            finish(hd)
                elif hd == HEADS - 1:
                    head_out(hd)

            def take_up(u, g, j, i):
                layer, tile, step = ADA_UP[g][j][2:]
                take_ada(u, layer, tile, i, 2 * step)

            def ffn(l, norm_y, norm, tokens, idx):
                segs = SEGS[tokens]
                nt = tokens // P
                roots(idx, nt)
                square_x(16 * l, norm, tokens)
                roots(idx + 1, nt)
                modulate(1 + 2 * l, l, 3, tokens)
                first_pair = FT // 2 * l
                act.wait_ge(sem("pads_zero"), l + 1)
                for g, size in enumerate(FFN_GROUPS):
                    with act.Fori(0, size // 2) as i:
                        u, n = U[f"up{l}{g}"], G[f"up{l}{g}"]
                        next_high(u, n, i)
                        psum_full(act, u, i)
                        act.wait_ge(sem("ffn_conv"), first_pair + 1 + i)
                        if not l:
                            take_up(u, g, 0, i)
                        for (t0, t1), c in zip(segs, (G_LAT, G_CTX)):
                            last = nc.scalar.activation(gpad[:, :, c:c + t1 - t0], acc[:, u % 2, :, t0:t1], ACT.Copy)
                        last.then_inc(set_free[u % 2], 1)
                        u, n = u + 1, n + 2
                        next_high(u, n, i)
                        act.wait_ge(sem("ffn_conv"), first_pair + 2 + i)
                        k = bass.ds(2 * i, 2)
                        nc.scalar.activation(hid[:, k, 0:tokens], hid[:, k, 0:tokens], ACT.Silu).then_inc(sem("ffn_silu"), 1)
                        if not l:
                            psum_full(act, u, i)
                            take_up(u, g, 1, i)
                        psum_read(act, u, i)
                        nc.scalar.activation(hid_hi[:, k, 0:tokens], hid[:, k, 0:tokens], ACT.Copy
                                             ).then_inc(sem("hid_high"), 1)
                    first_pair += size // 2
                    last_group = g == len(FFN_GROUPS) - 1

                    def down(j, i=0):
                        u, n = U[f"down{l}{g}"] + j, G[f"down{l}{g}"] + 2 * j
                        next_high(u, n, i)
                        if not l and ADA_DOWN[g][j % 2]:
                            psum_full(act, u, i)
                            layer, tile, step = ADA_DOWN[g][j % 2][2:]
                            take_ada(u, layer, tile, i, 2 * step)
                        return u

                    if last_group:
                        for j in range(4):
                            u = down(j)
                            square_y(u, norm_y, j, tokens)
                    else:
                        with act.Fori(0, 2) as i:
                            for j in range(2):
                                down(j, i)
                roots(idx + 2, nt)

            def mixer_out(l, norm_y, tokens):
                for j in range(4):
                    u, n = U[f"out{l}"] + j, G[f"out{l}"] + 2 * j
                    next_high(u, n)
                    if not l:
                        psum_full(act, u)
                        take_ada(u, 0, 24 + 4 * j, tiles=4)
                    square_y(u, norm_y, j, tokens)

            mixer_out(0, 0, T)
            ffn(0, 1, 1, T, 3)
            square_x(8, 2, T)
            roots(6, NT)
            modulate(2, 1, 0, T)
            with act.Fori(0, 2) as i:
                for j in range(2):
                    u, n = U["in1"] + j, G["in1"] + 2 * j
                    next_high(u, n, i)
                    psum_full(act, u, i)
                    nc.scalar.activation(inb[:, bass.ds(4 * i + 2 * j, 2), :], acc[:, u % 2, :, 0:LAT], ACT.Copy
                                         ).then_inc(set_free[u % 2], 1)
            def square_heads(first_tile, end_tile):
                for m in range(first_tile, end_tile):
                    if m == 7:
                        psum_full(act, U["qst"])
                    elif m >= 2:
                        act.wait_ge(sem("asq_used"), m - 1)
                    src, tokens = (inb[:, 2 + m, :], LAT) if m < N_Q else (kT[:, m - N_Q, :], T)
                    nc.scalar.activation(asq[:, m % 2, 0:tokens], src, ACT.Square).then_inc(sem("asq_ready"), 1)

            u = U["kin"]
            next_high(u, G["kin"])
            act.wait_ge(sem("tab_in"), 16 * 7)
            for q in range(2):
                nc.scalar.activation(rotw[:, 1 + q, :], rotw[:, 0, :], ACT.Copy, scale=vec1[:, 82 + q:83 + q]
                                     ).then_inc(sem("rotw_ready"), 1)
            psum_read(act, U["in1"] + 3)
            square_heads(0, 2)
            psum_full(act, u)
            nc.scalar.activation(kT[:, :, :], acc[:, u % 2, :, 0:T], ACT.Copy).then_inc(set_free[u % 2], 1)
            square_heads(2, N_Q)
            psum_read(act, U["kin"])
            u = U["vin"]
            next_high(u, G["vin"])
            square_heads(N_Q, N_Q + N_KV)
            psum_full(act, u)
            nc.scalar.activation(v1[:, 0:4, :], acc[:, u % 2, 0, :].rearrange("p (j c) -> p j c", c=256), ACT.Copy)
            nc.scalar.activation(v1[:, 4:6, :], acc[:, u % 2, 1, 0:512].rearrange("p (j c) -> p j c", c=256), ACT.Copy
                                 ).then_inc(set_free[u % 2], 1)
            act.wait_ge(recip, 7)
            nc.scalar.activation(acol[:, :], acol[:, :], ACT.Sqrt).then_inc(root, 1)
            act.wait_ge(sem("pool_float"), 1)
            nc.scalar.activation(h_hi[:, 0:2, 0:LAT], ps2[:, :, 0:LAT], ACT.Copy).then_inc(sem("pool_high"), 1)

            def head_high(hd):
                if hd < N_Q - 1:
                    act.wait_ge(sem("pv_done"), NL * (hd + 1))
                else:
                    psum_full(act, U["att"] + 1)
                c = (hd % 2) * 512
                nc.scalar.activation(h_hi[:, 2 + hd, 0:LAT], acc[:, 1, 1, c:c + 512], ACT.Copy).then_inc(sem("o_high"), 1)

            for n in range(N_Q * NL):
                hd, i_ = divmod(n, NL)
                act.wait_ge(sem("score_max"), n + 1)
                if n >= 2:
                    act.wait_ge(sem("pT_full"), n - 1)
                nc.scalar.activation(ptile[:, n % 2, :], acc[:, 0, n % 2, 0:T], ACT.Exp, bias=arow[:, n, 1:2],
                                     scale=acol[:, n:n + 1], accum_out=arow[:, n, 2:3]).then_inc(sem("score_exp"), 1)
                if i_ == 1 and hd:
                    head_high(hd - 1)
            head_high(N_Q - 1)
            mixer_out(1, 2, LAT)
            ffn(1, 3, 3, LAT, 8)
            for v in range(2):
                u = U["outT"] + v
                psum_full(act, u)
                for m in range(2):
                    nc.scalar.activation(o_tok[:, 2 * v + m, :], acc[:, u % 2, m, :], ACT.Copy).then_inc(sem("o_ready"), 1)

        @block.vector
        def _(dve):
            sd = Steps(dve, sem("dve_step"))
            mods_flat = mods[:, :, :, :, :].rearrange("p l c k s -> p l (c k) s")

            def vt(out_, in0, in1, op):
                return nc.vector.tensor_tensor(out_, in0, in1, op)

            def row_sums(w, dst, ready, signals):
                for k in range(KD):
                    if ready:
                        ready(k)
                    for c in range(2):
                        scale = cond[:, k, c:c + 1]
                        if not k:
                            ins = nc.vector.tensor_scalar(dst[:, c, :], w(k), scale, None, ALU.mult)
                        else:
                            if k - 1 in signals:
                                dve.wait_ge(*signals[k - 1])
                            else:
                                sd.wait(sd.value() - 1)
                            ins = nc.vector.scalar_tensor_tensor(dst[:, c, :], w(k), scale, dst[:, c, :], ALU.mult, ALU.add)
                        if k in signals and c:
                            ins.then_inc(signals[k][0], 1)
                        else:
                            sd.done(ins)

            def ada_sums(u, pair, i=0, per=2, pairs=1):
                if u is not None:
                    dve.wait_ge(unit_done, u + 2 * i)
                for x in range(pairs):
                    p_ = pair + x

                    def ready(k):
                        if k % 4 == 0:
                            dve.wait_ge(ada_full[k // 4], 16 * (p_ + 1) + 16 * per * i)

                    row_sums(lambda k: ada_w[:, k // 4, k % 4, :], (ada_acc, ada_acc_b)[x], ready,
                             {3: (ada_used, 2 * p_ + 3 + 2 * per * i), 7: (ada_used, 2 * p_ + 4 + 2 * per * i)})

            def gain_scale(l, comp, col):
                for s in range(2):
                    last = nc.vector.scalar_tensor_tensor(mods[:, l, comp, :, s], mods[:, l, comp, :, s], 1.0,
                                                          (vec1 if l else vec0)[:, col:col + KD], ALU.add, ALU.mult)
                return last

            def gain_gate(l, comp, col):
                for s in range(2):
                    last = vt(mods[:, l, comp, :, s], mods[:, l, comp, :, s], (vec1 if l else vec0)[:, col:col + KD], ALU.mult)
                return last

            def to_diagonals(dst, cols, nt, signal):
                vt(dst[:, 0:nt * P].rearrange("p (j t) -> p j t", t=P), ident[:, :].unsqueeze(1).to_broadcast([P, nt, P]),
                   cols[:, 0:nt].unsqueeze(2).to_broadcast([P, nt, P]), ALU.mult).then_inc(signal, 1)

            def root_means(u, idx, nt, scale, dst):
                psum_full(dve, u)
                nc.vector.tensor_scalar(st[:, 0, 0:nt], acc[:, u % 2, 0, 0:nt], scale, EPS, ALU.mult, ALU.add
                                        ).then_inc(set_free[u % 2], 1)
                psum_read(dve, u)
                nc.vector.reciprocal(st[:, 0, 0:nt], st[:, 0, 0:nt]).then_inc(recip, 1)
                dve.wait_ge(root, idx)
                to_diagonals(dst, st[:, 1], nt, diag_ready)

            def give_back(u):
                nc.vector.tensor_copy(mark[:, u % 2:u % 2 + 1], acc[:, u % 2, 0, 0:1]).then_inc(set_free[u % 2], 1)

            def normed(u, use, stage, tokens, l, comp):
                psum_full(dve, u)

                def low_part(m):
                    dve.wait_ge(t_high, KD * use + m + 1)
                    for s, (t0, t1) in enumerate(SEGS[tokens]):
                        last = nc.vector.scalar_tensor_tensor(h_lo[:, m, t0:t1], tbuf[:, m % 3, t0:t1], mods[:, l, comp, m, s:s + 1],
                                                              h_hi[:, m, t0:t1].bitcast(F32), ALU.add, ALU.subtract)
                    last.then_inc(h_ready, 1)

                for m in range(KD):
                    if m >= 3:
                        dve.wait_ge(h_ready, KD * stage + m - 2)
                    for s, (t0, t1) in enumerate(SEGS[tokens]):
                        last = nc.vector.scalar_tensor_tensor(tbuf[:, m % 3, t0:t1], xT[:, m, t0:t1],
                                                              mods[:, l, comp + 1, m, s:s + 1], acc[:, u % 2, 0, t0:t1],
                                                              ALU.mult, ALU.mult)
                    last.then_inc(t_ready, 1)
                    if m == KD - 1:
                        give_back(u)
                    if m:
                        low_part(m - 1)
                low_part(KD - 1)

            def residual(u, l, comp, tokens):
                psum_full(dve, u)

                def add(m, value):
                    sd.wait(value)
                    for s, (t0, t1) in enumerate(SEGS[tokens]):
                        last = nc.vector.scalar_tensor_tensor(xT[:, m, t0:t1], y[:, m, t0:t1], mods[:, l, comp, m, s:s + 1],
                                                              xT[:, m, t0:t1], ALU.mult, ALU.add)
                    last.then_inc(x_new, 1)

                before = None
                for m in range(KD):
                    value = sd.done(vt(y[:, m, 0:tokens], y[:, m, 0:tokens], acc[:, u % 2, 0, 0:tokens], ALU.mult))
                    if m:
                        add(m - 1, before)
                    before = value
                add(KD - 1, before)
                give_back(u)

            def y_unit(u, tiles, tokens, add, i=0, adas=0, per=2):
                psum_full(dve, u, i)
                if adas:
                    dve.wait_ge(ada_out, adas + per * i)
                dst = y[:, tiles, 0:tokens]
                src = acc[:, u % 2, :, 0:tokens]
                (vt(dst, src, dst, ALU.add) if add else nc.vector.tensor_copy(dst, src)).then_inc(set_free[u % 2], 1)

            def y_last(u, tokens, add, adas):
                psum_full(dve, u)
                if adas:
                    dve.wait_ge(ada_out, adas)
                for m in range(2):
                    dst, src = y[:, KD - 2 + m, 0:tokens], acc[:, u % 2, m, 0:tokens]
                    (vt(dst, src, dst, ALU.add) if add else nc.vector.tensor_copy(dst, src)
                     ).then_inc(set_free[u % 2] if m else sem("y_first"), 1)

            def add_squares(norm, m, tokens):
                dve.wait_ge(sem("ysq_ready"), KD * norm + m + 1)
                if m:
                    dve.wait_ge(sem("ysq_used"), 6 * norm + m)
                    ins = vt(sumsq[:, 0:tokens], sumsq[:, 0:tokens], sq[:, m % 2, 0:tokens], ALU.add)
                else:
                    ins = nc.vector.tensor_copy(sumsq[:, 0:tokens], sq[:, m % 2, 0:tokens])
                ins.then_inc(sem("ysq_used"), 1)

            def y_units(first, norm, tokens, add, adas=None):
                if adas:
                    ada_sums(first, 4, pairs=2)
                for j in range(4):
                    if j < 3:
                        y_unit(first + j, slice(2 * j, 2 * j + 2), tokens, add, adas=adas[j] if adas else 0)
                        if adas:
                            ada_sums(first + j + 1, 6 + 2 * j, pairs=2)
                        add_squares(norm, 2 * j, tokens)
                        add_squares(norm, 2 * j + 1, tokens)
                    else:
                        y_last(first + j, tokens, add, adas[j] if adas else 0)

            nc.vector.memset(ones[:, :], 1.0).then_inc(sem("ones_set"), 1)
            nc.vector.memset(mark[:, 0:1], 0.0).then_inc(set_free[0], 1)
            nc.vector.memset(mark[:, 1:2], 0.0).then_inc(set_free[1], 1)
            nc.vector.memset(mods[:, 1, 0, 0, :], 0.0).then_inc(sem("ffn_conv"), 1)
            psum_read(dve, U["cond"])
            for n, q in enumerate(BY_DVE):
                dve.wait_ge(ada0_in[q], 16)
                row_sums(lambda k: ada_0[:, q, k, :], ada_acc0[:, q], None, {KD - 1: (ada0_sums, n + 1)})
            ada_sums(None, 0, pairs=2)
            u = U["ada"]
            psum_full(dve, u)
            psum_read(dve, U["vec"])
            for s in range(2):
                last = vt(mods_flat[:, 0, 0:16, s], acc[:, u % 2, 0, s:32:2], vec0[:, 0:16], ALU.add)
            last.then_inc(set_free[u % 2], 1)
            psum_read(dve, u)
            sd.done(gain_scale(0, 1, 48))
            sd.wait()
            root_means(U["n0"], 1, NT, 1.0 / D, diag)
            normed(U["n0"] + 1, 0, 0, T, 0, 0)

            taps_len = LAT + HALF + CTX

            def gate_inputs(first):
                for t in (first, first + 1):
                    for (t0, t1), c in zip(SEGS[T], (U_LAT, U_CTX)):
                        last = vt(conv_u[:, t + 1, c:c + t1 - t0], conv_u[:, t + 1, c:c + t1 - t0], sig_b[:, t, t0:t1], ALU.mult)
                last.then_inc(sem("sig_used"), 1)

            def conv_pair(first):
                dve.wait_ge(sem("sig_used"), first // 2 + 1)
                with dve.Fori(0, 2) as t:
                    sd.loop(t, TAPS)
                    dst = conv_u[:, bass.ds(t + first, 1), HALF:HALF + taps_len]
                    for w in range(TAPS):
                        src = conv_u[:, bass.ds(t + (first + 1), 1), w:w + taps_len]
                        sd.wait()
                        tap = dw_w[:, w, bass.ds(t + first, 1)]
                        if w == 0:
                            ins = nc.vector.tensor_scalar(dst, src, tap, None, ALU.mult)
                        else:
                            ins = nc.vector.scalar_tensor_tensor(dst, src, tap, dst, ALU.mult, ALU.add)
                        sd.done(ins)
                    sd.end(2)
                sd.wait()

            ada_sums(U["conv"] + 1, 2, pairs=2)
            psum_read(dve, U["conv"] + 1)
            gate_inputs(0)
            conv_pair(0)
            psum_read(dve, U["conv"] + 3)
            gate_inputs(2)
            r8 = [rows[0:8, q, :] for q in range(6)]
            lat, con = slice(0, LAT), slice(LAT, T)
            dve.wait_ge(sem("gate_log"), 1)
            sd.done(nc.vector.scalar_tensor_tensor(r8[0], r8[0], 0.0, r8[1], ALU.min, ALU.subtract))
            sd.wait()

            def scan(dst, src, op, other):
                sd.done(nc.vector.tensor_tensor_scan(dst[0][:, con], src[0][:, con], src[0][:, con], 0.0, op, other))
                back = sd.done(nc.vector.tensor_tensor_scan(dst[1][:, ::-1], src[1][:, ::-1], src[1][:, ::-1], 0.0, op, other))
                sd.wait(back)
                sd.done(nc.vector.tensor_tensor_scan(dst[0][:, lat], src[0][:, lat], src[0][:, lat],
                                                     dst[0][:, T - 1:T], op, other))
                sd.wait()

            scan((r8[3], r8[4]), (r8[0], r8[0]), ALU.add, ALU.bypass)
            b_i = gate_b[0:8, 1:2]
            sd.done(nc.vector.scalar_tensor_tensor(r8[5], r8[2], b_i, r8[3], ALU.add, ALU.subtract))
            sd.done(nc.vector.scalar_tensor_tensor(r8[0], r8[2], b_i, r8[4], ALU.add, ALU.subtract))
            sd.wait()
            scan((r8[1], r8[2]), (r8[5], r8[0]), ALU.max, ALU.bypass)
            sd.done(vt(r8[3], r8[3], r8[1], ALU.add))
            sd.done(vt(r8[4], r8[4], r8[2], ALU.add))
            sd.wait()
            nc.vector.tensor_scalar(r8[1], r8[1], -1.0, None, ALU.mult)
            nc.vector.tensor_scalar(r8[2], r8[2], -1.0, None, ALU.mult).then_inc(sem("rows_ready"), 1)
            conv_pair(2)
            nc.vector.tensor_copy(mark[:, 2:3], ident[:, 0:1]).then_inc(sem("conv_done"), 1)
            conv_segs = tuple(zip(SEGS[T], (HALF, U_CTX)))

            def conv_norm(step, slot):
                if step % 2 == 0:
                    scale_, eps = 1.0 / 512, (EPS if step else 0.0)
                    nc.vector.tensor_scalar(st[:, 0 if step else 1, 0:NT], acc[:, 1, slot, 0:NT], scale_, eps, ALU.mult, ALU.add
                                            ).then_inc(sem("ln_cols"), 1)
                    dve.wait_ge(sem("ln_cols"), 1 + step // 2)
                    if step:
                        nc.vector.reciprocal(st[:, 0, 0:NT], st[:, 0, 0:NT]).then_inc(recip, 1)
                        dve.wait_ge(root, 2)
                    to_diagonals(ln_diag, st[:, 1], NT, diag_ready)
                    return
                op, signal = ((ALU.subtract, sem("conv_centred")), (ALU.mult, sem("conv_normed")))[step // 2]
                for t in range(4):
                    for (t0, t1), c in conv_segs:
                        x_ = conv_u[:, t, c:c + t1 - t0]
                        last = vt(x_, x_, acc[:, 1, slot, t0:t1], op)
                    last.then_inc(signal, 1)

            scale = float(HD) ** -0.5
            masked = 0
            for z, (kind, hd, q) in enumerate(ITEMS):
                if z < len(ITEMS) - 1:
                    dve.wait_ge(sem("slot_full"), z + 1)
                else:
                    psum_full(dve, U["mlstm"] + 1)
                if kind == "X":
                    if hd:
                        dve.wait_ge(h_ready, KD + 4 + hd)
                    nc.vector.scalar_tensor_tensor(merged[:, :], acc[:, 1, z % 2, 0:T], vec0[:, 88 + hd:89 + hd],
                                                   qkov[:, 12 + hd, :], ALU.mult, ALU.mult).then_inc(sem("merged_ready"), 1)
                    continue
                if kind == "L":
                    conv_norm(q, z % 2)
                    continue
                for e, (d, t0, t1) in STEPS[q]:
                    e += 16 * hd
                    s_tile = ORDER[q]
                    if t0 <= s_tile * P < t1:
                        masked += 1
                        dve.wait_ge(sem("e_masked"), masked)
                    else:
                        dve.wait_ge(sem("e_ready"), e + 1)
                    p_ = probs[e % 4][:, 0:t1 - t0]
                    nc.vector.scalar_tensor_tensor(p_, acc[:, 1, z % 2, t0:t1], scale, p_, ALU.mult, ALU.mult
                                                   ).then_inc(sem("p_ready"), 1)
                if q == 5:
                    dve.wait_ge(sem("den_abs"), hd + 1)
                    for d in range(2):
                        sd.done(vt(den[:, 1].rearrange("p b c -> p (b c)")[:, 6 * d:6 * d + 6],
                                   den[:, 0].rearrange("p b c -> p (b c)")[:, 6 * d:6 * d + 6],
                                   gcols[:, 2 + d, :, hd + 4 * d], ALU.max))
                    sd.wait()
                    sd.done(nc.vector.reciprocal(den[:, 1], den[:, 1]))
                    sd.wait()
                    w_ = den[:, 1].rearrange("p b c -> p (b c)")

                    def sums(d, t):
                        b, c = divmod(6 * d + t, 3)
                        c = (b % 2) * 512 + c * VW
                        return acc[:, 0, b // 2, c:c + HD]

                    if hd:
                        dve.wait_ge(sem("merged_ready"), hd)
                    forward = acc[:, 0, 0, :].rearrange("p (b x) -> p b x", b=2)[:, :, 0:3 * VW].rearrange(
                        "p b (c v) -> p b c v", v=VW)[:, :, :, 0:HD]
                    sd.done(vt(h_tok[:, :, :].rearrange("p (b c) t -> p b c t", b=2), forward,
                               w_[:, 0:NT].rearrange("p (b c) -> p b c", b=2).unsqueeze(3).to_broadcast([P, 2, 3, HD]), ALU.mult))
                    sd.wait()
                    for t in range(NT):
                        last = nc.vector.scalar_tensor_tensor(h_tok[:, t, :], sums(1, t), w_[:, 6 + t:7 + t], h_tok[:, t, :],
                                                              ALU.mult, ALU.add)
                    last.then_inc(sem("sums_read"), 1)
                    if hd < HEADS - 1:
                        continue
                if (q == 0 and hd) or q == 5:
                    of = hd if q == 5 else hd - 1
                    dve.wait_ge(sem("hss_ready"), of + 1)
                    sd.done(nc.vector.tensor_scalar(hss[:, 1, :], hss[:, 0, :], 1.0 / HD, EPS, ALU.mult, ALU.add))
                    sd.wait()
                    nc.vector.reciprocal(hss[:, 1, :], hss[:, 1, :]).then_inc(sem("hss_recip"), 1)
                    dve.wait_ge(sem("hss_root"), of + 1)
                    vt(h_tok[:, :, :], h_tok[:, :, :], hss[:, 1, :].unsqueeze(2).to_broadcast([P, NT, P]), ALU.mult
                       ).then_inc(sem("hn_ready"), 1)
            dve.wait_ge(sem("merged_ready"), HEADS)
            nc.vector.tensor_copy(mark[:, 3:4], ident[:, 0:1]).then_inc(set_free[0], 1)
            nc.vector.tensor_copy(mark[:, 4:5], ident[:, 0:1]).then_inc(set_free[1], 1)

            def ffn(l, norm, tokens, idx, stage):
                segs = tuple(zip(SEGS[tokens], (G_LAT, G_CTX)))
                nt = tokens // P
                root_means(U[f"n{1 + 3 * l}"], idx, nt, 1.0 / D, diag)
                if not l:
                    dve.wait_ge(ada_out, 6)
                    last = gain_gate(0, 2, 56)
                    last = gain_scale(0, 4, 64)
                else:
                    last = gain_gate(1, 2, 56)
                    last = gain_scale(1, 4, 64)
                    last = gain_gate(1, 5, 72)
                sd.done(last)
                residual(U[f"n{1 + 3 * l}"] + 1, l, 2, tokens)
                root_means(U[f"m{1 + 3 * l}"], idx + 1, nt, 1.0 / D, diag)
                normed(U[f"m{1 + 3 * l}"] + 1, 1 + 2 * l, stage, tokens, l, 3)
                for c in (0, LAT + 1, T + 2):
                    last = nc.vector.memset(gpad[:, :, c:c + 1], 0.0)
                last.then_inc(sem("pads_zero"), 1)
                tile, pair, adas = 0, FT // 2 * l, 6
                for g, size in enumerate(FFN_GROUPS):
                    with dve.Fori(0, size // 2) as i:
                        sd.loop(i, 5 if l else 5 + 2 * 14)
                        u = U[f"up{l}{g}"]
                        if not l:
                            ada_sums(u, ADA_UP[g][0][0], i)
                        psum_read(dve, u, i)
                        for w in range(3):
                            for m in range(2):
                                c = ffn_cw[:, l, bass.ds(2 * i + (w * FT + tile + m), 1)]
                                if w:
                                    sd.wait(sd.value() - 1)
                                for (t0, t1), c0 in segs:
                                    src = gpad[:, m, c0 - 1 + w:c0 - 1 + w + t1 - t0]
                                    dst = hid[:, bass.ds(2 * i + m, 1), t0:t1]
                                    if w:
                                        ins = nc.vector.scalar_tensor_tensor(dst, src, c, dst, ALU.mult, ALU.add)
                                    else:
                                        ins = nc.vector.tensor_scalar(dst, src, c, None, ALU.mult)
                                if w == 2 and m:
                                    ins.then_inc(sem("ffn_conv"), 1)
                                else:
                                    sd.done(ins)
                        u += 1
                        if not l:
                            ada_sums(u, ADA_UP[g][1][0], i)
                        psum_full(dve, u, i)
                        dve.wait_ge(sem("ffn_silu"), pair + 1 + i)
                        if not l:
                            dve.wait_ge(ada_out, adas + 2 + 2 * i)
                        k = bass.ds(2 * i, 2)
                        hid_ = hid[:, k, 0:tokens]
                        vt(hid_, hid_, acc[:, u % 2, :, 0:tokens], ALU.mult).then_inc(set_free[u % 2], 1)
                        dve.wait_ge(sem("hid_high"), pair + 1 + i)
                        vt(hid_lo[:, k, 0:tokens], hid_, hid_hi[:, k, 0:tokens].bitcast(F32), ALU.subtract
                           ).then_inc(sem("hid_ready"), 1)
                        sd.end(size // 2)
                    tile += size
                    pair += size // 2
                    adas += size
                    first = U[f"down{l}{g}"]
                    if g == len(FFN_GROUPS) - 1:
                        y_units(first, norm + 1, tokens, True)
                    else:
                        with dve.Fori(0, 2) as i:
                            carry = [ADA_DOWN[g][j] if not l else None for j in range(2)]
                            count = sum(x is not None for x in carry)
                            sd.loop(i, 14 * count)
                            for j in range(2):
                                if carry[j]:
                                    ada_sums(first + j, carry[j][0], i, count)
                                y_unit(first + j, bass.ds(4 * i + 2 * j, 2), tokens, g > 0, i,
                                       adas + 1 + j if carry[j] else 0, count)
                            sd.end(2)
                        adas += 2 * count
                if not l:
                    sd.done(gain_gate(0, 5, 72))
                root_means(U[f"n{2 + 3 * l}"], idx + 2, nt, 1.0 / D, diag)
                residual(U[f"n{2 + 3 * l}"] + 1, l, 5, tokens)

            y_units(U["out0"], 0, T, False, adas=(3, 4, 5, 6))
            ffn(0, 0, T, 3, 2)
            dve.wait_ge(ada_out, 34)
            sd.done(gain_scale(1, 1, 48))
            sd.wait()
            root_means(U["n3"], 6, NT, 1.0 / D, diag)
            normed(U["n3"] + 1, 2, 3, T, 1, 0)
            nc.vector.memset(poolw[:, :, :], 0.0).then_inc(sem("poolw_zero"), 1)
            sd.done(nc.vector.memset(pu[:, :, :], 0.0))
            sd.wait()
            psum_read(dve, U["in1"])
            sd.done(nc.vector.tensor_copy(pu[:, :, 8:8 + LAT], inb[:, 0:2, :]))
            sd.wait()
            sd.done(vt(ps2[:, :, 1:PW], pu[:, :, 0:PW - 1], pu[:, :, 1:PW], ALU.add))
            sd.wait()
            sd.done(vt(ps4[:, :, 2:PW - 1], ps2[:, :, 1:PW - 2], ps2[:, :, 3:PW], ALU.add))
            sd.wait()
            c8 = slice(8, 8 + LAT)
            dve.wait_ge(sem("tab_in"), 16 * 7)
            sd.done(vt(ps2[0:64, 0, c8], ps2[0:64, 0, c8], icnt[0:64, 0, :], ALU.mult))
            sd.done(vt(ps2[64:128, 0, c8], ps4[64:128, 0, c8], icnt[64:128, 0, :], ALU.mult))
            sd.done(vt(ps2[:, 1, 4:PW - 3], ps4[:, 1, 2:PW - 5], ps4[:, 1, 6:PW - 1], ALU.add))
            sd.wait()
            sd.done(vt(ps4[:, 1, c8], ps2[:, 1, 4:4 + LAT], ps2[:, 1, 12:12 + LAT], ALU.add))
            sd.wait()
            sd.done(vt(ps4[64:128, 1, c8], ps4[64:128, 1, c8], icnt[64:128, 1, :], ALU.mult))
            sd.done(vt(ps4[0:64, 1, c8], ps2[0:64, 1, c8], icnt[0:64, 1, :], ALU.mult))
            sd.wait()
            vt(pu[:, 0, c8], ps2[:, 0, c8], pu[:, 0, c8], ALU.subtract)
            vt(pu[:, 1, c8], ps4[:, 1, c8], pu[:, 1, c8], ALU.subtract).then_inc(sem("pooled"), 1)

            def head_means(u, cols):
                psum_full(dve, u)
                nc.vector.tensor_scalar(acol[:, cols], acc[:, u % 2, 0, 0:cols.stop - cols.start], 1.0 / HD, EPS, ALU.mult, ALU.add
                                        ).then_inc(set_free[u % 2], 1)

            def rotary(v):
                u = U[f"rot{v // 2 * 2}"] + v % 2
                psum_full(dve, u)
                for m in range(2):
                    x_ = inb[:, 2 + 2 * v + m, :] if v < 3 else kT[:, m, 0:LAT]
                    g = vec1[:, 82 + v // 3:83 + v // 3]
                    sd.done(vt(rt1[:, m, :], acc[:, u % 2, m, 0:LAT], rope[:, 1, :], ALU.mult))
                    sd.done(nc.vector.scalar_tensor_tensor(x_, x_, g, rope[:, 0, :], ALU.mult, ALU.mult))
                    sd.wait()
                    last = vt(x_, x_, rt1[:, m, :], ALU.add)
                last.then_inc(set_free[u % 2], 1)
                psum_read(dve, u)

            head_means(U["qst"], slice(0, NL * N_Q))
            rotary(0)
            rotary(1)
            u = U["pool"]
            psum_full(dve, u)
            for m in range(2):
                last = nc.vector.tensor_scalar(ps2[:, m, 0:LAT], acc[:, u % 2, m, 0:LAT], vec1[:, 80 + m:81 + m], None, ALU.mult)
            last.then_inc(set_free[u % 2], 1)
            psum_read(dve, u)
            nc.vector.tensor_copy(mark[:, 6:7], ident[:, 0:1]).then_inc(sem("pool_float"), 1)
            head_means(U["kst"], slice(NL * N_Q, 36))
            psum_read(dve, U["kst"])
            nc.vector.reciprocal(acol[:, :], acol[:, :]).then_inc(recip, 1)
            rotary(2)
            dve.wait_ge(root, 7)
            for m in range(2):
                c = NL * N_Q + NT * m
                vt(adiag[:, m, :].rearrange("p (j t) -> p j t", t=P), ident[:, :].unsqueeze(1).to_broadcast([P, NT, P]),
                   acol[:, c:c + NT].unsqueeze(2).to_broadcast([P, NT, P]), ALU.mult).then_inc(
                       sem("kdiag_ready"), 1)
            rotary(3)
            sd.done(nc.vector.tensor_scalar(kT[:, :, LAT:T], kT[:, :, LAT:T], vec1[:, 83:84], None, ALU.mult))
            sd.done(nc.vector.tensor_scalar(acol[:, 0:NL * N_Q], acol[:, 0:NL * N_Q], scale, None, ALU.mult))
            sd.wait()
            u = U["kb"]
            psum_full(dve, u)
            nc.vector.tensor_tensor(kT[:, :, :], kT[:, :, :], acc[:, u % 2, :, 0:T], ALU.mult).then_inc(set_free[u % 2], 1)
            psum_read(dve, u)
            nc.vector.tensor_copy(mark[:, 5:6], ident[:, 0:1]).then_inc(sem("qk_ready"), 1)
            dve.wait_ge(sem("pool_high"), 1)
            vt(h_lo[:, 0:2, 0:LAT], ps2[:, :, 0:LAT], h_hi[:, 0:2, 0:LAT].bitcast(F32), ALU.subtract).then_inc(h_ready, 2)

            def head_low(hd):
                dve.wait_ge(sem("o_high"), hd + 1)
                c = (hd % 2) * 512
                vt(h_lo[:, 2 + hd, 0:LAT], acc[:, 1, 1, c:c + 512], h_hi[:, 2 + hd, 0:LAT].bitcast(F32), ALU.subtract
                   ).then_inc(h_ready, 1)

            for n in range(N_Q * NL + 1):
                if n < N_Q * NL:
                    dve.wait_ge(sem("score_full"), n + 1)
                    sd.done(nc.vector.reduce_max(arow[:, n, 0:1], acc[:, 0, n % 2, 0:T], AX.X))
                    sd.wait()
                    nc.vector.tensor_scalar(arow[:, n, 1:2], arow[:, n, 0:1], acol[:, n:n + 1], -1.0, ALU.mult, ALU.mult
                                            ).then_inc(sem("score_max"), 1)
                if n >= 1:
                    dve.wait_ge(sem("pT_full"), n)
                    if n >= 3:
                        dve.wait_ge(sem("pv_done"), n - 2)
                    nc.vector.tensor_copy(pT[:, (n - 1) % 2, :], acc[:, 1, 0, 0:T]).then_inc(sem("pT_ready"), 1)
                if n < N_Q * NL:
                    dve.wait_ge(sem("score_exp"), n + 1)
                    sd.done(nc.vector.reciprocal(arow[:, n, 3:4], arow[:, n, 2:3]))
                    sd.wait()
                    nc.vector.tensor_scalar(ptile[:, n % 2, :], ptile[:, n % 2, :], arow[:, n, 3:4], None, ALU.mult
                                            ).then_inc(sem("pn_ready"), 1)
                    if n % NL == 2 and n > NL:
                        head_low(n // NL - 1)
            head_low(N_Q - 1)
            dve.wait_ge(h_ready, 5 * KD)
            nc.vector.tensor_copy(mark[:, 7:8], ident[:, 0:1]).then_inc(set_free[0], 1)
            nc.vector.tensor_copy(mark[:, 8:9], ident[:, 0:1]).then_inc(set_free[1], 1)
            y_units(U["out1"], 2, LAT, False)
            ffn(1, 2, LAT, 8, 5)

        @block.gpsimd
        def _(pool):
            def take_low(n, i=0):
                pool.wait_ge(high, n + 1 + 4 * i)
                nc.gpsimd.tensor_tensor(w_lo[:, n % 4], raw[:, n % 2], w_hi[:, n % 4].bitcast(F32), ALU.subtract).then_inc(low, 1)

            def take_lows(first, turns):
                with pool.Fori(0, turns) as i:
                    for j in range(4):
                        take_low(first + j, i)

            def sum_squares(norm, tokens):
                for m in range(1, KD - 1):
                    pool.wait_ge(sq_ready, KD * norm + m + 1)
                    if m > 1:
                        pool.wait_ge(sq_used, 6 * norm + m - 1)
                    one = sq[:, 0, 0:tokens] if m == 1 else sumsq[:, 0:tokens]
                    nc.gpsimd.tensor_tensor(sumsq[:, 0:tokens], one, sq[:, m % 2, 0:tokens], ALU.add).then_inc(sq_used, 1)

            nc.gpsimd.memset(mark[:, 9:10], 0.0).then_inc(low, 4)
            nc.gpsimd.memset(mark[:, 10:11], 0.0).then_inc(ada_used, 2)
            sum_squares(0, T)
            take_low(0)
            take_low(1)
            pool.wait_ge(unit_done, U["n0"] + 2)
            nc.gpsimd.memset(conv_u[:, :, :], 0.0).then_inc(sem("conv_zero"), 1)
            n = G["conv"] + 2
            take_lows(n, 2)
            take_low(n + 8)
            take_low(n + 9)
            take_lows(n + 10, 4)
            pool.wait_ge(unit_done, U["gcol"] + 1)
            pool.wait_ge(sem("m_out"), 32)
            nc.gpsimd.memset(v_tok[:, :, :, HD:VW], 1.0).then_inc(sem("v_ones"), 1)
            for kind, hd, q in ITEMS:
                if kind == "L":
                    for t in range(4 if q == 3 else 0):
                        pool.wait_ge(sem("mix_high"), t + 1)
                        for (t0, t1), c in zip(SEGS[T], (HALF, U_CTX)):
                            last = nc.gpsimd.tensor_tensor(h_lo[:, t, t0:t1], conv_u[:, t, c:c + t1 - t0],
                                                           h_hi[:, t, t0:t1].bitcast(F32), ALU.subtract)
                        last.then_inc(h_ready, 1)
                    continue
                if kind == "S":
                    s_tile = ORDER[q]
                    for e, (d, t0, t1) in STEPS[q]:
                        if t0 <= s_tile * P < t1:
                            pool.wait_ge(sem("e_ready"), 16 * hd + e + 1)
                            block_ = probs[e % 4][:, s_tile * P - t0:s_tile * P - t0 + P]
                            sign = -1 if d else 1
                            nc.gpsimd.affine_select(out=block_, in_=block_, compare_op=ALU.is_ge, fill=0.0, base=0,
                                                    pattern=[[sign, P]], channel_multiplier=-sign).then_inc(sem("e_masked"), 1)
                of = hd - 1 if (kind, q) == ("S", 3) else hd if (kind, hd) == ("X", HEADS - 1) else -1
                if of >= 0:
                    pool.wait_ge(sem("mix_high"), 5 + of)
                    nc.gpsimd.tensor_tensor(h_lo[:, 4 + of, :], merged[:, :], h_hi[:, 4 + of, :].bitcast(F32), ALU.subtract
                                            ).then_inc(h_ready, 1)
            take_lows(G["out0"] + 2, 2)
            sum_squares(1, T)
            take_lows(G["up00"] + 2, 17)
            sum_squares(2, T)
            take_lows(G["in1"] + 2, 3)
            take_lows(G["out1"] + 2, 2)
            sum_squares(3, LAT)
            take_lows(G["up10"] + 2, 16)
            take_low(N_GRANULES - 2)
            take_low(N_GRANULES - 1)



_INS = ("x", "c", "ctx", "c_ctx", "ada_w", "ada_b", "mix_pre_g", "mix_post_g", "ffn_pre_g", "ffn_post_g", "ffn_w_in",
        "ffn_conv_w", "ffn_w_out", "even_w_in", "even_w_out", "conv_dw_w", "conv_ln_g", "conv_ln_b", "mlstm_gate_b",
        "mlstm_norm_g", "odd_w_in", "odd_w_out", "pool_w", "pool_scale", "q_norm_g", "k_norm_g")


def constants():
    freq = HD // 4
    inv = (10000.0 ** (-np.arange(freq, dtype=np.float32) / np.float32(freq))).astype(np.float32)
    t = np.arange(LAT)
    row, col = (t // 64).astype(np.float32), (t % 64).astype(np.float32)
    angle = np.concatenate([row[:, None] * inv, col[:, None] * inv], axis=-1).astype(np.float32)
    of_pair = np.arange(HD) // 2
    rope = np.stack([np.cos(angle)[:, of_pair].T, np.sin(angle)[:, of_pair].T]).astype(np.float32)
    rotate = np.zeros((P, P), np.float32)
    even = np.arange(0, P, 2)
    rotate[even + 1, even] = -1.0
    rotate[even, even + 1] = 1.0
    count = np.zeros((2, P, LAT), np.float32)
    for g, w in enumerate(WINDOWS):
        n = np.clip(t + w // 2, 0, LAT) - np.clip(t - w // 2, 0, LAT)
        count[g // 2, 64 * (g % 2):64 * (g % 2) + 64] = 1.0 / n
    return {"identity": np.eye(P, dtype=np.float32), "rope": rope, "rotate": rotate, "pool_count": count}


def kernel(**inputs):
    import concourse.bacc as bacc
    from concourse.bass_utils import run_bass_kernel_spmd

    nc = bacc.Bacc("TRN2", target_bir_lowering=False, num_devices=1)
    arrays, a = {}, {}
    for name, x in [(n, inputs[n]) for n in _INS] + list(constants().items()):
        x = np.ascontiguousarray(x)
        arrays[f"in_{name}"] = x
        a[name] = nc.dram_tensor(f"in_{name}", x.shape, mybir.dt.from_np(x.dtype), kind="ExternalInput").ap()
    out = nc.dram_tensor("out_x", (1, LAT, D), F32, kind="ExternalOutput").ap()
    build(nc, a, out)
    r = run_bass_kernel_spmd(nc, [arrays], core_ids=[0])
    return r.results[0]["out_x"]
```
